# Optimizing a Trainium2 kernel written in Bass

```python
import jax, jax.numpy as jnp
from jax import lax
import numpy as np

D_MODEL = 2048
BATCH = 1
SEQ = 256
DEPTH = 2

N_MEM = 256
EPS = 1e-6

SC_WIDTH = 1024
SC_KERNEL = 3

SSD_HEADS = 32
SSD_HEAD_DIM = 64
SSD_WIDTH = SSD_HEADS * SSD_HEAD_DIM
SSD_STATE = 128
SSD_GROUPS = 4
SSD_CONV = 4
SSD_CHUNK = 128
SSD_CONV_DIM = SSD_WIDTH + 2 * SSD_GROUPS * SSD_STATE
DT_MIN = 0.001
DT_MAX = 0.1

MLA_HEADS = 16
MLA_Q_RANK = 768
MLA_KV_RANK = 512
MLA_NOPE = 128
MLA_ROPE = 64
MLA_V = 128
MLA_WIDTH = MLA_HEADS * MLA_V
ROPE_THETA = 10000.0
Q_BLOCK = 128

MEM_HEADS = 4
MEM_HEAD_DIM = 128
MEM_WIDTH = MEM_HEADS * MEM_HEAD_DIM

EVEN_SPLITS = (SC_WIDTH, SC_WIDTH, SC_WIDTH, SC_WIDTH,
               SSD_WIDTH, SSD_CONV_DIM, SSD_HEADS, MEM_WIDTH, MEM_WIDTH)
EVEN_IN = sum(EVEN_SPLITS)
EVEN_OUT = SC_WIDTH + SSD_WIDTH + MEM_WIDTH
ODD_SPLITS = (MLA_Q_RANK, MLA_KV_RANK, MLA_ROPE, MLA_WIDTH, MEM_WIDTH, MEM_WIDTH)
ODD_IN = sum(ODD_SPLITS)
ODD_OUT = MLA_WIDTH + MEM_WIDTH


def _split(t, sizes):
    idx = [int(i) for i in np.cumsum(sizes)[:-1]]
    return jnp.split(t, idx, axis=-1)

def rms_norm(x, w):
    xf = x.astype(jnp.float32)
    y = xf * lax.rsqrt(jnp.mean(xf * xf, axis=-1, keepdims=True) + EPS)
    return (y * w.astype(jnp.float32)).astype(x.dtype)

def causal_depthwise_conv(u, w):
    k_w, c = w.shape
    return lax.conv_general_dilated(
        u, w.reshape(k_w, 1, c).astype(u.dtype), window_strides=(1,),
        padding=[(k_w - 1, 0)], dimension_numbers=("NWC", "WIO", "NWC"),
        feature_group_count=c)

def rope(t, pos):
    half = MLA_ROPE // 2
    inv = ROPE_THETA ** (-jnp.arange(half, dtype=jnp.float32) / half)
    ang = pos.astype(jnp.float32)[..., None] * inv
    cos = jnp.cos(ang)[:, :, None, :]
    sin = jnp.sin(ang)[:, :, None, :]
    t1 = t[..., :half].astype(jnp.float32)
    t2 = t[..., half:].astype(jnp.float32)
    return jnp.concatenate([t1 * cos - t2 * sin, t1 * sin + t2 * cos], axis=-1).astype(t.dtype)

def memory_attention(q, mem_n, w_mk, w_mv):
    b_, l_, _ = q.shape
    qh = q.reshape(b_, l_, MEM_HEADS, MEM_HEAD_DIM)
    k = (mem_n @ w_mk).reshape(b_, -1, MEM_HEADS, MEM_HEAD_DIM)
    v = (mem_n @ w_mv).reshape(b_, -1, MEM_HEADS, MEM_HEAD_DIM)
    s = jnp.einsum('bqhd,bkhd->bhqk', qh, k).astype(jnp.float32) * (MEM_HEAD_DIM ** -0.5)
    p = jax.nn.softmax(s, axis=-1).astype(v.dtype)
    o = jnp.einsum('bhqk,bkhd->bqhd', p, v)
    return o.reshape(b_, l_, MEM_WIDTH)

def ssd_chunked(xs, dt, a, bm, cm):
    b_, l_, h_, p_ = xs.shape
    nc = l_ // SSD_CHUNK
    hpg = h_ // SSD_GROUPS
    xdt = (xs * dt[..., None]).reshape(b_, nc, SSD_CHUNK, SSD_GROUPS, hpg, p_)
    bm = bm.reshape(b_, nc, SSD_CHUNK, SSD_GROUPS, SSD_STATE)
    cm = cm.reshape(b_, nc, SSD_CHUNK, SSD_GROUPS, SSD_STATE)
    a_cum = jnp.cumsum((dt * a).reshape(b_, nc, SSD_CHUNK, SSD_GROUPS, hpg), axis=2)
    seg = a_cum[:, :, :, None] - a_cum[:, :, None, :]
    causal = (jnp.arange(SSD_CHUNK)[:, None] >= jnp.arange(SSD_CHUNK)[None, :])[:, :, None, None]
    decay = jnp.exp(jnp.where(causal, seg, -jnp.inf))
    cb = jnp.einsum('bcqgn,bckgn->bcqkg', cm, bm)
    y_diag = jnp.einsum('bcqkg,bcqkgh,bckghp->bcqghp', cb, decay, xdt)
    decay_to_end = jnp.exp(a_cum[:, :, -1:] - a_cum)
    states = jnp.einsum('bckgn,bckgh,bckghp->bcghpn', bm, decay_to_end, xdt)
    chunk_decay = jnp.exp(a_cum[:, :, -1])

    def step(s, inp):
        st, dec = inp
        return s * dec[..., None, None] + st, s

    init = jnp.zeros((b_, SSD_GROUPS, hpg, p_, SSD_STATE), jnp.float32)
    _, s_enter = lax.scan(step, init, (jnp.moveaxis(states, 1, 0), jnp.moveaxis(chunk_decay, 1, 0)))
    s_enter = jnp.moveaxis(s_enter, 0, 1)
    y_off = jnp.einsum('bcqgn,bcghpn,bcqgh->bcqghp', cm, s_enter, jnp.exp(a_cum))
    return (y_diag + y_off).reshape(b_, l_, h_, p_)

def causal_block_attention(q, k, v):
    b_, l_, h_, dk = q.shape
    nb = l_ // Q_BLOCK
    scale = dk ** -0.5
    qb = jnp.moveaxis(q.reshape(b_, nb, Q_BLOCK, h_, dk), 1, 0)
    k_pos = jnp.arange(l_)

    def one_block(args):
        q_blk, i = args
        s = jnp.einsum('bqhd,bkhd->bhqk', q_blk, k).astype(jnp.float32) * scale
        q_pos = i * Q_BLOCK + jnp.arange(Q_BLOCK)
        s = jnp.where(k_pos[None, :] <= q_pos[:, None], s, -jnp.inf)
        p = jax.nn.softmax(s, axis=-1).astype(v.dtype)
        return jnp.einsum('bhqk,bkhv->bqhv', p, v)

    o = lax.map(one_block, (qb, jnp.arange(nb)))
    return jnp.moveaxis(o, 0, 1).reshape(b_, l_, h_ * v.shape[-1])

def even_layer(x, mem_n, norm_w, w_in, sc_conv_w, ssd_conv_w, ssd_conv_b, ssd_dt_bias,
               ssd_a_log, ssd_d, ssd_norm_w, w_mk, w_mv, w_out):
    b_, l_, _ = x.shape
    h = rms_norm(x, norm_w)
    proj = h @ w_in
    sc_b, sc_c, sc_v, sc_z, ssd_z, ssd_xbc, ssd_dt, mq, mz = _split(proj, EVEN_SPLITS)
    y_a = sc_b * causal_depthwise_conv(sc_c * sc_v, sc_conv_w)
    y_a = y_a * jax.nn.silu(sc_z)
    xbc = jax.nn.silu(causal_depthwise_conv(ssd_xbc, ssd_conv_w) + ssd_conv_b)
    xs, bm, cm = _split(xbc, (SSD_WIDTH, SSD_GROUPS * SSD_STATE, SSD_GROUPS * SSD_STATE))
    xs = xs.reshape(b_, l_, SSD_HEADS, SSD_HEAD_DIM).astype(jnp.float32)
    bm = bm.reshape(b_, l_, SSD_GROUPS, SSD_STATE).astype(jnp.float32)
    cm = cm.reshape(b_, l_, SSD_GROUPS, SSD_STATE).astype(jnp.float32)
    dt = jax.nn.softplus(ssd_dt.astype(jnp.float32) + ssd_dt_bias.astype(jnp.float32))
    a = -jnp.exp(ssd_a_log.astype(jnp.float32))
    y_b = ssd_chunked(xs, dt, a, bm, cm) + xs * ssd_d.astype(jnp.float32)[:, None]
    y_b = y_b.reshape(b_, l_, SSD_WIDTH) * jax.nn.silu(ssd_z.astype(jnp.float32))
    y_b = y_b.reshape(b_, l_, SSD_GROUPS, SSD_WIDTH // SSD_GROUPS)
    y_b = y_b * lax.rsqrt(jnp.mean(y_b * y_b, axis=-1, keepdims=True) + EPS)
    y_b = (y_b.reshape(b_, l_, SSD_WIDTH) * ssd_norm_w.astype(jnp.float32)).astype(x.dtype)
    y_m = memory_attention(mq, mem_n, w_mk, w_mv) * jax.nn.silu(mz)
    return x + jnp.concatenate([y_a, y_b, y_m], axis=-1) @ w_out

def odd_layer(x, mem_n, positions, norm_w, w_in, mla_q_norm_w, mla_kv_norm_w, mla_w_uq,
              mla_w_ukv, w_mk, w_mv, w_out):
    b_, l_, _ = x.shape
    h = rms_norm(x, norm_w)
    proj = h @ w_in
    c_q, c_kv, k_r, z_c, mq, mz = _split(proj, ODD_SPLITS)
    q = (rms_norm(c_q, mla_q_norm_w) @ mla_w_uq).reshape(b_, l_, MLA_HEADS, MLA_NOPE + MLA_ROPE)
    kv = (rms_norm(c_kv, mla_kv_norm_w) @ mla_w_ukv).reshape(b_, l_, MLA_HEADS, MLA_NOPE + MLA_V)
    q_nope, q_rope = q[..., :MLA_NOPE], rope(q[..., MLA_NOPE:], positions)
    k_nope, v = kv[..., :MLA_NOPE], kv[..., MLA_NOPE:]
    k_rope = jnp.broadcast_to(rope(k_r[:, :, None, :], positions), (b_, l_, MLA_HEADS, MLA_ROPE))
    q_full = jnp.concatenate([q_nope, q_rope], axis=-1)
    k_full = jnp.concatenate([k_nope, k_rope], axis=-1)
    y_c = causal_block_attention(q_full, k_full, v) * jax.nn.silu(z_c)
    y_m = memory_attention(mq, mem_n, w_mk, w_mv) * jax.nn.silu(mz)
    return x + jnp.concatenate([y_c, y_m], axis=-1) @ w_out

def first_inputs(seed: int = 0) -> dict:
    key = jax.random.key(seed)
    ks = jax.random.split(key, 32)
    f32 = jnp.float32

    def dense(k, fan_in, fan_out):
        return jax.random.normal(k, (fan_in, fan_out), f32) * fan_in ** -0.5

    def gain(k, n):
        return 1.0 + 0.05 * jax.random.normal(k, (n,), f32)

    x = jax.random.normal(ks[0], (BATCH, SEQ, D_MODEL), f32)
    mem = jax.random.normal(ks[1], (BATCH, N_MEM, D_MODEL), f32)
    offsets = jax.random.randint(ks[2], (BATCH, 1), 0, 4096, dtype=jnp.int32)
    positions = offsets + jnp.arange(SEQ, dtype=jnp.int32)[None, :]
    dt0 = jnp.exp(jax.random.uniform(ks[3], (SSD_HEADS,), f32) * (np.log(DT_MAX) - np.log(DT_MIN)) + np.log(DT_MIN))
    return {
        "x": x,
        "mem": mem,
        "positions": positions,
        "mem_norm_w": gain(ks[4], D_MODEL),
        "norm0_w": gain(ks[5], D_MODEL),
        "w_in0": dense(ks[6], D_MODEL, EVEN_IN),
        "sc_conv_w": jax.random.normal(ks[7], (SC_KERNEL, SC_WIDTH), f32) * SC_KERNEL ** -0.5,
        "ssd_conv_w": jax.random.normal(ks[8], (SSD_CONV, SSD_CONV_DIM), f32) * SSD_CONV ** -0.5,
        "ssd_conv_b": 0.01 * jax.random.normal(ks[9], (SSD_CONV_DIM,), f32),
        "ssd_dt_bias": dt0 + jnp.log(-jnp.expm1(-dt0)),
        "ssd_a_log": jnp.log(jax.random.uniform(ks[10], (SSD_HEADS,), f32, 1.0, 16.0)),
        "ssd_d": 1.0 + 0.1 * jax.random.normal(ks[11], (SSD_HEADS,), f32),
        "ssd_norm_w": gain(ks[12], SSD_WIDTH),
        "mem_k0": dense(ks[13], D_MODEL, MEM_WIDTH),
        "mem_v0": dense(ks[14], D_MODEL, MEM_WIDTH),
        "w_out0": dense(ks[15], EVEN_OUT, D_MODEL),
        "norm1_w": gain(ks[16], D_MODEL),
        "w_in1": dense(ks[17], D_MODEL, ODD_IN),
        "mla_q_norm_w": gain(ks[18], MLA_Q_RANK),
        "mla_kv_norm_w": gain(ks[19], MLA_KV_RANK),
        "mla_w_uq": dense(ks[20], MLA_Q_RANK, MLA_HEADS * (MLA_NOPE + MLA_ROPE)),
        "mla_w_ukv": dense(ks[21], MLA_KV_RANK, MLA_HEADS * (MLA_NOPE + MLA_V)),
        "mem_k1": dense(ks[22], D_MODEL, MEM_WIDTH),
        "mem_v1": dense(ks[23], D_MODEL, MEM_WIDTH),
        "w_out1": dense(ks[24], ODD_OUT, D_MODEL),
        "final_norm_w": gain(ks[25], D_MODEL),
    }

def first_block(x, mem, positions, mem_norm_w, norm0_w, w_in0, sc_conv_w, ssd_conv_w, ssd_conv_b,
              ssd_dt_bias, ssd_a_log, ssd_d, ssd_norm_w, mem_k0, mem_v0, w_out0, norm1_w, w_in1,
              mla_q_norm_w, mla_kv_norm_w, mla_w_uq, mla_w_ukv, mem_k1, mem_v1, w_out1, final_norm_w):
    mem_n = rms_norm(mem, mem_norm_w)
    even_params = (norm0_w, w_in0, sc_conv_w, ssd_conv_w, ssd_conv_b, ssd_dt_bias, ssd_a_log,
                   ssd_d, ssd_norm_w, mem_k0, mem_v0, w_out0)
    odd_params = (norm1_w, w_in1, mla_q_norm_w, mla_kv_norm_w, mla_w_uq, mla_w_ukv,
                  mem_k1, mem_v1, w_out1)
    layer_params = [even_params, odd_params]
    for layer in range(DEPTH):
        if layer % 2 == 0:
            x = even_layer(x, mem_n, *layer_params[layer])
        else:
            x = odd_layer(x, mem_n, positions, *layer_params[layer])
    return rms_norm(x, final_norm_w)


DEPTH_2 = 1

CHUNK = 64
N_MIXERS = 4
D_FF = 4 * D_MODEL
NORM_EPS = 1e-6

RET_HEADS = 8
RET_DK = D_MODEL // RET_HEADS
RET_DV = 2 * D_MODEL // RET_HEADS
RET_IN = 2 * RET_HEADS * RET_DK + 2 * RET_HEADS * RET_DV
ROPE_BASE = 10000.0

GDN_HEADS = 16
GDN_DK = D_MODEL // GDN_HEADS
GDN_DV = D_MODEL // GDN_HEADS
GDN_QKV = GDN_HEADS * (2 * GDN_DK + GDN_DV)
GDN_IN = GDN_QKV + GDN_HEADS * GDN_DV + 2 * GDN_HEADS
CONV_WIDTH = 4

GLA_HEADS = 4
GLA_DK = D_MODEL // 2 // GLA_HEADS
GLA_DV = D_MODEL // GLA_HEADS
GLA_GATE_RANK = 16
GLA_TAU = 16.0
GLA_IN = 2 * GLA_HEADS * GLA_DK + 2 * GLA_HEADS * GLA_DV + GLA_GATE_RANK

LRU_WIDTH = D_MODEL
LRU_BLOCKS = 16
LRU_BLOCK = LRU_WIDTH // LRU_BLOCKS
LRU_C = 8.0


F32 = jnp.float32

def _layers_of(m):
    return (DEPTH_2 - m + N_MIXERS - 1) // N_MIXERS

def rmsnorm(x, g):
    xf = x.astype(F32)
    y = xf * lax.rsqrt(jnp.mean(xf * xf, axis=-1, keepdims=True) + NORM_EPS)
    return (y * g.astype(F32)).astype(x.dtype)

def head_norm(o, gain, center):
    of = o.astype(F32)
    if center:
        of = of - jnp.mean(of, axis=-1, keepdims=True)
    of = of * lax.rsqrt(jnp.mean(of * of, axis=-1, keepdims=True) + NORM_EPS)
    of = of * gain.astype(F32)
    return of.reshape(o.shape[0], o.shape[1], -1)

def l2norm(x):
    return x * lax.rsqrt(jnp.sum(x * x, axis=-1, keepdims=True) + NORM_EPS)

def causal_depthwise_conv_2(x, w):
    width, s = w.shape[0], x.shape[1]
    xp = jnp.pad(x, ((0, 0), (width - 1, 0), (0, 0)))
    out = xp[:, 0:s] * w[0]
    for tap in range(1, width):
        out = out + xp[:, tap:tap + s] * w[tap]
    return out

def to_chunks(x):
    b, s, h, d = x.shape
    return x.reshape(b, s // CHUNK, CHUNK, h, d).transpose(0, 3, 1, 2, 4)

def from_chunks(x):
    b, h, n, c, d = x.shape
    return x.transpose(0, 2, 3, 1, 4).reshape(b, n * c, h, d)

def scalar_chunks(x):
    b, s, h = x.shape
    return x.reshape(b, s // CHUNK, CHUNK, h).transpose(0, 3, 1, 2)

def rotary(x):
    s, d = x.shape[1], x.shape[-1]
    inv = ROPE_BASE ** (-jnp.arange(0, d, 2, dtype=F32) / d)
    ang = jnp.arange(s, dtype=F32)[:, None] * inv[None, :]
    cos, sin = jnp.cos(ang)[:, None, :], jnp.sin(ang)[:, None, :]
    x1, x2 = x[..., : d // 2], x[..., d // 2:]
    return jnp.concatenate([x1 * cos - x2 * sin, x1 * sin + x2 * cos], axis=-1)

def retention_mixer(h, w_in, gn_gain, w_out):
    b, s, _ = h.shape
    H, DK, DV = RET_HEADS, RET_DK, RET_DV
    q, k, v, g = jnp.split(h @ w_in, [H * DK, 2 * H * DK, 2 * H * DK + H * DV], axis=-1)
    q = rotary(q.astype(F32).reshape(b, s, H, DK))
    k = rotary(k.astype(F32).reshape(b, s, H, DK)) * DK ** -0.5
    v = v.astype(F32).reshape(b, s, H, DV)
    qc, kc, vc = to_chunks(q), to_chunks(k), to_chunks(v)
    log_gamma = jnp.log1p(-jnp.exp2(-5.0 - jnp.arange(H, dtype=F32)))
    pos = jnp.arange(CHUNK, dtype=F32)
    dist = jnp.abs(pos[:, None] - pos[None, :])
    decay_intra = jnp.exp(log_gamma[:, None, None] * dist)
    scores = jnp.einsum('bhncd,bhnmd->bhncm', qc, kc) * decay_intra[None, :, None]
    o_intra = jnp.einsum('bhncm,bhnmv->bhncv', scores, vc)
    q_decay = jnp.exp(log_gamma[:, None] * (pos + 1.0))[None, :, :, None]
    k_decay = jnp.exp(log_gamma[:, None] * (CHUNK - 1.0 - pos))[None, :, :, None]
    chunk_decay = jnp.exp(log_gamma * CHUNK)[None, :, None, None]

    def step(state, xs):
        q_n, k_n, v_n = xs
        o = jnp.einsum('bhcd,bhdv->bhcv', q_n * q_decay, state)
        state = state * chunk_decay + jnp.einsum('bhcd,bhcv->bhdv', k_n * k_decay, v_n)
        return state, o

    xs = (jnp.moveaxis(qc, 2, 0), jnp.moveaxis(kc, 2, 0), jnp.moveaxis(vc, 2, 0))
    _, o_inter = lax.scan(step, jnp.zeros((b, H, DK, DV), F32), xs)
    o = from_chunks(o_intra + jnp.moveaxis(o_inter, 0, 2))
    o = head_norm(o, gn_gain, center=True) * jax.nn.silu(g.astype(F32))
    return o.astype(h.dtype) @ w_out

def gated_deltanet_mixer(h, w_in, conv_w, a_log, dt_bias, norm_gain, w_out):
    b, s, _ = h.shape
    H, DK, DV = GDN_HEADS, GDN_DK, GDN_DV
    qkv, z, beta_logit, a_logit = jnp.split(
        h @ w_in, [GDN_QKV, GDN_QKV + H * DV, GDN_QKV + H * DV + H], axis=-1)
    qkv = jax.nn.silu(causal_depthwise_conv_2(qkv, conv_w)).astype(F32)
    q, k, v = jnp.split(qkv, [H * DK, 2 * H * DK], axis=-1)
    q = l2norm(q.reshape(b, s, H, DK)) * DK ** -0.5
    k = l2norm(k.reshape(b, s, H, DK))
    v = v.reshape(b, s, H, DV)
    beta = jax.nn.sigmoid(beta_logit.astype(F32))
    log_alpha = -jnp.exp(a_log.astype(F32)) * jax.nn.softplus(a_logit.astype(F32) + dt_bias.astype(F32))
    qc, kc, vc = to_chunks(q), to_chunks(k), to_chunks(v)
    beta_c = scalar_chunks(beta)
    cum = jnp.cumsum(scalar_chunks(log_alpha), axis=-1)
    idx = jnp.arange(CHUNK)
    strict = idx[:, None] > idx[None, :]
    rel = jnp.where(strict, jnp.exp(jnp.where(strict, cum[..., :, None] - cum[..., None, :], 0.0)), 0.0)
    a_mat = beta_c[..., :, None] * rel * jnp.einsum('bhncd,bhnmd->bhncm', kc, kc)
    l_mat = a_mat + jnp.eye(CHUNK, dtype=F32)
    rhs = jnp.concatenate([beta_c[..., None] * vc, (beta_c * jnp.exp(cum))[..., None] * kc], axis=-1)
    sol = lax.linalg.triangular_solve(l_mat, rhs, left_side=True, lower=True, unit_diagonal=True)
    u, w = sol[..., :DV], sol[..., DV:]
    k_end = kc * jnp.exp(cum[..., -1:] - cum)[..., None]
    trans = (jnp.exp(cum[..., -1])[..., None, None] * jnp.eye(DK, dtype=F32)
             - jnp.einsum('bhnck,bhncj->bhnkj', k_end, w))
    inject = jnp.einsum('bhnck,bhncv->bhnkv', k_end, u)

    def step(state, xs):
        t, g, q_n = xs
        state = jnp.einsum('bhkj,bhjv->bhkv', t, state) + g
        return state, jnp.einsum('bhck,bhkv->bhcv', q_n, state)

    xs = (jnp.moveaxis(trans, 2, 0), jnp.moveaxis(inject, 2, 0), jnp.moveaxis(qc, 2, 0))
    _, o = lax.scan(step, jnp.zeros((b, H, DK, DV), F32), xs)
    o = from_chunks(jnp.moveaxis(o, 0, 2))
    o = head_norm(o, norm_gain, center=False) * jax.nn.silu(z.astype(F32))
    return o.astype(h.dtype) @ w_out

def gla_mixer(h, w_in, w_gate_up, gate_bias, norm_gain, w_out):
    b, s, _ = h.shape
    H, DK, DV = GLA_HEADS, GLA_DK, GLA_DV
    QK, V = H * DK, H * DV
    q, k, v, r, gate_low = jnp.split(h @ w_in, [QK, 2 * QK, 2 * QK + V, 2 * QK + 2 * V], axis=-1)
    gate_logit = (gate_low @ w_gate_up + gate_bias).astype(F32)
    log_alpha = jax.nn.log_sigmoid(gate_logit) / GLA_TAU
    qc = to_chunks(q.astype(F32).reshape(b, s, H, DK)) * DK ** -0.5
    kc = to_chunks(k.astype(F32).reshape(b, s, H, DK))
    vc = to_chunks(v.astype(F32).reshape(b, s, H, DV))
    cum = jnp.cumsum(to_chunks(log_alpha.reshape(b, s, H, DK)), axis=-2)
    ref = cum[..., CHUNK // 2 - 1:CHUNK // 2, :]
    fwd, bwd = jnp.exp(cum - ref), jnp.exp(ref - cum)
    s_lo = jnp.einsum('bhnck,bhnmk->bhncm', qc * fwd, kc * bwd)
    s_up = jnp.einsum('bhnck,bhnmk->bhncm', qc * bwd, kc * fwd)
    idx = jnp.arange(CHUNK)
    scores = jnp.where(idx[:, None] >= idx[None, :], s_lo, s_up)
    o_intra = jnp.einsum('bhncm,bhnmv->bhncv', scores, vc)
    q_in = qc * jnp.exp(cum)
    k_end = kc * jnp.exp(cum[..., -1:, :] - cum)
    chunk_dec = jnp.exp(cum[..., -1, :])

    def step(state, xs):
        q_n, k_n, v_n, dec = xs
        o = jnp.einsum('bhck,bhkv->bhcv', q_n, state)
        state = state * dec[..., None] + jnp.einsum('bhck,bhcv->bhkv', k_n, v_n)
        return state, o

    xs = tuple(jnp.moveaxis(t, 2, 0) for t in (q_in, k_end, vc, chunk_dec))
    _, o_inter = lax.scan(step, jnp.zeros((b, H, DK, DV), F32), xs)
    o = from_chunks(o_intra + jnp.moveaxis(o_inter, 0, 2))
    o = head_norm(o, norm_gain, center=False) * jax.nn.silu(r.astype(F32))
    return o.astype(h.dtype) @ w_out

def rglru_mixer(h, w_in, conv_w, conv_b, w_rgate, b_rgate, w_igate, b_igate, lam, w_out):
    b, s, _ = h.shape
    xb, yb = jnp.split(h @ w_in, [LRU_WIDTH], axis=-1)
    yb = jax.nn.gelu(yb.astype(F32))
    xb = (causal_depthwise_conv_2(xb, conv_w) + conv_b).astype(F32)
    xblk = xb.reshape(b, s, LRU_BLOCKS, LRU_BLOCK)
    r = jax.nn.sigmoid(jnp.einsum('bsnd,nde->bsne', xblk, w_rgate.astype(F32)) + b_rgate.astype(F32))
    i = jax.nn.sigmoid(jnp.einsum('bsnd,nde->bsne', xblk, w_igate.astype(F32)) + b_igate.astype(F32))
    r, i = r.reshape(b, s, LRU_WIDTH), i.reshape(b, s, LRU_WIDTH)
    log_a = -LRU_C * jax.nn.softplus(-lam.astype(F32)) * r
    a = jnp.exp(log_a)
    u = jnp.sqrt(-jnp.expm1(2.0 * log_a)) * (i * xb)

    def combine(left, right):
        a_l, b_l = left
        a_r, b_r = right
        return a_l * a_r, a_r * b_l + b_r

    _, hs = lax.associative_scan(combine, (a, u), axis=1)
    return (hs * yb).astype(h.dtype) @ w_out

def squared_relu_mlp(h, w_up, w_down):
    return jnp.square(jax.nn.relu(h @ w_up)) @ w_down

def second_inputs(seed: int = 0) -> dict:
    key = jax.random.key(seed)
    ks = iter(jax.random.split(key, 40))

    def nrm(shape, scale):
        return scale * jax.random.normal(next(ks), shape, F32)

    def uni(shape, lo, hi):
        return jax.random.uniform(next(ks), shape, F32, lo, hi)

    n_ret, n_gdn, n_gla, n_lru = (_layers_of(m) for m in range(N_MIXERS))
    d_in = D_MODEL ** -0.5
    dt = jnp.exp(uni((n_gdn, GDN_HEADS), float(np.log(1e-3)), float(np.log(1e-1))))
    a0 = uni((n_lru, LRU_WIDTH), 0.9, 0.999)
    s0 = a0 ** (1.0 / LRU_C)
    return {
        "x": nrm((BATCH, SEQ, D_MODEL), 1.0),
        "norm1": 1.0 + nrm((DEPTH_2, D_MODEL), 0.02),
        "norm2": 1.0 + nrm((DEPTH_2, D_MODEL), 0.02),
        "final_norm": 1.0 + nrm((D_MODEL,), 0.02),
        "ret_w_in": nrm((n_ret, D_MODEL, RET_IN), d_in),
        "ret_gn_gain": 1.0 + nrm((n_ret, RET_HEADS, RET_DV), 0.02),
        "ret_w_out": nrm((n_ret, RET_HEADS * RET_DV, D_MODEL), (RET_HEADS * RET_DV) ** -0.5),
        "gdn_w_in": nrm((n_gdn, D_MODEL, GDN_IN), d_in),
        "gdn_conv_w": nrm((n_gdn, CONV_WIDTH, GDN_QKV), CONV_WIDTH ** -0.5),
        "gdn_a_log": jnp.log(uni((n_gdn, GDN_HEADS), 1.0, 16.0)),
        "gdn_dt_bias": dt + jnp.log(-jnp.expm1(-dt)),
        "gdn_norm_gain": 1.0 + nrm((n_gdn, GDN_DV), 0.02),
        "gdn_w_out": nrm((n_gdn, GDN_HEADS * GDN_DV, D_MODEL), (GDN_HEADS * GDN_DV) ** -0.5),
        "gla_w_in": nrm((n_gla, D_MODEL, GLA_IN), d_in),
        "gla_w_gate_up": nrm((n_gla, GLA_GATE_RANK, GLA_HEADS * GLA_DK), GLA_GATE_RANK ** -0.5),
        "gla_gate_bias": nrm((n_gla, GLA_HEADS * GLA_DK), 0.1),
        "gla_norm_gain": 1.0 + nrm((n_gla, GLA_HEADS, GLA_DV), 0.02),
        "gla_w_out": nrm((n_gla, GLA_HEADS * GLA_DV, D_MODEL), (GLA_HEADS * GLA_DV) ** -0.5),
        "lru_w_in": nrm((n_lru, D_MODEL, 2 * LRU_WIDTH), d_in),
        "lru_conv_w": nrm((n_lru, CONV_WIDTH, LRU_WIDTH), CONV_WIDTH ** -0.5),
        "lru_conv_b": nrm((n_lru, LRU_WIDTH), 0.02),
        "lru_w_rgate": nrm((n_lru, LRU_BLOCKS, LRU_BLOCK, LRU_BLOCK), LRU_BLOCK ** -0.5),
        "lru_b_rgate": nrm((n_lru, LRU_BLOCKS, LRU_BLOCK), 0.02),
        "lru_w_igate": nrm((n_lru, LRU_BLOCKS, LRU_BLOCK, LRU_BLOCK), LRU_BLOCK ** -0.5),
        "lru_b_igate": nrm((n_lru, LRU_BLOCKS, LRU_BLOCK), 0.02),
        "lru_lambda": jnp.log(s0) - jnp.log1p(-s0),
        "lru_w_out": nrm((n_lru, LRU_WIDTH, D_MODEL), LRU_WIDTH ** -0.5),
        "mlp_w_up": nrm((DEPTH_2, D_MODEL, D_FF), d_in),
        "mlp_w_down": nrm((DEPTH_2, D_FF, D_MODEL), D_FF ** -0.5),
    }

def second_block(x, norm1, norm2, final_norm,
              ret_w_in, ret_gn_gain, ret_w_out,
              gdn_w_in, gdn_conv_w, gdn_a_log, gdn_dt_bias, gdn_norm_gain, gdn_w_out,
              gla_w_in, gla_w_gate_up, gla_gate_bias, gla_norm_gain, gla_w_out,
              lru_w_in, lru_conv_w, lru_conv_b, lru_w_rgate, lru_b_rgate, lru_w_igate,
              lru_b_igate, lru_lambda, lru_w_out,
              mlp_w_up, mlp_w_down):
    for layer in range(DEPTH_2):
        m, j = layer % N_MIXERS, layer // N_MIXERS
        hn = rmsnorm(x, norm1[layer])
        if m == 0:
            y = retention_mixer(hn, ret_w_in[j], ret_gn_gain[j], ret_w_out[j])
        elif m == 1:
            y = gated_deltanet_mixer(hn, gdn_w_in[j], gdn_conv_w[j], gdn_a_log[j], gdn_dt_bias[j],
                                     gdn_norm_gain[j], gdn_w_out[j])
        elif m == 2:
            y = gla_mixer(hn, gla_w_in[j], gla_w_gate_up[j], gla_gate_bias[j], gla_norm_gain[j], gla_w_out[j])
        else:
            y = rglru_mixer(hn, lru_w_in[j], lru_conv_w[j], lru_conv_b[j], lru_w_rgate[j], lru_b_rgate[j],
                            lru_w_igate[j], lru_b_igate[j], lru_lambda[j], lru_w_out[j])
        x = x + y
        x = x + squared_relu_mlp(rmsnorm(x, norm2[layer]), mlp_w_up[layer], mlp_w_down[layer])
    return rmsnorm(x, final_norm)


def setup_inputs(seed=0):
    out = dict(first_inputs(seed))
    for name, value in second_inputs(seed + 1).items():
        if name != "x":
            out[name + "_2"] = value
    return out


def reference(
    x, mem, positions, mem_norm_w, norm0_w, w_in0, sc_conv_w, ssd_conv_w, ssd_conv_b,
    ssd_dt_bias, ssd_a_log, ssd_d, ssd_norm_w, mem_k0, mem_v0, w_out0, norm1_w, w_in1,
    mla_q_norm_w, mla_kv_norm_w, mla_w_uq, mla_w_ukv, mem_k1, mem_v1, w_out1, final_norm_w,
    norm1_2, norm2_2, final_norm_2, ret_w_in_2, ret_gn_gain_2, ret_w_out_2, gdn_w_in_2,
    gdn_conv_w_2, gdn_a_log_2, gdn_dt_bias_2, gdn_norm_gain_2, gdn_w_out_2, gla_w_in_2,
    gla_w_gate_up_2, gla_gate_bias_2, gla_norm_gain_2, gla_w_out_2, lru_w_in_2, lru_conv_w_2,
    lru_conv_b_2, lru_w_rgate_2, lru_b_rgate_2, lru_w_igate_2, lru_b_igate_2, lru_lambda_2,
    lru_w_out_2, mlp_w_up_2, mlp_w_down_2,
):
    x = first_block(
        x, mem, positions, mem_norm_w, norm0_w, w_in0, sc_conv_w, ssd_conv_w, ssd_conv_b,
        ssd_dt_bias, ssd_a_log, ssd_d, ssd_norm_w, mem_k0, mem_v0, w_out0, norm1_w, w_in1,
        mla_q_norm_w, mla_kv_norm_w, mla_w_uq, mla_w_ukv, mem_k1, mem_v1, w_out1, final_norm_w,
    )
    return second_block(
        x, norm1_2, norm2_2, final_norm_2, ret_w_in_2, ret_gn_gain_2, ret_w_out_2, gdn_w_in_2,
        gdn_conv_w_2, gdn_a_log_2, gdn_dt_bias_2, gdn_norm_gain_2, gdn_w_out_2, gla_w_in_2,
        gla_w_gate_up_2, gla_gate_bias_2, gla_norm_gain_2, gla_w_out_2, lru_w_in_2,
        lru_conv_w_2, lru_conv_b_2, lru_w_rgate_2, lru_b_rgate_2, lru_w_igate_2, lru_b_igate_2,
        lru_lambda_2, lru_w_out_2, mlp_w_up_2, mlp_w_down_2,
    )


_drawn_inputs = setup_inputs


def setup_inputs(seed=0):
    import zlib

    import numpy as np

    out = dict(_drawn_inputs(seed))
    spreads = {}
    factors = {'mem_norm_w': 8.0,
     'ssd_conv_b': 4.463,
     'norm1_w': 4.374,
     'mla_q_norm_w': 8.0,
     'mla_kv_norm_w': 6.811,
     'norm2_2': 3.304,
     'final_norm_2': 2.883,
     'ret_gn_gain_2': 5.112}
    for name, (base, spread) in spreads.items():
        noise = np.random.default_rng([zlib.crc32(name.encode()), seed]).standard_normal(out[name].shape)
        drawn = base * np.exp(spread * noise) if base else spread * noise
        out[name] = __import__('jax').numpy.asarray(drawn.astype(out[name].dtype))
    for name, factor in factors.items():
        out[name] = (out[name] * factor).astype(out[name].dtype)
    return out
```

```python
from contextlib import ExitStack

import numpy as np
import concourse.bass as bass
from concourse import mybir

P = 128
T = 256
D = 2048
KT = D // P
EPS = 1e-6
F32 = mybir.dt.float32
F32R = mybir.dt.float32r
I32 = mybir.dt.int32
ALU = mybir.AluOpType
ACT = mybir.ActivationFunctionType
AX = mybir.AxisListType

GROUPS = 4
SSD_HEADS = 32
MEM_SCALE = 128 ** -0.5
MLA_SCALE = 192 ** -0.5
RET_HEADS = 8
FF_BLOCKS = 4

PHASES = {
    "mem": ([16] * 8, 2),
    "gate": ([16] * 4, 8),
    "gate_out": ([16] * 4, 2),
    "ssd": ([16] * 12, 4),
    "out0": ([10] * 8, 4),
    "latent": ([16] * 4, 2),
    "latent_tail": ([16] * 3, 1),
    "memq": ([16] * 4, 2),
    "mla": ([6, 6, 6, 8, 4, 4, 16, 16], 8),
    "out1": ([10] * 8, 4),
    "ret_a": ([16] * 12, 4),
    "ret_out_a": ([16] * 4, 4),
    "ret_b": ([16] * 12, 4),
    "ret_out_b": ([16] * 4, 4),
}
for _b in range(FF_BLOCKS):
    PHASES[f"up{_b}"] = ([16] * 4, 4)
    PHASES[f"down{_b}"] = ([16] * 4, 4)
ORDER = list(PHASES)

VEC = {}
_at = 0
for _name, _n in (("mem_norm", 16), ("norm0", 16), ("norm1", 16), ("final", 16), ("norm1_2", 16), ("norm2_2", 16),
                  ("final_2", 16), ("q_norm", 6), ("kv_norm", 4), ("gn_gain", 32), ("gate_conv", 24),
                  ("ssd_conv", GROUPS * 30), ("ssd_d", 16), ("ssd_norm", 16), ("dt_bias", 32), ("a_log", 32),
                  ("inv_freq", 1), ("sin_sign", 1)):
    VEC[_name] = (_at, _at + _n)
    _at += _n
NVEC = _at

CONST = {}
_at = 0
for _name, _n in (("ident", 128), ("ones", 128), ("upto", 128), ("after", 128)):
    CONST[_name] = (_at, _at + _n)
    _at += _n
NCONST = _at


class Count:

    def __init__(self, first, per=0, i=0):
        self.first, self.per, self.i = first, per, i

    def __call__(self, j, lead=0):
        return self.i * self.per + (self.first + j + lead)

    def slot(self, j, n):
        assert self.per % n == 0
        return (self.first + j) % n

    def filled(self, j):
        assert self.per % 4 == 0
        return self.i * (self.per * 4) + 16 * ((self.first + j) // 4 + 1)


def build(nc, streams, w_dt, vecs, consts, mla_mask, ret_tab, ret_decay, pos, x, mem, out, debug=None, stop=None):
    ctx = ExitStack()
    with ctx:
        def sb(name, shape, dt=F32):
            return ctx.enter_context(nc.sbuf_tensor(name, shape, dt))

        def sem(name):
            return ctx.enter_context(nc.semaphore(name))

        NB = 2
        raw = sb("raw", [P, 4, 16, 128])
        w_hi = sb("w_hi", [P, 2, 16, 128], F32R)
        w_lo = sb("w_lo", [P, 2, 16, 128], F32R)
        hs = sb("hs", [P, 16, 2, T], F32R)
        ys = sb("ys", [P, 20, 2, T], F32R)
        lat = sb("lat", [P, 10, 2, T], F32R)
        xT = sb("xT", [P, 16, T])
        kv = sb("kv", [P, 2048])
        half = sb("half", [P, NB, T])
        wdt = sb("wdt", [P, 16, 32])
        small = sb("small", [P, 224])
        vec = sb("vec", [P, NVEC])
        con = sb("con", [P, NCONST])
        GEN = 4608
        gen = sb("gen", [P, GEN])
        pj = ctx.enter_context(nc.psum_tensor("pj", [P, 2, 512], F32))
        mx = ctx.enter_context(nc.psum_tensor("mx", [P, 6, 512], F32))
        kv_spill = nc.dram_tensor("kv_spill", [2, P, 2048], F32).ap()
        x_spill = nc.dram_tensor("x_spill", [P, 16 * T], F32).ap()

        ident, ones, upto, after = (con[:, CONST[n][0]:CONST[n][1]] for n in ("ident", "ones", "upto", "after"))
        keys = kv[:, 0:1024].rearrange("p (n t) -> p n t", n=4)
        values = kv[:, 1024:2048].rearrange("p (m c) -> p m c", m=2)
        xflat = xT[:].rearrange("p a b -> p (a b)")

        def V(name, k=0):
            a = VEC[name][0] + k
            return vec[:, a:a + 1]

        def carve(start, sizes):
            views, at = [], start
            for n in sizes:
                if at < GEN and at + n > GEN:
                    at = GEN
                views.append(gen[:, at:at + n] if at + n <= GEN else xflat[:, at - GEN:at - GEN + n])
                at += n
            assert at <= GEN + 16 * T, at
            return views

        outs_per = {"gate_out": 8, "out0": 4, "out1": 4, "ret_out_a": 4, "ret_out_b": 4, "mla": 10}
        first_panel, first_out = {}, {}
        p0 = o0 = 0
        for name in ORDER:
            first_panel[name], first_out[name] = p0, o0
            sizes, n = PHASES[name]
            p0 += len(sizes) * n
            o0 += outs_per.get(name, len(sizes)) * n
        total_panels = p0

        def panels(name, i=0):
            return Count(first_panel[name], len(PHASES[name][0]) if PHASES[name][1] > 1 else 0, i)

        def outputs(name, i=0):
            return Count(first_out[name], outs_per.get(name, len(PHASES[name][0])) if PHASES[name][1] > 1 else 0, i)

        def next_size(name, j):
            sizes, _ = PHASES[name]
            if j + 1 < len(sizes):
                return sizes[j + 1]
            k = ORDER.index(name) + 1
            return max(sizes[0], PHASES[ORDER[k]][0][0]) if k < len(ORDER) else sizes[0]

        loaded = [sem(f"weights_loaded{s}") for s in range(4)]
        hi_ready = sem("weights_hi_ready")
        split_ready = sem("weights_split_ready")
        panel_started = sem("panel_started")
        output_ready = sem("output_ready")
        half_copied = sem("half_copied")
        evacuated = sem("evacuated")

        names = """mem_rows x_rows tables mem_squares mem_var mem_rsqrt mem_scaled x_squares x_var x_rsqrt x_scaled
            transposed part_hi part_taken v_rows v_rows_taken kv_spilled kv_free kv_loaded
            gate_tanh y_gate dt_logits dt_exp_in dt_exp dt_ready dte_logits dte_ready
            x_tile x_square x_spilled x_loaded acc_ready stat_ready var_ready rsqrt_ready h_f32 h_hi h_ready
            conv_done conv_tanh bc_ready cb_ready cb_taken brow_ready seg_rhs seg_ready decay_ready mix_ready ydiag_ready
            xs_ready xs_rows xdt_ready state_ready state_copied yoff_ready eq_lhs eq_logits eq_ready
            z_tanh mz_tanh ssd_gated ssd_squares y_ssd
            mem_scores mem_shift mem_probs mem_scaled_probs mem_pt mem_pt_copied mem_values mem_pv y_mem
            pos_loaded angle_ready sin_ready mask_loaded latent_ready latent_squares lat_ready krope_ready
            qk_ready mla_vt mla_vrow mla_scores mla_shift mla_probs mla_probs_scaled mla_pt mla_pt_copied mla_pv mla_tanh y_mla
            ret_tab_loaded decay_loaded decay_used ret_qk ret_vt ret_vrow ret_scores ret_mixed ret_pv ret_o
            ret_mean ret_centred ret_squares ret_tanh y_ret y_up fin_ready fin_rows fin_taken out_done""".split()
        S = {n: sem(n) for n in names}

        block = ctx.enter_context(nc.Block())
        live = ORDER if stop is None else ORDER[:ORDER.index(stop) + 1]
        last_tile_of = {n: live.index(n) for n in live}

        def run(engine, name, body, first=0):
            n = PHASES[name][1]
            if n - first == 1:
                body(first)
            else:
                with engine.Fori(first, n) as i:
                    body(i)

        MEMH = {"ssd": 0, "memq": 4}
        NORM = {"ssd": 0, "b_latent": 4, "kv": 5, "q": 6, "b_final": 7, "b_ret": 8, "ret_a": 9, "ret_b": 13, "b_mlp": 17,
                "b_out": 18}
        RES = ["gate_out", "out0", "out1", "b_ret", "ret_out_a", "ret_out_b"] + [f"down{b}" for b in range(FF_BLOCKS)]
        RES = {n: 16 * k for k, n in enumerate(RES)}

        rows = gen[:, 0:4096].rearrange("p (r c) -> p r c", r=2)
        mem_rows = xflat.rearrange("p (r c) -> p r c", r=2)
        vt = [gen[:, 4096:4352], gen[:, 4352:4608]]
        z_g, c_g, v_g, b_g, th_g, u_g, a_g, e_g, s_g = carve(0, [256] * 5 + [260] + [256] * 3)
        res = carve(0, [256, 256])
        sq = carve(512, [256, 256])
        acc, = carve(1024, [256])
        hf = carve(1280, [1024, 1024])
        nv, ny, nt, rstd = carve(3328, [256] * 4)
        ss, var4, rs4, tmp4 = small[:, 0:4], small[:, 4:8], small[:, 8:12], small[:, 12:16]
        mstat = small[:, 16:24]
        pstat = small[:, 24:48]
        dt = small[:, 48:112].rearrange("p (c h) -> p c h", c=2)
        da = small[:, 112:176].rearrange("p (c h) -> p c h", c=2)
        dte = small[:, 176:208]
        dtw = [w.rearrange("p (c h) -> p c h", c=2) for w in carve(2600, [64] * 8)]
        ea, = carve(3200, [32])

        (cp0, cp1, cv0, cv1, th0, th1, bT, cT, r0, r1, cbm, brow, xs_) = carve(
            0, [260, 260, 256, 256, 256, 256, 256, 256, 512, 512, 256, 128, 1024])
        em0, em1, xdt0, xdt1, xdte, state, sz_ = carve(GEN, [512] * 6 + [1024])
        cp, cv, th, rr, em, xdt = (cp0, cp1), (cv0, cv1), (th0, th1), (r0, r1), (em0, em1), (xdt0, xdt1)
        xs = xs_.rearrange("p (a t) -> p a t", a=4)
        sz = sz_.rearrange("p (a t) -> p a t", a=4)
        ssq = xflat[:, 1024:2048].rearrange("p (a t) -> p a t", a=4)

        cosT, sinT, krA, krB, latr = carve(0, [256, 256, 256, 256, 2560])
        lraw = latr.rearrange("p (a t) -> p a t", a=10)
        lnv, lny, lnt, lrstd = carve(3584, [256] * 4)
        mq_m, mz_m, mt_m, vh_m, p_m, pt_m = carve(GEN, [512, 512, 512, 512, 1024, 1024])
        lsq = xflat[:, 0:2560].rearrange("p (a t) -> p a t", a=10)
        qn_, kn_, vt_, vrow_, zz_, zt_, qr, qro, qb = carve(1024, [512] * 6 + [256] + [256] * 2)
        mask, s_, pt_ = carve(GEN + 256, [384, 768, 768])
        qn, kn, vtm = ([w[:, 0:256], w[:, 256:512]] for w in (qn_, kn_, vt_))

        ang, kk_, tt_ = (latr[:, 256 * k:256 * k + 256] for k in range(3))
        pos_i = latr[:, 768:1024].bitcast(I32)

        rq, t12, q_r, k_r, vt_r, sd, dec, cs_r, th_r = carve(0, [512, 512, 512, 512, 512, 384, 384, 512, 512])
        o_r = kv[:, 0:1024].rearrange("p (a t) -> p a t", a=4)
        vrow_r = kv[:, 1024:2048].rearrange("p (k c) -> p k c", k=2)
        sg_r = gen[:, 1024:2048].rearrange("p (a t) -> p a t", a=4)
        sq_r = gen[:, 0:1024].rearrange("p (a t) -> p a t", a=4)

        up_t = carve(0, [256, 256, 256, 256])

        @block.sync
        def _(sp):
            def load(name, i, j, reused=True):
                c = panels(name, i)
                sizes = PHASES[name][0]
                a, b = 128 * sum(sizes[:j]), 128 * sum(sizes[:j + 1])
                if reused:
                    sp.wait_ge(split_ready, c(j, -3))
                sp.dma_start(raw[:, c.slot(j, 4), 0:sizes[j], :].rearrange("p t c -> p (t c)"),
                             streams[name][i, :, a:b]).then_inc(loaded[c.slot(j, 4)], 16)

            for name in live:
                count = len(PHASES[name][0])
                if name == "mem":
                    for j in range(count):
                        load(name, 0, j, j >= 4)
                    load_rest = 1
                else:
                    load_rest = 0
                run(sp, name, lambda i: [load(name, i, j) for j in range(count)], load_rest)
            end = Count(first_panel[live[-1]] + len(PHASES[live[-1]][0]) * PHASES[live[-1]][1])
            sp.wait_ge(split_ready, end(-3))
            sp.dma_start(raw[:, end.slot(0, 4), :, :].rearrange("p t c -> p (t c)"),
                         streams["mem"][0, :, 0:2048]).then_inc(loaded[end.slot(0, 4)], 16)
            sp.wait_ge(loaded[end.slot(0, 4)], end.filled(0))
            if debug is None:
                sp.wait_ge(S["fin_taken"], 8)
                sp.dma_start(out.rearrange("b (r p) c -> p (b r) c", p=P), rows).then_inc(S["out_done"], 16)
            else:
                sp.wait_ge(S["x_tile"], RES[live[-1]] + 16)
                sp.dma_start(debug, xflat).then_inc(S["out_done"], 16)
            sp.wait_ge(S["out_done"], 16)

        @block.gpsimd
        def _(pool):
            pool.nop().then_inc(S["kv_free"], 1)

            def spill(i):
                pool.wait_ge(S["v_rows_taken"], i * 4 + 4)
                pool.dma_start(kv_spill[i], kv[:]).then_inc(S["kv_spilled"], 16)
                pool.wait_ge(S["kv_spilled"], i * 16 + 16)
                pool.nop().then_inc(S["kv_free"], 1)
            run(pool, "mem", spill)
            if "ssd" in live:
                pool.wait_ge(S["x_tile"], 16)
                pool.dma_start(x_spill, xflat).then_inc(S["x_spilled"], 16)
                pool.wait_ge(S["y_ssd"], 4)
                pool.wait_ge(S["x_spilled"], 16)
                pool.dma_start(xflat, x_spill).then_inc(S["x_loaded"], 16)
                pool.wait_ge(S["y_mem"], 4)
                pool.dma_start(kv[:], kv_spill[0]).then_inc(S["kv_loaded"], 16)
            if "latent" in live:
                pool.wait_ge(S["h_ready"], 4)
                pool.wait_ge(S["x_loaded"], 16)
                pool.dma_start(x_spill, xflat).then_inc(S["x_spilled"], 16)
                pool.dma_start(pos_i, pos).then_inc(S["pos_loaded"], 16)
                pool.wait_ge(S["x_spilled"], 32)
                pool.wait_ge(S["lat_ready"], 2)
                pool.dma_start(mask, mla_mask).then_inc(S["mask_loaded"], 16)
                pool.wait_ge(S["y_mla"], 8)
                pool.dma_start(xflat, x_spill).then_inc(S["x_loaded"], 16)
            if "ret_a" in live:
                pool.wait_ge(S["h_ready"], 8)
                pool.dma_start(cs_r, ret_tab).then_inc(S["ret_tab_loaded"], 16)
                pool.dma_start(dec, ret_decay[0]).then_inc(S["decay_loaded"], 16)
                for half_, ph in enumerate(("ret_a", "ret_b")):
                    if ph not in live:
                        continue
                    first, last = (0, 4) if half_ == 0 else (4, 8)
                    if half_:
                        pool.wait_ge(S["x_tile"], RES["ret_out_a"] + 16)
                        pool.dma_start(cs_r, ret_tab).then_inc(S["ret_tab_loaded"], 16)
                        pool.dma_start(dec, ret_decay[4]).then_inc(S["decay_loaded"], 16)
                    with pool.Fori(first + 1, last) as h:
                        pool.wait_ge(S["decay_used"], h * 1)
                        pool.dma_start(dec, ret_decay[h]).then_inc(S["decay_loaded"], 16)
                    pool.wait_ge(S["decay_loaded"], 16 * last)
            if "ssd" in live:
                pool.wait_ge(S["kv_loaded"], 16)

        @block.scalar
        def _(act):
            A = nc.scalar.activation

            def split(name, i, j):
                c, n = panels(name, i), next_size(name, j)
                act.wait_ge(loaded[c.slot(j + 1, 4)], c.filled(j + 1))
                act.wait_ge(panel_started, c(j + 1, 1))
                A(w_hi[:, c.slot(j + 1, 2), 0:n, :], raw[:, c.slot(j + 1, 4), 0:n, :], ACT.Copy).then_inc(hi_ready, 1)

            def copy_half(name, i, o, weight=1):
                c = outputs(name, i)
                act.wait_ge(output_ready, c(o, 1))
                A(half[:, c.slot(o, NB)], pj[:, c.slot(o, NB), 0:T], ACT.Copy).then_inc(half_copied, weight)

            def rsqrt(k, v, y):
                act.wait_ge(S["var_ready"], k)
                A(y, v, ACT.Ln)
                act.drain()
                A(y, y, ACT.Exp, scale=-0.5).then_inc(S["rsqrt_ready"], 1)

            act.dma_start(mem_rows, mem.rearrange("b (r p) c -> p (b r) c", p=P)).then_inc(S["mem_rows"], 16)
            act.dma_start(vec[:], vecs).then_inc(S["tables"], 16)
            act.dma_start(con[:], consts).then_inc(S["tables"], 16)
            act.dma_start(rows, x.rearrange("b (r p) c -> p (b r) c", p=P)).then_inc(S["x_rows"], 16)
            act.dma_start(wdt[:], w_dt).then_inc(S["tables"], 16)
            for k, (src, loaded_, sq_, var_, rs_, dst, w) in enumerate((
                    (mem_rows, "mem_rows", "mem_squares", "mem_var", "mem_rsqrt", ys, "mem_norm"),
                    (rows, "x_rows", "x_squares", "x_var", "x_rsqrt", hs, "norm0"))):
                act.wait_ge(S[loaded_], 16)
                for r in range(2):
                    junk = hs[:, 8 * k + 4 * r:8 * k + 4 * r + 4].rearrange("p a b c -> p (a b c)")
                    A(junk, src[:, r], ACT.Square, accum_out=ss[:, 2 * k + r:2 * k + r + 1])
                act.drain().then_inc(S[sq_], 1)
                if k == 0:
                    act.wait_ge(loaded[0], 16)
                    A(w_hi[:, 0], raw[:, 0], ACT.Copy).then_inc(hi_ready, 1)
                    act.wait_ge(S["tables"], 48)
                act.wait_ge(S[var_], 1)
                A(rs4[:, 2 * k:2 * k + 2], var4[:, 2 * k:2 * k + 2], ACT.Ln)
                act.drain()
                A(rs4[:, 2 * k:2 * k + 2], rs4[:, 2 * k:2 * k + 2], ACT.Exp, scale=-0.5).then_inc(S[rs_], 1)
                for g in range(8):
                    act.wait_ge(S["transposed"], 16 * k + g + 1)
                    for u in range(2):
                        c = 2 * g + u
                        A(dst[:, c, 0], mx[:, (16 * k + g) % 6, T * u:T * (u + 1)], ACT.Copy,
                          scale=V(w, c)).then_inc(S["part_hi"], 1)

            def mem_body(i):
                for j in range(8):
                    split("mem", i, j)
                    copy_half("mem", i, j)
                    if j >= 5:
                        value_rows(i, j - 5)
                value_rows(i, 3)

            def value_rows(i, n):
                act.wait_ge(S["v_rows"], i * 4 + n + 1)
                A(values[:, :, 128 * n:128 * n + 128], mx[:, n, 0:256].rearrange("p (m c) -> p m c", m=2),
                  ACT.Copy).then_inc(S["v_rows_taken"], 1)
            run(act, "mem", mem_body)

            def gate_body(i):
                for j in range(4):
                    split("gate", i, j)
                    if j == 1:
                        act.wait_ge(evacuated, outputs("gate", i)(0, 1 + NB))
                        A(th_g, z_g, ACT.Tanh, scale=0.5).then_inc(S["gate_tanh"], 1)
                    copy_half("gate", i, j)
            run(act, "gate", gate_body)

            act.wait_ge(S["dt_exp_in"], 1)
            A(dtw[2], dtw[1], ACT.Exp)
            A(ea, vec[:, VEC["a_log"][0]:VEC["a_log"][1]], ACT.Exp)
            act.drain().then_inc(S["dt_exp"], 1)

            def gate_out_body(i):
                for j in range(4):
                    split("gate_out", i, j)
                    copy_half("gate_out", i, 2 * j)
                    copy_half("gate_out", i, 2 * j + 1)
            run(act, "gate_out", gate_out_body)
            act.wait_ge(S["dte_logits"], 1)
            A(dte, mx[:, 1, 0:32], ACT.Exp).then_inc(S["dte_ready"], 1)

            def residual(name, ppo):
                def body(i):
                    for j in range(len(PHASES[name][0])):
                        split(name, i, j)
                        if j % ppo == ppo - 1:
                            o = j // ppo
                            copy_half(name, i, o)
                            act.wait_ge(S["x_tile"], i * 4 + (RES[name] + o + 1))
                            A(sq[o % 2], xT[:, i * 4 + o], ACT.Square).then_inc(S["x_square"], 1)
                run(act, name, body)

            def boundary(k, hk, split_h=True):
                rsqrt(NORM[k] + 1, nv, ny)
                if split_h:
                    for q in range(4):
                        act.wait_ge(S["h_f32"], 4 * hk + q + 1)
                        A(hs[:, 4 * q:4 * q + 4, 0], hf[q % 2].rearrange("p (a t) -> p a t", a=4),
                          ACT.Copy).then_inc(S["h_hi"], 1)

            def mem_exp(c, heads, scores, probs, vh, values_):
                for u in range(heads):
                    A(vh[u].rearrange("p (m c) -> p m c", m=2), values_(u), ACT.Copy)
                    act.wait_ge(S["mem_shift"], c(u, 1))
                    for q in range(2):
                        A(probs[u][:, T * q:T * q + T], scores(u)[:, T * q:T * q + T], ACT.Exp, scale=MEM_SCALE,
                          bias=mstat[:, 4 * u + q:4 * u + q + 1], accum_out=mstat[:, 4 * u + 2 + q:4 * u + 3 + q])
                    act.drain().then_inc(S["mem_probs"], 1)

            def ssd_body(i):
                O = outputs("ssd", i)
                M = Count(0, 1, i)
                for j in range(12):
                    split("ssd", i, j)
                    if 1 <= j <= 6:
                        act.wait_ge(S["conv_done"], i * 6 + j)
                        A(th[(j - 1) % 2], cv[(j - 1) % 2], ACT.Tanh).then_inc(S["conv_tanh"], 1)
                    if j == 5:
                        act.wait_ge(S["x_spilled"], 16)
                        act.wait_ge(S["cb_ready"], i * 1 + 1)
                        A(brow, mx[:, 0, 256:384], ACT.Copy).then_inc(S["brow_ready"], 1)
                    if j in (6, 7, 9, 10):
                        r = {6: 0, 7: 1, 9: 2, 10: 3}[j]
                        act.wait_ge(S["seg_ready"], i * 4 + r + 1)
                        if r >= 2:
                            act.wait_ge(S["ydiag_ready"], i * 4 + r - 1)
                        A(em[r % 2], mx[:, 1 + r % 2], ACT.Exp).then_inc(S["decay_ready"], 1)
                    if j == 8:
                        act.wait_ge(evacuated, O(7, 1 + NB))
                        A(cv1, th0, ACT.Tanh, scale=0.5).then_inc(S["mz_tanh"], 1)
                    if j == 9:
                        act.wait_ge(S["state_ready"], i * 1 + 1)
                        A(state, mx[:, 5], ACT.Copy).then_inc(S["state_copied"], 1)
                    if j >= 9:
                        act.wait_ge(evacuated, O(j - 1, 1 + NB))
                        A(sz[:, j - 9], cp[(j - 9) % 2][:, 3:259], ACT.Tanh, scale=0.5).then_inc(S["z_tanh"], 1)
                    if j == 10:
                        act.wait_ge(S["ydiag_ready"], i * 4 + 3)
                        mem_exp(M, 1, lambda u: mx[:, 1], [em0], [th1],
                                lambda u: values[:, :, bass.ds(i * 128, 128)])
                    if j == 11:
                        act.wait_ge(S["mem_pt"], M(0, 1))
                        A(r1, mx[:, 5], ACT.Copy).then_inc(S["mem_pt_copied"], 1)
                    copy_half("ssd", i, j)
                act.wait_ge(S["eq_logits"], i * 1 + 1)
                A(xdte, mx[:, 2], ACT.Exp).then_inc(S["eq_ready"], 1)
                act.wait_ge(evacuated, O(11, 1 + NB))
                A(sz[:, 3], cp1[:, 3:259], ACT.Tanh, scale=0.5).then_inc(S["z_tanh"], 1)
                act.wait_ge(S["ssd_gated"], i * 1 + 1)
                A(ssq, xs, ACT.Square).then_inc(S["ssd_squares"], 1)
                rsqrt(i * 1 + 1, r0[:, 0:256], em1[:, 0:256])
            if "ssd" in live:
                run(act, "ssd", ssd_body)
            if "out0" in live:
                residual("out0", 2)
            if "latent" in live:
                boundary("b_latent", 0)
                act.wait_ge(S["angle_ready"], 1)
                A(sinT, latr[:, 0:256], ACT.Sin)
                A(cosT, latr[:, 0:256], ACT.Sin, scale=0.5)
                act.drain().then_inc(S["sin_ready"], 1)

                def copy_body(name):
                    def body(i):
                        for j in range(len(PHASES[name][0])):
                            split(name, i, j)
                            copy_half(name, i, j)
                    return body
                run(act, "latent", copy_body("latent"))
                run(act, "latent_tail", copy_body("latent_tail"))

                def memq_body(i):
                    O = outputs("memq", i)
                    M = Count(4, 2, i)
                    for j in range(4):
                        split("memq", i, j)
                        if j == 3:
                            mem_exp(M, 2, lambda u: mx[:, u], [p_m[:, 0:512], p_m[:, 512:1024]],
                                    [vh_m[:, 0:256], vh_m[:, 256:512]],
                                    lambda u: values[:, :, bass.ds(i * 256 + 128 * u, 128)])
                        copy_half("memq", i, j)
                    act.wait_ge(evacuated, O(3, 1 + NB))
                    A(mt_m, mz_m, ACT.Tanh, scale=0.5).then_inc(S["mz_tanh"], 1)
                    for u in range(2):
                        act.wait_ge(S["mem_pt"], M(u, 1))
                        A(pt_m[:, 512 * u:512 * u + 512], mx[:, 2 + u], ACT.Copy).then_inc(S["mem_pt_copied"], 1)
                act.wait_ge(S["x_spilled"], 32)
                act.wait_ge(S["kv_loaded"], 16)
                run(act, "memq", memq_body)
                act.wait_ge(S["latent_ready"], 1)
                A(lsq, lraw, ACT.Square).then_inc(S["latent_squares"], 1)
                rsqrt(NORM["kv"] + 1, lnv, lny)
                rsqrt(NORM["q"] + 1, lnv, lny)
            if "mla" in live:
                def mla_body(i):
                    O = outputs("mla", i)
                    for j in range(8):
                        split("mla", i, j)
                        if j == 6:
                            act.wait_ge(S["mla_shift"], i * 1 + 1)
                            for u in range(2):
                                for q, a, b in ((0, 0, 128), (1, 128, 384)):
                                    k = 2 * u + q
                                    e = s_[:, 384 * u + a:384 * u + b]
                                    A(e, e, ACT.Exp, scale=MLA_SCALE, bias=pstat[:, k:k + 1],
                                      accum_out=pstat[:, 4 + k:5 + k])
                            act.drain().then_inc(S["mla_probs"], 1)
                        if j == 7:
                            act.wait_ge(S["mla_vt"], i * 1 + 1)
                            A(vrow_, mx[:, 2], ACT.Copy).then_inc(S["mla_vrow"], 1)
                            act.wait_ge(S["mla_pt"], i * 1 + 1)
                            A(pt_.rearrange("p (u c) -> p u c", u=2), mx[:, 3:5, 0:384],
                              ACT.Copy).then_inc(S["mla_pt_copied"], 1)
                        if j == 3:
                            copy_half("mla", i, 3)
                            copy_half("mla", i, 4)
                        elif j == 7:
                            copy_half("mla", i, 8, 2)
                        else:
                            copy_half("mla", i, j if j < 3 else j + 1)
                    act.wait_ge(evacuated, O(8, 2 + NB))
                    A(zt_, zz_, ACT.Tanh, scale=0.5).then_inc(S["mla_tanh"], 1)
                run(act, "mla", mla_body)
            if "out1" in live:
                residual("out1", 2)
            if "ret_a" in live:
                boundary("b_final", 0, split_h=False)
                for k in range(16):
                    act.wait_ge(S["x_tile"], RES["b_ret"] + k + 1)
                    A(sq[k % 2], xT[:, k], ACT.Square).then_inc(S["x_square"], 1)
                boundary("b_ret", 1)

            def ret_body(name, first):
                def body(i):
                    O = outputs(name, i)
                    for j in range(12):
                        split(name, i, j)
                        if 6 <= j <= 9:
                            n = j - 6
                            act.wait_ge(S["ret_vt"], i * 4 + (4 * first + n + 1))
                            A(vrow_r[:, :, 128 * n:128 * n + 128],
                              mx[:, 1 + n % 2, 0:256].rearrange("p (k c) -> p k c", k=2),
                              ACT.Copy).then_inc(S["ret_vrow"], 1)
                        if j == 10:
                            act.wait_ge(S["ret_pv"], i * 1 + (first + 1))
                            A(kv[:, 0:1024], mx[:, 3:5].rearrange("p b c -> p (b c)"), ACT.Copy).then_inc(S["ret_o"], 1)
                        if j >= 9:
                            n = j - 9
                            act.wait_ge(evacuated, O(j - 1, 1 + NB))
                            A(th_r[:, T * (n % 2):T * (n % 2) + T], sg_r[:, n], ACT.Tanh,
                              scale=0.5).then_inc(S["ret_tanh"], 1)
                        copy_half(name, i, j)
                    act.wait_ge(S["ret_centred"], i * 1 + (first + 1))
                    A(sq_r, o_r, ACT.Square).then_inc(S["ret_squares"], 1)
                    act.wait_ge(evacuated, O(11, 1 + NB))
                    A(th_r[:, T:2 * T], sg_r[:, 3], ACT.Tanh, scale=0.5).then_inc(S["ret_tanh"], 1)
                    rsqrt(i * 1 + (NORM[name] + 1), vt_r[:, 0:256], vt_r[:, 256:512])
                run(act, name, body)

            for ph, first in (("ret_a", 0), ("ret_b", 4)):
                if ph in live:
                    ret_body(ph, first)
                    residual("ret_out" + ph[3:], 1)
            if "up0" in live:
                boundary("b_mlp", 2)
            for b in range(FF_BLOCKS):
                if f"up{b}" in live:
                    def up_body(i):
                        for j in range(4):
                            split(f"up{b}", i, j)
                            copy_half(f"up{b}", i, j)
                    run(act, f"up{b}", up_body)
                    residual(f"down{b}", 1)
            if debug is None:
                boundary("b_out", 0, split_h=False)
                for g in range(8):
                    act.wait_ge(S["fin_rows"], g + 1)
                    A(rows[:, g // 4, 512 * (g % 4):512 * (g % 4) + 512], mx[:, g % 6], ACT.Copy).then_inc(S["fin_taken"], 1)
        @block.vector
        def _(dve):
            v = nc.vector
            TT, TS, STT = v.tensor_tensor, v.tensor_scalar, v.scalar_tensor_tensor

            def split(name, i, j):
                c, n = panels(name, i), next_size(name, j)
                dve.wait_ge(hi_ready, c(j + 1, 1))
                s2, s4 = c.slot(j + 1, 2), c.slot(j + 1, 4)
                TT(w_lo[:, s2, 0:n, :], raw[:, s4, 0:n, :], w_hi[:, s2, 0:n, :].bitcast(F32),
                   ALU.subtract).then_inc(split_ready, 1)

            def evac(name, i, o, dst, weight=1):
                c = outputs(name, i)
                dve.wait_ge(half_copied, c(o, 1))
                k = c.slot(o, NB)
                TT(dst, pj[:, k, T:2 * T], half[:, k], ALU.add).then_inc(evacuated, weight)

            def hi_lo(dst, src):
                dve.drain()
                v.tensor_copy(dst[0], src)
                dve.drain()
                return TT(dst[1], src, dst[0].bitcast(F32), ALU.subtract)

            def newton(vv, y, t, out_, s=1.0):
                TT(t, y, y, ALU.mult)
                dve.drain()
                TT(t, t, vv, ALU.mult)
                dve.drain()
                TS(t, t, -0.5, 1.5, ALU.mult, ALU.add)
                dve.drain()
                ins = TT(out_, y, t, ALU.mult)
                dve.drain()
                return ins

            def inverse_rms(k, bank, n, vv, y, t, out_):
                dve.wait_ge(S["stat_ready"], k)
                TS(vv, mx[:, bank, 0:T], 1.0 / n, EPS, ALU.mult, ALU.add).then_inc(S["var_ready"], 1)
                dve.wait_ge(S["rsqrt_ready"], k)
                newton(vv, y, t, out_)

            v.nop().then_inc(evacuated, NB)
            for k, (sq_, var_, rs_, rows_, scaled) in enumerate((
                    ("mem_squares", "mem_var", "mem_rsqrt", mem_rows, "mem_scaled"),
                    ("x_squares", "x_var", "x_rsqrt", rows, "x_scaled"))):
                a, b = 2 * k, 2 * k + 2
                dve.wait_ge(S[sq_], 1)
                TS(var4[:, a:b], ss[:, a:b], 1.0 / D, EPS, ALU.mult, ALU.add).then_inc(S[var_], 1)
                if k == 0:
                    dve.wait_ge(hi_ready, 1)
                    TT(w_lo[:, 0], raw[:, 0], w_hi[:, 0].bitcast(F32), ALU.subtract).then_inc(split_ready, 1)
                else:
                    dve.wait_ge(S["transposed"], 16)
                dve.wait_ge(S[rs_], 1)
                newton(var4[:, a:b], rs4[:, a:b], tmp4[:, a:b], rs4[:, a:b])
                for r in range(2):
                    ins = TS(rows_[:, r], rows_[:, r], rs4[:, a + r:a + r + 1], None, ALU.mult)
                ins.then_inc(S[scaled], 1)
                if k == 0:
                    for g in range(8):
                        for u in range(2):
                            c = 2 * g + u
                            dve.wait_ge(S["part_hi"], 2 * g + 2)
                            STT(out=ys[:, c, 1], in0=mx[:, g % 6, T * u:T * u + T], scalar=V("mem_norm", c),
                                in1=ys[:, c, 0].bitcast(F32), op0=ALU.mult,
                                op1=ALU.subtract).then_inc(S["part_taken"], 1)
                    for g in range(8):
                        dve.wait_ge(S["transposed"], 8 + g + 1)
                        v.tensor_copy(xT[:, 2 * g:2 * g + 2].rearrange("p a t -> p (a t)"),
                                      mx[:, (8 + g) % 6]).then_inc(S["part_taken"], 2)
            for g in range(8):
                for u in range(2):
                    c = 2 * g + u
                    dve.wait_ge(S["part_hi"], 16 + 2 * g + 2)
                    STT(out=hs[:, c, 1], in0=mx[:, (16 + g) % 6, T * u:T * u + T], scalar=V("norm0", c),
                        in1=hs[:, c, 0].bitcast(F32), op0=ALU.mult, op1=ALU.subtract).then_inc(S["part_taken"], 1)

            def mem_body(i):
                for j in range(8):
                    split("mem", i, j)
                    if j == 0:
                        dve.wait_ge(S["kv_free"], i * 1 + 1)
                    if j >= 6:
                        dve.wait_ge(S["v_rows"], i * 4 + (j - 5))
                    evac("mem", i, j, keys[:, j] if j < 4 else vt[j % 2])
            run(dve, "mem", mem_body)

            v.memset(u_g[:, 0:2], 0.0)
            a_v = VEC["ssd_conv"][0]
            TS(vec[:, a_v:a_v + 30 * GROUPS], vec[:, a_v:a_v + 30 * GROUPS], 0.5, None, ALU.mult)

            def gate_body(i):
                w0 = VEC["gate_conv"][0]

                def tap(k):
                    return vec[:, bass.ds(i * 3 + (w0 + k), 1)]
                split("gate", i, 0)
                evac("gate", i, 0, z_g)
                split("gate", i, 1)
                evac("gate", i, 1, c_g)
                dve.wait_ge(S["gate_tanh"], i * 1 + 1)
                STT(out=s_g, in0=th_g, scalar=1.0, in1=z_g, op0=ALU.add, op1=ALU.mult)
                split("gate", i, 2)
                evac("gate", i, 2, v_g)
                dve.drain()
                TT(u_g[:, 2:258], c_g, v_g, ALU.mult)
                split("gate", i, 3)
                dve.drain()
                TS(a_g, u_g[:, 0:256], tap(0), None, ALU.mult)
                dve.drain()
                STT(out=e_g, in0=u_g[:, 1:257], scalar=tap(1), in1=a_g, op0=ALU.mult, op1=ALU.add)
                dve.drain()
                STT(out=a_g, in0=u_g[:, 2:258], scalar=tap(2), in1=e_g, op0=ALU.mult, op1=ALU.add)
                evac("gate", i, 3, b_g)
                dve.drain()
                STT(out=e_g, in0=a_g, scalar=0.5, in1=b_g, op0=ALU.mult, op1=ALU.mult)
                dve.drain()
                TT(a_g, e_g, s_g, ALU.mult)
                hi_lo((ys[:, i, 0], ys[:, i, 1]), a_g).then_inc(S["y_gate"], 1)
            run(dve, "gate", gate_body)

            zt, mn, ex, den, s1, zz, pp, tt = dtw
            dve.wait_ge(S["dt_logits"], 1)
            b0 = VEC["dt_bias"][0]
            TT(zt, mx[:, 0, 0:64].rearrange("p (c h) -> p c h", c=2),
               vec[:, b0:b0 + 32].unsqueeze(1).to_broadcast([P, 2, 32]), ALU.add)
            dve.drain()
            TS(tt, zt, -1.0, None, ALU.mult)
            dve.drain()
            TT(mn, zt, tt, ALU.min).then_inc(S["dt_exp_in"], 1)
            dve.wait_ge(S["dt_exp"], 1)
            TS(den, ex, 2.0, None, ALU.add)
            dve.drain()
            v.reciprocal(den, den)
            dve.drain()
            TT(s1, ex, den, ALU.mult)
            dve.drain()
            TT(zz, s1, s1, ALU.mult)
            dve.drain()
            TS(pp, zz, 1.0 / 15, None, ALU.mult)
            dve.drain()
            for k in (13, 11, 9, 7, 5, 3):
                STT(out=pp, in0=pp, scalar=1.0 / k, in1=zz, op0=ALU.add, op1=ALU.mult)
                dve.drain()
            STT(out=pp, in0=pp, scalar=1.0, in1=s1, op0=ALU.add, op1=ALU.mult)
            TS(zt, zt, 0.0, None, ALU.max)
            dve.drain()
            STT(out=dt, in0=pp, scalar=2.0, in1=zt, op0=ALU.mult, op1=ALU.add)
            dve.drain()
            STT(out=da, in0=dt, scalar=-1.0, in1=ea.unsqueeze(1).to_broadcast([P, 2, 32]), op0=ALU.mult,
                op1=ALU.mult).then_inc(S["dt_ready"], 1)

            def residual(name, ppo, squares=True, opp=1):
                r0_ = RES[name]
                n_out = outs_per.get(name, len(PHASES[name][0]))
                if squares:
                    dve.drain()
                    v.memset(acc, 0.0)

                def body(i):
                    for j in range(len(PHASES[name][0])):
                        split(name, i, j)
                        if j % ppo != ppo - 1:
                            continue
                        for u in range(opp):
                            o = j // ppo * opp + u
                            evac(name, i, o, res[o % 2])
                            dve.drain()
                            xo = xT[:, i * n_out + o]
                            TT(xo, xo, res[o % 2], ALU.add).then_inc(S["x_tile"], 1)
                            if squares:
                                dve.wait_ge(S["x_square"], i * n_out + (r0_ - 16 + o + 1))
                                TT(acc, acc, sq[o % 2], ALU.add)
                run(dve, name, body)
                if squares:
                    dve.drain().then_inc(S["acc_ready"], 1)

            if "gate_out" in live:
                residual("gate_out", 1, False, 2)

            def boundary(k, hk, w):
                inverse_rms(NORM[k] + 1, 0, D, nv, ny, nt, rstd)
                for q in range(4):
                    if q >= 2:
                        dve.wait_ge(S["h_hi"], 4 * hk + q - 1)
                        dve.drain()
                    for u in range(4):
                        c = 4 * q + u
                        ins = STT(out=hf[q % 2][:, T * u:T * u + T], in0=xT[:, c], scalar=V(w, c), in1=rstd,
                                  op0=ALU.mult, op1=ALU.mult)
                    ins.then_inc(S["h_f32"], 1)
                    if q:
                        h_lo(hk, q - 1)
                h_lo(hk, 3)

            def h_lo(hk, q):
                dve.wait_ge(S["h_hi"], 4 * hk + q + 1)
                TT(hs[:, 4 * q:4 * q + 4, 1], hf[q % 2].rearrange("p (a t) -> p a t", a=4),
                   hs[:, 4 * q:4 * q + 4, 0].bitcast(F32), ALU.subtract).then_inc(S["h_ready"], 1)

            def softmax(M, heads, scores, probs, gap):
                for u in range(heads):
                    dve.wait_ge(S["mem_scores"], M(u, 1))
                    v.reduce_max(mstat[:, 4 * u:4 * u + 2], scores(u).rearrange("p (q k) -> p q k", q=2), AX.X)
                    dve.drain()
                    TS(mstat[:, 4 * u:4 * u + 2], mstat[:, 4 * u:4 * u + 2], -MEM_SCALE, None,
                       ALU.mult).then_inc(S["mem_shift"], 1)
                gap()
                for u in range(heads):
                    dve.wait_ge(S["mem_probs"], M(u, 1))
                    v.reciprocal(mstat[:, 4 * u + 2:4 * u + 4], mstat[:, 4 * u + 2:4 * u + 4])
                    dve.drain()
                    for q in range(2):
                        ins = TS(probs[u][:, T * q:T * q + T], probs[u][:, T * q:T * q + T],
                                 mstat[:, 4 * u + 2 + q:4 * u + 3 + q], None, ALU.mult)
                    ins.then_inc(S["mem_scaled_probs"], 1)

            def rope(dst, tmp):
                for h in range(4):
                    a, b = 32 * h, 32 * (h ^ 1)
                    TT(tmp[a:a + 32], dst[b:b + 32], sinT[b:b + 32], ALU.mult)
                dve.drain()
                TT(dst, dst, cosT, ALU.mult)
                dve.drain()
                ins = TT(dst, dst, tmp, ALU.add)
                dve.drain()
                return ins

            if "ssd" in live:
                dve.drain()
                v.memset(cp0[:, 0:3], 0.0)
                v.memset(cp1[:, 0:3], 0.0)

            def ssd_body(i):
                w0 = VEC["ssd_conv"][0]
                M = Count(0, 1, i)
                xdt_v = [w.rearrange("p (h d) -> p h d", h=8) for w in xdt]

                def conv(n):
                    src, t3, t2 = cp[n % 2], cv[n % 2], th[n % 2]

                    def w(k):
                        return vec[:, bass.ds(i * 30 + (w0 + 5 * n + k), 1)]
                    dve.drain()
                    TS(t2, src[:, 0:256], w(0), w(4), ALU.mult, ALU.add)
                    dve.drain()
                    STT(out=t3, in0=src[:, 1:257], scalar=w(1), in1=t2, op0=ALU.mult, op1=ALU.add)
                    dve.drain()
                    STT(out=t2, in0=src[:, 2:258], scalar=w(2), in1=t3, op0=ALU.mult, op1=ALU.add)
                    dve.drain()
                    STT(out=t3, in0=src[:, 3:259], scalar=w(3), in1=t2, op0=ALU.mult,
                        op1=ALU.add).then_inc(S["conv_done"], 1)

                def silu(n):
                    dve.wait_ge(S["conv_tanh"], i * 6 + (n + 1))
                    dst = (bT, cT, xs[:, 0], xs[:, 1], xs[:, 2], xs[:, 3])[n]
                    ins = STT(out=dst, in0=th[n % 2], scalar=1.0, in1=cv[n % 2], op0=ALU.add, op1=ALU.mult)
                    if n == 1:
                        ins.then_inc(S["bc_ready"], 1)
                    if n == 5:
                        ins.then_inc(S["xs_ready"], 1)

                def seg_rhs(r):
                    if r >= 2:
                        dve.wait_ge(S["seg_ready"], i * 4 + r - 1)
                    TT(rr[r % 2].rearrange("p (h q) -> p h q", h=4),
                       da[:, r // 2, bass.ds(i * 8 + 4 * (r % 2), 4)].unsqueeze(2).to_broadcast([P, 4, 128]),
                       upto.unsqueeze(1).to_broadcast([P, 4, 128]), ALU.mult).then_inc(S["seg_rhs"], 1)

                def mix(r):
                    dve.wait_ge(S["decay_ready"], i * 4 + r + 1)
                    e = em[r % 2].rearrange("p (h q) -> p h q", h=4)
                    c = r // 2
                    TT(e, e, cbm[:, 128 * c:128 * c + 128].unsqueeze(1).to_broadcast([P, 4, 128]),
                       ALU.mult).then_inc(S["mix_ready"], 1)

                def z_gate(n):
                    dve.wait_ge(S["z_tanh"], i * 4 + n + 1)
                    STT(out=sz[:, n], in0=sz[:, n], scalar=1.0, in1=cp[n % 2][:, 3:259], op0=ALU.add, op1=ALU.mult)

                for j in range(12):
                    split("ssd", i, j)
                    if j >= 2 and j <= 7:
                        silu(j - 2)
                    if 1 <= j <= 6:
                        conv(j - 1)
                    if j == 5:
                        dve.wait_ge(S["brow_ready"], i * 1 + 1)
                        TT(cbm.rearrange("p (c q) -> p c q", c=2), mx[:, 0, 0:256].rearrange("p (c q) -> p c q", c=2),
                           upto.unsqueeze(1).to_broadcast([P, 2, 128]), ALU.mult).then_inc(S["cb_taken"], 1)
                    if 4 <= j <= 7:
                        seg_rhs(j - 4)
                        if j == 4:
                            dve.wait_ge(S["x_spilled"], 16)
                    if j in (6, 7, 9, 10):
                        mix({6: 0, 7: 1, 9: 2, 10: 3}[j])
                    if j == 8:
                        dve.wait_ge(S["xs_rows"], i * 1 + 1)
                        for c, bank in ((0, 5), (1, 0)):
                            TT(xdt_v[c], mx[:, bank].rearrange("p (h d) -> p h d", h=8),
                               dt[:, c, bass.ds(i * 8, 8)].unsqueeze(2).to_broadcast([P, 8, 64]), ALU.mult)
                        dve.drain()
                        TT(xdte.rearrange("p (h d) -> p h d", h=8), xdt_v[0],
                           dte[:, bass.ds(i * 8, 8)].unsqueeze(2).to_broadcast([P, 8, 64]),
                           ALU.mult).then_inc(S["xdt_ready"], 1)
                    if j == 9:
                        dve.wait_ge(S["seg_ready"], i * 4 + 3)
                        TT(r0.rearrange("p (h d) -> p h d", h=8),
                           da[:, 1, bass.ds(i * 8, 8)].unsqueeze(2).to_broadcast([P, 8, 64]),
                           ones[:, 0:64].unsqueeze(1).to_broadcast([P, 8, 64]), ALU.mult).then_inc(S["eq_lhs"], 1)
                        dve.wait_ge(S["mz_tanh"], i * 1 + 1)
                        STT(out=th0, in0=cv1, scalar=1.0, in1=th0, op0=ALU.add, op1=ALU.mult)
                    if j >= 9:
                        z_gate(j - 9)
                    if j == 10:
                        softmax(M, 1, lambda u: mx[:, 1], [em0], lambda: None)
                    dst = (cp0[:, 3:259], cp1[:, 3:259], cp0[:, 3:259], cp1[:, 3:259], cp0[:, 3:259], cp1[:, 3:259],
                           cv0, th0, cp0[:, 3:259], cp1[:, 3:259], cp0[:, 3:259], cp1[:, 3:259])[j]
                    evac("ssd", i, j, dst)
                dve.wait_ge(S["mem_pv"], M(0, 1))
                STT(out=cv1, in0=mx[:, 1, 0:256], scalar=0.5, in1=th0, op0=ALU.mult, op1=ALU.mult)
                hi_lo((ys[:, i, 0], ys[:, i, 1]), cv1).then_inc(S["y_mem"], 1)
                dve.wait_ge(S["ydiag_ready"], i * 4 + 4)
                d0 = VEC["ssd_d"][0]
                for n in range(4):
                    for c in range(2):
                        w = xs[:, n, 128 * c:128 * c + 128]
                        STT(out=w, in0=w, scalar=vec[:, bass.ds(i * 4 + (d0 + n), 1)],
                            in1=mx[:, 3 + c, 128 * n:128 * n + 128], op0=ALU.mult, op1=ALU.add)
                dve.wait_ge(S["yoff_ready"], i * 1 + 1)
                dve.wait_ge(S["eq_ready"], i * 1 + 1)
                TT(xdte, mx[:, 0], xdte, ALU.mult)
                dve.drain()
                TT(xs[:, :, 128:256], xs[:, :, 128:256], xdte.rearrange("p (a q) -> p a q", a=4), ALU.add)
                z_gate(3)
                dve.drain()
                STT(out=xs_, in0=xs_, scalar=0.5, in1=sz_, op0=ALU.mult, op1=ALU.mult).then_inc(S["ssd_gated"], 1)
                inverse_rms(i * 1 + 1, 5, 512, r0[:, 0:256], em1[:, 0:256], r0[:, 256:512], em1[:, 256:512])
                n0 = VEC["ssd_norm"][0]
                for n in range(4):
                    STT(out=xs[:, n], in0=xs[:, n], scalar=vec[:, bass.ds(i * 4 + (n0 + n), 1)], in1=em1[:, 256:512],
                        op0=ALU.mult, op1=ALU.mult)
                hi_lo((ys[:, bass.ds(i * 4 + 4, 4), 0], ys[:, bass.ds(i * 4 + 4, 4), 1]), xs).then_inc(S["y_ssd"], 1)
            if "ssd" in live:
                run(dve, "ssd", ssd_body)
            if "out0" in live:
                dve.wait_ge(S["x_loaded"], 16)
                residual("out0", 2)
            if "latent" in live:
                boundary("b_latent", 0, "norm1")
                dve.wait_ge(S["pos_loaded"], 16)
                v.tensor_copy(tt_, pos_i)
                dve.drain()
                TS(ang, tt_, V("inv_freq"), None, ALU.mult)
                dve.drain()
                TS(kk_, ang, float(np.float32(1 / (2 * np.pi))), 12582912.0, ALU.mult, ALU.add)
                dve.drain()
                TS(kk_, kk_, -12582912.0, None, ALU.add)
                two_pi = 2 * np.pi
                c1 = 6.28125
                c2 = float(np.float32(np.round((two_pi - c1) * 2 ** 22) / 2 ** 22))
                c3 = float(np.float32(two_pi - c1 - c2))
                for cc in (c1, c2, c3):
                    dve.drain()
                    STT(out=ang, in0=kk_, scalar=-cc, in1=ang, op0=ALU.mult, op1=ALU.add)
                dve.drain()
                pi = float(np.nextafter(np.float32(np.pi), np.float32(0)))
                TS(ang, ang, pi, -pi, ALU.min, ALU.max).then_inc(S["angle_ready"], 1)
                dve.wait_ge(S["sin_ready"], 1)
                TT(cosT, cosT, cosT, ALU.mult)
                TS(sinT, sinT, V("sin_sign"), None, ALU.mult)
                dve.drain()
                TS(cosT, cosT, -2.0, 1.0, ALU.mult, ALU.add)
                dve.drain()

                def latent_body(i):
                    for j in range(4):
                        split("latent", i, j)
                        evac("latent", i, j, lraw[:, i * 4 + j])
                run(dve, "latent", latent_body)
                for j in range(3):
                    split("latent_tail", 0, j)
                    evac("latent_tail", 0, j, lraw[:, 8 + j] if j < 2 else krA)
                dve.drain()
                rope(krA, lnv)
                v.tensor_copy(krB[64:128], krA[64:128])
                v.memset(krB[0:64], 0.0)
                dve.drain()
                v.memset(krA[64:128], 0.0).then_inc(S["krope_ready"], 1)
                dve.wait_ge(S["x_spilled"], 32)

                def memq_body(i):
                    M = Count(4, 2, i)
                    for j in range(4):
                        split("memq", i, j)
                        if j == 3:
                            softmax(M, 2, lambda u: mx[:, u], [p_m[:, 0:512], p_m[:, 512:1024]], lambda: None)
                        evac("memq", i, j, (mq_m, mz_m)[j // 2][:, T * (j % 2):T * (j % 2) + T])
                    dve.wait_ge(S["mz_tanh"], i * 1 + 5)
                    STT(out=mz_m, in0=mt_m, scalar=1.0, in1=mz_m, op0=ALU.add, op1=ALU.mult)
                    dve.drain()
                    dve.wait_ge(S["mem_pv"], M(1, 1))
                    STT(out=mt_m.rearrange("p (u t) -> p u t", u=2), in0=mx[:, 4:6, 0:256], scalar=0.5,
                        in1=mz_m.rearrange("p (u t) -> p u t", u=2), op0=ALU.mult, op1=ALU.mult)
                    yy = ys[:, bass.ds(i * 2, 2)]
                    hi_lo((yy[:, :, 0], yy[:, :, 1]), mt_m.rearrange("p (u t) -> p u t", u=2)
                          ).then_inc(S["y_mem"], 2)
                run(dve, "memq", memq_body)
                dve.drain().then_inc(S["latent_ready"], 1)
                for k, (name, a, b) in enumerate((("kv", 0, 4), ("q", 4, 10))):
                    inverse_rms(NORM[name] + 1, k, 128 * (b - a), lnv, lny, lnt, lrstd)
                    for c in range(a, b):
                        STT(out=lraw[:, c], in0=lraw[:, c], scalar=V(name + "_norm", c - a), in1=lrstd, op0=ALU.mult,
                            op1=ALU.mult)
                    hi_lo((lat[:, a:b, 0], lat[:, a:b, 1]), lraw[:, a:b]).then_inc(S["lat_ready"], 1)

            if "mla" in live:
                dve.wait_ge(S["mask_loaded"], 16)
                s3 = s_.rearrange("p (u c) -> p u c", u=2)

                def mla_body(i):
                    for j in range(8):
                        split("mla", i, j)
                        if j == 3:
                            dve.drain()
                            rope(qr, qro)
                        if j == 5:
                            dve.wait_ge(S["mla_scores"], i * 1 + 1)
                            TT(s3, mx[:, 0:2, 0:384], mask.unsqueeze(1).to_broadcast([P, 2, 384]), ALU.add)
                            dve.drain()
                            pm = pstat[:, 0:4].rearrange("p (u q) -> p u q", u=2)
                            v.reduce_max(pm[:, :, 0], s3[:, :, 0:128], AX.X)
                            v.reduce_max(pm[:, :, 1], s3[:, :, 128:384], AX.X)
                            dve.drain()
                            TS(pstat[:, 0:4], pstat[:, 0:4], -MLA_SCALE, None, ALU.mult).then_inc(S["mla_shift"], 1)
                        if j == 6:
                            dve.wait_ge(S["mla_probs"], i * 1 + 1)
                            v.reciprocal(pstat[:, 8:12], pstat[:, 4:8])
                            dve.drain()
                            for u in range(2):
                                for q, a, b in ((0, 0, 128), (1, 128, 384)):
                                    k = 8 + 2 * u + q
                                    e = s_[:, 384 * u + a:384 * u + b]
                                    ins = TS(e, e, pstat[:, k:k + 1], None, ALU.mult)
                            ins.then_inc(S["mla_probs_scaled"], 1)
                        if j == 3:
                            evac("mla", i, 3, kn[0])
                            evac("mla", i, 4, kn[1])
                            dve.drain().then_inc(S["qk_ready"], 1)
                        elif j == 7:
                            evac("mla", i, 8, zz_[:, 256:512], 2)
                        else:
                            evac("mla", i, j if j < 3 else j + 1,
                                 (qn[0], qn[1], qr, None, vtm[0], vtm[1], zz_[:, 0:256])[j])
                    dve.wait_ge(S["mla_tanh"], i * 1 + 1)
                    STT(out=zz_, in0=zt_, scalar=1.0, in1=zz_, op0=ALU.add, op1=ALU.mult)
                    dve.drain()
                    dve.wait_ge(S["mla_pv"], i * 1 + 1)
                    STT(out=zt_, in0=mx[:, 5], scalar=0.5, in1=zz_, op0=ALU.mult, op1=ALU.mult)
                    yy = ys[:, bass.ds(i * 2 + 4, 2)]
                    hi_lo((yy[:, :, 0], yy[:, :, 1]), zt_.rearrange("p (u t) -> p u t", u=2)).then_inc(S["y_mla"], 1)
                run(dve, "mla", mla_body)
            if "out1" in live:
                dve.wait_ge(S["x_loaded"], 32)
                residual("out1", 2)
            if "ret_a" in live:
                inverse_rms(NORM["b_final"] + 1, 0, D, nv, ny, nt, rstd)
                v.memset(acc, 0.0)

                def add_square(k):
                    dve.wait_ge(S["x_square"], RES["b_ret"] - 16 + k + 1)
                    TT(acc, acc, sq[k % 2], ALU.add)
                    dve.drain()
                for k in range(16):
                    STT(out=xT[:, k], in0=xT[:, k], scalar=V("final", k), in1=rstd, op0=ALU.mult,
                        op1=ALU.mult).then_inc(S["x_tile"], 1)
                    if k:
                        add_square(k - 1)
                add_square(15)
                dve.drain().then_inc(S["acc_ready"], 1)
                boundary("b_ret", 1, "norm1_2")

            def ret_body(name, first):
                def body(i):
                    def rotate(src, dst):
                        dve.drain()
                        a, b = src[:, 0:256], src[:, 256:512]
                        t1, t2 = t12[:, 0:256], t12[:, 256:512]
                        c_, s1_ = cs_r[:, 0:256], cs_r[:, 256:512]
                        TT(t1, a, c_, ALU.mult)
                        TT(t2, b, s1_, ALU.mult)
                        dve.drain()
                        TT(dst[:, 0:256], t1, t2, ALU.subtract)
                        dve.drain()
                        TT(t1, a, s1_, ALU.mult)
                        TT(t2, b, c_, ALU.mult)
                        dve.drain()
                        return TT(dst[:, 256:512], t1, t2, ALU.add)

                    def gate(n):
                        dve.wait_ge(S["ret_tanh"], i * 4 + (4 * first + n + 1))
                        STT(out=sg_r[:, n], in0=th_r[:, T * (n % 2):T * (n % 2) + T], scalar=1.0, in1=sg_r[:, n],
                            op0=ALU.add, op1=ALU.mult)

                    for j in range(12):
                        split(name, i, j)
                        if j == 2:
                            rotate(rq, q_r)
                            dve.drain()
                        if j == 4:
                            rotate(rq, k_r).then_inc(S["ret_qk"], 1)
                        if j in (6, 7):
                            dve.wait_ge(S["ret_vt"], i * 4 + (4 * first + j - 5))
                        if j == 7:
                            dve.wait_ge(S["ret_scores"], i * 1 + (first + 1))
                            dve.wait_ge(S["decay_loaded"], i * 16 + 16 * (first + 1))
                            TT(sd, mx[:, 0, 0:384], dec, ALU.mult).then_inc(S["decay_used"], 1)
                        if j >= 9:
                            gate(j - 9)
                        if j == 11:
                            dve.wait_ge(S["ret_mean"], i * 1 + (first + 1))
                            TS(vt_r[:, 0:256], mx[:, 5, 0:256], 1.0 / 512, None, ALU.mult)
                            dve.drain()
                            TT(o_r, o_r, vt_r[:, 0:256].unsqueeze(1).to_broadcast([P, 4, 256]),
                               ALU.subtract).then_inc(S["ret_centred"], 1)
                        dst = (rq[:, 0:256], rq[:, 256:512], rq[:, 0:256], rq[:, 256:512],
                               vt_r[:, 0:256], vt_r[:, 256:512], vt_r[:, 0:256], vt_r[:, 256:512],
                               sg_r[:, 0], sg_r[:, 1], sg_r[:, 2], sg_r[:, 3])[j]
                        evac(name, i, j, dst)
                    inverse_rms(i * 1 + (NORM[name] + 1), 5, 512, vt_r[:, 0:256], vt_r[:, 256:512],
                                rq[:, 0:256], rq[:, 256:512])
                    gate(3)
                    g0 = VEC["gn_gain"][0] + 4 * first
                    for n in range(4):
                        STT(out=o_r[:, n], in0=o_r[:, n], scalar=vec[:, bass.ds(i * 4 + (g0 + n), 1)],
                            in1=rq[:, 256:512], op0=ALU.mult, op1=ALU.mult)
                    dve.drain()
                    STT(out=o_r, in0=o_r, scalar=0.5, in1=sg_r, op0=ALU.mult, op1=ALU.mult)
                    yy = ys[:, bass.ds(i * 4, 4)]
                    hi_lo((yy[:, :, 0], yy[:, :, 1]), o_r).then_inc(S["y_ret"], 1)
                run(dve, name, body)

            for ph, first in (("ret_a", 0), ("ret_b", 4)):
                if ph in live:
                    dve.wait_ge(S["ret_tab_loaded"], 16 if first == 0 else 32)
                    ret_body(ph, first)
                    residual("ret_out" + ph[3:], 1)
            if "up0" in live:
                boundary("b_mlp", 2, "norm2_2")
            for b in range(FF_BLOCKS):
                if f"up{b}" in live:
                    def up_body(i):
                        for j in range(4):
                            split(f"up{b}", i, j)
                            evac(f"up{b}", i, j, up_t[j % 2])
                            dve.drain()
                            STT(out=up_t[2 + j % 2], in0=up_t[j % 2], scalar=0.0, in1=up_t[j % 2], op0=ALU.max,
                                op1=ALU.mult)
                            yy = ys[:, i * 4 + j]
                            hi_lo((yy[:, 0], yy[:, 1]), up_t[2 + j % 2]).then_inc(S["y_up"], 1)
                    run(dve, f"up{b}", up_body)
                    residual(f"down{b}", 1)
            if debug is None:
                inverse_rms(NORM["b_out"] + 1, 0, D, nv, ny, nt, rstd)
                for k in range(16):
                    ins = STT(out=xT[:, k], in0=xT[:, k], scalar=V("final_2", k), in1=rstd, op0=ALU.mult, op1=ALU.mult)
                ins.then_inc(S["fin_ready"], 1)
        @block.tensor
        def _(pe):
            mm = nc.tensor.matmul

            def panel(name, i, j, pieces):
                c, O = panels(name, i), outputs(name, i)
                s = c.slot(j, 2)
                pe.wait_ge(split_ready, c(j, 1))
                fresh = True
                for o, moving, at, opens, closes, weight in pieces:
                    k = O.slot(o, NB)
                    if opens:
                        pe.wait_ge(evacuated, O(o, 1))
                    for t, m in enumerate(moving):
                        ins = mm(pj[:, k], w_hi[:, s, at + t], m, start=opens and t == 0, stop=False)
                        if fresh:
                            ins.then_inc(panel_started, 1)
                            fresh = False
                        ins = mm(pj[:, k, 0:T], w_lo[:, s, at + t], m[:, 0], start=False,
                                 stop=closes and t == len(moving) - 1)
                    if closes:
                        ins.then_inc(output_ready, weight)

            def tiles(src, a, b):
                return [src[:, k] for k in range(a, b)]

            def whole(name, i, j, src, o=None):
                panel(name, i, j, [(j if o is None else o, tiles(src, 0, 16), 0, True, True, 1)])

            def transpose_to(dst, src):
                return nc.tensor.transpose(dst, src, ident)

            pe.nop().then_inc(panel_started, 1)
            pe.wait_ge(S["tables"], 48)
            pe.wait_ge(S["mem_scaled"], 1)
            for g in range(24):
                if g == 8:
                    pe.wait_ge(S["x_rows"], 16)
                if g == 16:
                    pe.wait_ge(S["x_scaled"], 1)
                if g >= 6:
                    pe.wait_ge(S["part_taken"], 2 * (g - 6) + 2)
                src = mem_rows if g < 8 else rows
                for u in range(2):
                    for r in range(2):
                        c = 2 * (g % 8) + u
                        ins = transpose_to(mx[:, g % 6, T * u + 128 * r:T * u + 128 * r + 128],
                                           src[:, r, 128 * c:128 * c + 128])
                ins.then_inc(S["transposed"], 1)

            def mem_body(i):
                O = outputs("mem", i)

                def value_rows(n):
                    pe.wait_ge(evacuated, O(4 + n, 1 + NB))
                    for m in range(2):
                        ins = transpose_to(mx[:, n, 128 * m:128 * m + 128], vt[n % 2][:, 128 * m:128 * m + 128])
                    ins.then_inc(S["v_rows"], 1)
                for j in range(8):
                    whole("mem", i, j, ys)
                    if j >= 5:
                        value_rows(j - 5)
                value_rows(3)
            pe.wait_ge(S["part_taken"], 48)
            run(pe, "mem", mem_body)

            def gate_body(i):
                for j in range(4):
                    whole("gate", i, j, hs)
            run(pe, "gate", gate_body)

            for r in range(2):
                for k in range(16):
                    for part in range(2):
                        ins = mm(mx[:, 0, 32 * r:32 * r + 32],
                                 hs[:, k, part, 128 * r:128 * r + 128].bitcast(F32), wdt[:, k],
                                 start=k == 0 and part == 0, stop=k == 15 and part == 1)
            ins.then_inc(S["dt_logits"], 1)

            def gate_out_body(i):
                for j in range(4):
                    panel("gate_out", i, j, [(2 * j + u, tiles(ys, 0, 8), 8 * u, True, True, 1) for u in range(2)])
            pe.wait_ge(S["y_gate"], 8)
            run(pe, "gate_out", gate_out_body)
            pe.wait_ge(S["dt_ready"], 1)
            mm(mx[:, 1, 0:32], after, da[:, 0], start=True, stop=True).then_inc(S["dte_logits"], 1)

            def residual(name, ppo, src):
                def body(i):
                    for j in range(len(PHASES[name][0])):
                        n = PHASES[name][0][j]
                        a = (j % ppo) * n
                        panel(name, i, j, [(j // ppo, tiles(src, a, a + n), 0, j % ppo == 0, j % ppo == ppo - 1, 1)])
                run(pe, name, body)

            def square_sum():
                pe.wait_ge(S["acc_ready"], square_sum.n)
                square_sum.n += 1
                mm(mx[:, 0, 0:T], ones, acc, start=True, stop=True).then_inc(S["stat_ready"], 1)

            def mem_scores(q_, key_, bank):
                for q in range(2):
                    ins = mm(mx[:, bank, T * q:T * q + T], q_[:, 128 * q:128 * q + 128], key_, start=True, stop=True)
                ins.then_inc(S["mem_scores"], 1)

            def mem_pt(probs, bank):
                for k in range(2):
                    for q in range(2):
                        ins = transpose_to(mx[:, bank, T * k + 128 * q:T * k + 128 * q + 128],
                                           probs[:, T * q + 128 * k:T * q + 128 * k + 128])
                ins.then_inc(S["mem_pt"], 1)

            def mem_pv(vh, pt, bank):
                for k in range(2):
                    ins = mm(mx[:, bank, 0:T], vh[:, 128 * k:128 * k + 128], pt[:, T * k:T * k + T], start=k == 0,
                             stop=k == 1)
                ins.then_inc(S["mem_pv"], 1)

            def ssd_body(i):
                O = outputs("ssd", i)
                M = Count(0, 1, i)

                def seg(r):
                    pe.wait_ge(S["seg_rhs"], i * 4 + r + 1)
                    if r >= 2:
                        pe.wait_ge(S["decay_ready"], i * 4 + r - 1)
                    mm(mx[:, 1 + r % 2], after, rr[r % 2], start=True, stop=True).then_inc(S["seg_ready"], 1)

                def ydiag(r):
                    pe.wait_ge(S["mix_ready"], i * 4 + r + 1)
                    for h in range(4):
                        hh = 4 * (r % 2) + h
                        ins = mm(mx[64 * (h % 2):64 * (h % 2) + 64, 3 + r // 2, 128 * (hh // 2):128 * (hh // 2) + 128],
                                 xdt[r // 2][:, 64 * hh:64 * hh + 64], em[r % 2][:, 128 * h:128 * h + 128],
                                 start=True, stop=True)
                    ins.then_inc(S["ydiag_ready"], 1)

                for j in range(12):
                    whole("ssd", i, j, hs)
                    if j == 4:
                        pe.wait_ge(S["bc_ready"], i * 1 + 1)
                        for c in range(2):
                            mm(mx[:, 0, 128 * c:128 * c + 128], bT[:, 128 * c:128 * c + 128],
                               cT[:, 128 * c:128 * c + 128], start=True, stop=True)
                        transpose_to(mx[:, 0, 256:384], bT[:, 0:128]).then_inc(S["cb_ready"], 1)
                    if j == 5:
                        seg(0)
                    if j == 6:
                        seg(1)
                    if j == 7:
                        pe.wait_ge(S["xs_ready"], i * 1 + 1)
                        pe.wait_ge(S["cb_taken"], i * 1 + 1)
                        pe.wait_ge(S["brow_ready"], i * 1 + 1)
                        for c, bank in ((0, 5), (1, 0)):
                            for n in range(4):
                                ins = transpose_to(mx[:, bank, 128 * n:128 * n + 128],
                                                   xs[:, n, 128 * c:128 * c + 128])
                        ins.then_inc(S["xs_rows"], 1)
                    if j == 8:
                        seg(2)
                        pe.wait_ge(S["xdt_ready"], i * 1 + 1)
                        ydiag(0)
                        ydiag(1)
                        mm(mx[:, 5], brow, xdte, start=True, stop=True).then_inc(S["state_ready"], 1)
                    if j == 9:
                        seg(3)
                        ydiag(2)
                        pe.wait_ge(evacuated, O(6, 1 + NB))
                        mem_scores(cv0, keys[:, i], 1)
                    if j == 10:
                        ydiag(3)
                        pe.wait_ge(S["state_copied"], i * 1 + 1)
                        for n in range(4):
                            ins = mm(mx[:, 0, 128 * n:128 * n + 128], state[:, 128 * n:128 * n + 128], cT[:, 128:256],
                                     start=True, stop=True)
                        ins.then_inc(S["yoff_ready"], 1)
                        pe.wait_ge(S["mem_scaled_probs"], M(0, 1))
                        mem_pt(em0, 5)
                    if j == 11:
                        pe.wait_ge(S["eq_lhs"], i * 1 + 1)
                        for n in range(4):
                            ins = mm(mx[:, 2, 128 * n:128 * n + 128], r0[:, 128 * n:128 * n + 128], upto, start=True,
                                     stop=True)
                        ins.then_inc(S["eq_logits"], 1)
                        pe.wait_ge(S["mem_pt_copied"], M(0, 1))
                        mem_pv(th1, r1, 1)
                pe.wait_ge(S["ssd_squares"], i * 1 + 1)
                for n in range(4):
                    ins = mm(mx[:, 5, 0:T], ones, ssq[:, n], start=n == 0, stop=n == 3)
                ins.then_inc(S["stat_ready"], 1)
            if "ssd" in live:
                pe.wait_ge(S["dte_ready"], 1)
                run(pe, "ssd", ssd_body)
            square_sum.n = 1
            if "out0" in live:
                pe.wait_ge(S["y_ssd"], 4)
                residual("out0", 2, ys)
            if "latent" in live:
                square_sum()
                pe.wait_ge(S["h_ready"], 4)

                def latent_body(i):
                    for j in range(4):
                        whole("latent", i, j, hs)
                run(pe, "latent", latent_body)
                for j in range(3):
                    whole("latent_tail", 0, j, hs)

                def memq_body(i):
                    O = outputs("memq", i)
                    M = Count(4, 2, i)
                    for j in range(4):
                        whole("memq", i, j, hs)
                        if j == 2:
                            pe.wait_ge(evacuated, O(1, 1 + NB))
                            for u in range(2):
                                mem_scores(mq_m[:, T * u:T * u + T], keys[:, i * 2 + u], u)
                    for u in range(2):
                        pe.wait_ge(S["mem_scaled_probs"], M(u, 1))
                        mem_pt(p_m[:, 512 * u:512 * u + 512], 2 + u)
                    for u in range(2):
                        pe.wait_ge(S["mem_pt_copied"], M(u, 1))
                        mem_pv(vh_m[:, T * u:T * u + T], pt_m[:, 512 * u:512 * u + 512], 4 + u)
                pe.wait_ge(S["kv_loaded"], 16)
                run(pe, "memq", memq_body)
                pe.wait_ge(S["latent_squares"], 1)
                for k, (a, b) in enumerate(((0, 4), (4, 10))):
                    for c in range(a, b):
                        ins = mm(mx[:, k, 0:T], ones, lsq[:, c], start=c == a, stop=c == b - 1)
                    ins.then_inc(S["stat_ready"], 1)
            if "mla" in live:
                def mla_body(i):
                    O = outputs("mla", i)
                    kv_t, q_t = tiles(lat, 0, 4), tiles(lat, 4, 10)
                    for j in range(8):
                        panel("mla", i, j, (
                            [(0, q_t, 0, True, True, 1)], [(1, q_t, 0, True, True, 1)], [(2, q_t, 0, True, True, 1)],
                            [(3, kv_t, 0, True, True, 1), (4, kv_t, 4, True, True, 1)],
                            [(5, kv_t, 0, True, True, 1)], [(6, kv_t, 0, True, True, 1)],
                            [(7, tiles(hs, 0, 16), 0, True, True, 1)], [(8, tiles(hs, 0, 16), 0, True, True, 2)])[j])
                        if j == 4:
                            pe.wait_ge(S["qk_ready"], i * 1 + 1)
                            for u, kr_ in enumerate((krA, krB)):
                                for q, a, n in ((0, 0, 128), (1, 128, 256)):
                                    dst = mx[:, u, a:a + n]
                                    mm(dst, qn[u][:, 128 * q:128 * q + 128], kn[u][:, 0:n], start=True, stop=False)
                                    ins = mm(dst, qr[:, 128 * q:128 * q + 128], kr_[:, 0:n], start=False, stop=True)
                            ins.then_inc(S["mla_scores"], 1)
                        if j in (5, 6):
                            u = j - 5
                            pe.wait_ge(evacuated, O(5 + u, 1 + NB))
                            for k in range(2):
                                ins = transpose_to(mx[:, 2, T * u + 128 * k:T * u + 128 * k + 128],
                                                   vtm[u][:, 128 * k:128 * k + 128])
                            if u == 1:
                                ins.then_inc(S["mla_vt"], 1)
                        if j == 6:
                            pe.wait_ge(S["mla_probs_scaled"], i * 1 + 1)
                            for u in range(2):
                                for a in (0, 128, 256):
                                    ins = transpose_to(mx[:, 3 + u, a:a + 128], s_[:, 384 * u + a:384 * u + a + 128])
                            ins.then_inc(S["mla_pt"], 1)
                    pe.wait_ge(S["mla_vrow"], i * 1 + 1)
                    pe.wait_ge(S["mla_pt_copied"], i * 1 + 1)
                    for u in range(2):
                        mm(mx[:, 5, T * u:T * u + T], vrow_[:, T * u:T * u + 128], pt_[:, 384 * u:384 * u + 256],
                           start=True, stop=False)
                        ins = mm(mx[:, 5, T * u + 128:T * u + 256], vrow_[:, T * u + 128:T * u + 256],
                                 pt_[:, 384 * u + 256:384 * u + 384], start=False, stop=True)
                    ins.then_inc(S["mla_pv"], 1)
                pe.wait_ge(S["lat_ready"], 2)
                pe.wait_ge(S["krope_ready"], 1)
                run(pe, "mla", mla_body)
            if "out1" in live:
                pe.wait_ge(S["y_mla"], 8)
                residual("out1", 2, ys)
            if "ret_a" in live:
                square_sum()
                square_sum()
                pe.wait_ge(S["h_ready"], 8)

            def ret_body(name, first):
                def body(i):
                    O = outputs(name, i)
                    for j in range(12):
                        whole(name, i, j, hs)
                        if 5 <= j <= 8:
                            n = j - 5
                            pe.wait_ge(evacuated, O(4 + n, 1 + NB))
                            if n >= 2:
                                pe.wait_ge(S["ret_vrow"], i * 4 + (4 * first + n - 1))
                            for k in range(2):
                                ins = transpose_to(mx[:, 1 + n % 2, 128 * k:128 * k + 128],
                                                   vt_r[:, T * (n % 2) + 128 * k:T * (n % 2) + 128 * k + 128])
                            ins.then_inc(S["ret_vt"], 1)
                        if j == 6:
                            pe.wait_ge(S["ret_qk"], i * 1 + (first + 1))
                            for k, a, n in ((0, 0, 256), (1, 256, 128)):
                                for d in range(2):
                                    ins = mm(mx[:, 0, a:a + n], k_r[:, T * d + 128 * k:T * d + 128 * k + 128],
                                             q_r[:, T * d + T - n:T * d + T], start=d == 0, stop=d == 1)
                            ins.then_inc(S["ret_scores"], 1)
                        if j == 9:
                            pe.wait_ge(S["ret_vrow"], i * 4 + (4 * first + 4))
                            pe.wait_ge(S["decay_used"], i * 1 + (first + 1))
                            for n in range(4):
                                dst = mx[:, 3 + n // 2, T * (n % 2):T * (n % 2) + T]
                                mm(dst, vrow_r[:, 0, 128 * n:128 * n + 128], sd[:, 0:256], start=True, stop=False)
                                ins = mm(dst[:, 128:256], vrow_r[:, 1, 128 * n:128 * n + 128], sd[:, 256:384],
                                         start=False, stop=True)
                            ins.then_inc(S["ret_pv"], 1)
                        if j == 10:
                            pe.wait_ge(S["ret_o"], i * 1 + (first + 1))
                            for n in range(4):
                                ins = mm(mx[:, 5, 0:T], ones, o_r[:, n], start=n == 0, stop=n == 3)
                            ins.then_inc(S["ret_mean"], 1)
                    pe.wait_ge(S["ret_squares"], i * 1 + (first + 1))
                    for n in range(4):
                        ins = mm(mx[:, 5, 0:T], ones, sq_r[:, n], start=n == 0, stop=n == 3)
                    ins.then_inc(S["stat_ready"], 1)
                run(pe, name, body)

            for ph, first in (("ret_a", 0), ("ret_b", 4)):
                if ph in live:
                    ret_body(ph, first)
                    pe.wait_ge(S["y_ret"], first + 4)
                    residual("ret_out" + ph[3:], 1, ys)
            for b in range(FF_BLOCKS):
                if f"up{b}" in live:
                    if b == 0:
                        square_sum.n += 1
                        square_sum()
                        pe.wait_ge(S["h_ready"], 12)

                    def up_body(i):
                        for j in range(4):
                            whole(f"up{b}", i, j, hs)
                    run(pe, f"up{b}", up_body)
                    pe.wait_ge(S["y_up"], 16 * b + 16)
                    residual(f"down{b}", 1, ys)
            if debug is None:
                square_sum.n += FF_BLOCKS - 1
                square_sum()
                pe.wait_ge(S["fin_ready"], 1)
                for g in range(8):
                    if g >= 6:
                        pe.wait_ge(S["fin_taken"], g - 5)
                    for u in range(4):
                        c = 4 * (g % 4) + u
                        ins = transpose_to(mx[:, g % 6, 128 * u:128 * u + 128],
                                           xT[:, c, 128 * (g // 4):128 * (g // 4) + 128])
                    ins.then_inc(S["fin_rows"], 1)


def _tiles(w, rows, cols):
    return [w[128 * r:128 * r + 128, c:c + 128] for c in cols for r in rows]


def _stream(name, inp):
    w_in0, w_out0, w_in1, w_out1 = inp["w_in0"], inp["w_out0"], inp["w_in1"], inp["w_out1"]
    n = PHASES[name][1]
    k16 = range(16)
    its = []
    ret_in, ret_out = inp["ret_w_in_2"][0], inp["ret_w_out_2"][0]
    up, down = inp["mlp_w_up_2"][0], inp["mlp_w_down_2"][0]
    for i in range(n):
        if name == "mem":
            cols = range(0, 512, 128)
            its.append(_tiles(inp[f"mem_k{1 - i}"], k16, cols) + _tiles(inp[f"mem_v{1 - i}"], k16, cols))
        elif name == "gate":
            its.append(_tiles(w_in0, k16, [s * 1024 + 128 * i for s in (3, 1, 2, 0)]))
        elif name == "gate_out":
            its.append(_tiles(w_out0, range(8), range(1024 * i, 1024 * i + 1024, 128)))
        elif name == "ssd":
            xbc = 4096 + 2048
            its.append(_tiles(w_in0, k16, [xbc + 2048 + 128 * i, xbc + 2560 + 128 * i]
                              + [xbc + 512 * i + 128 * t for t in range(4)]
                              + [9248 + 128 * i, 9760 + 128 * i]
                              + [4096 + 512 * i + 128 * t for t in range(4)]))
        elif name == "out0":
            its.append(_tiles(w_out0, list(range(24, 28)) + list(range(8, 24)), range(512 * i, 512 * i + 512, 128)))
        elif name == "latent":
            its.append(_tiles(w_in1, k16, [(768 if i == 0 else 0) + 128 * t for t in range(4)]))
        elif name == "latent_tail":
            kr = np.concatenate([w_in1[:, 1280:1344]] * 2, axis=1)
            its.append(_tiles(w_in1, k16, [512, 640]) + _tiles(kr, k16, [0]))
        elif name == "memq":
            its.append(_tiles(w_in1, k16, [3392 + 256 * i, 3520 + 256 * i, 3904 + 256 * i, 4032 + 256 * i]))
        elif name == "mla":
            uq, ukv = inp["mla_w_uq"], inp["mla_w_ukv"]
            qc, kc = 384 * i, 512 * i
            qr = np.concatenate([uq[:, qc + 128:qc + 192], uq[:, qc + 320:qc + 384]], axis=1)
            its.append(_tiles(uq, range(6), [qc, qc + 192]) + _tiles(qr, range(6), [0])
                       + _tiles(ukv, range(4), [kc, kc + 256, kc + 128, kc + 384])
                       + _tiles(w_in1, k16, [1344 + 256 * i, 1472 + 256 * i]))
        elif name == "out1":
            its.append(_tiles(w_out1, list(range(16, 20)) + list(range(16)), range(512 * i, 512 * i + 512, 128)))
        elif name in ("ret_a", "ret_b"):
            h = i + (4 if name == "ret_b" else 0)
            its.append(_tiles(ret_in, k16, [256 * h, 256 * h + 128, 2048 + 256 * h, 2176 + 256 * h]
                              + [4096 + 512 * h + 128 * t for t in range(4)]
                              + [8192 + 512 * h + 128 * t for t in range(4)]))
        elif name in ("ret_out_a", "ret_out_b"):
            r = 16 if name == "ret_out_b" else 0
            its.append(_tiles(ret_out, range(r, r + 16), range(512 * i, 512 * i + 512, 128)))
        elif name.startswith("up"):
            b = int(name[2:])
            its.append(_tiles(up, k16, [2048 * b + 512 * i + 128 * t for t in range(4)]))
        else:
            b = int(name[4:])
            its.append(_tiles(down, range(16 * b, 16 * b + 16), range(512 * i, 512 * i + 512, 128)))
    out = np.empty((n, P, sum(PHASES[name][0]) * 128), np.float32)
    for i, parts in enumerate(its):
        for t, w in enumerate(parts):
            out[i, :, 128 * t:128 * t + 128] = w
    return out


def _columns(v):
    return np.asarray(v).reshape(-1, P).T


def _vectors(inp):
    out = np.zeros((P, NVEC), np.float32)

    def put(name, cols):
        a, b = VEC[name]
        out[:, a:b] = cols
    for name, src in (("mem_norm", "mem_norm_w"), ("norm0", "norm0_w"), ("norm1", "norm1_w"), ("final", "final_norm_w"),
                      ("norm1_2", "norm1_2"), ("norm2_2", "norm2_2"), ("final_2", "final_norm_2"),
                      ("q_norm", "mla_q_norm_w"), ("kv_norm", "mla_kv_norm_w"), ("gn_gain", "ret_gn_gain_2"),
                      ("ssd_norm", "ssd_norm_w")):
        put(name, _columns(inp[src].reshape(-1)))
    gate = inp["sc_conv_w"]
    put("gate_conv", np.stack([_columns(gate[k]) for k in range(3)], axis=2).reshape(P, 24))
    taps = np.stack([_columns(inp["ssd_conv_w"][k]) for k in range(4)] + [_columns(inp["ssd_conv_b"])], axis=2)
    groups = [[16 + g, 20 + g] + [4 * g + t for t in range(4)] for g in range(GROUPS)]
    put("ssd_conv", np.concatenate([taps[:, t].reshape(P, 5) for g in groups for t in g], axis=1))
    put("ssd_d", _columns(np.repeat(inp["ssd_d"], 64)))
    put("dt_bias", np.broadcast_to(inp["ssd_dt_bias"], (P, 32)))
    put("a_log", np.broadcast_to(inp["ssd_a_log"], (P, 32)))
    inv = (10000.0 ** (-np.arange(32, dtype=np.float32) / np.float32(32))).astype(np.float32)
    put("inv_freq", np.tile(inv, 4)[:, None])
    put("sin_sign", np.where(np.arange(P) % 64 < 32, 1.0, -1.0)[:, None])
    return out


def _constants():
    k, q = np.arange(P)[:, None], np.arange(P)[None, :]
    con = np.zeros((P, NCONST), np.float32)
    for name, m in (("ident", k == q), ("ones", k == k), ("upto", k <= q), ("after", k > q)):
        con[:, CONST[name][0]:CONST[name][1]] = m
    causal = np.where(q <= k, 0.0, -1e30).astype(np.float32)
    mask = np.concatenate([causal, np.zeros((P, 128), np.float32), causal], axis=1)
    half_ = np.arange(0, 256, 2, dtype=np.float32)
    inv = (np.float32(10000.0) ** (-half_ / np.float32(256))).astype(np.float32)
    ang = (inv[:, None] * np.arange(T, dtype=np.float32)[None]).astype(np.float32).astype(np.float64)
    tab = np.concatenate([np.cos(ang), np.sin(ang)], axis=1).astype(np.float32)
    tk, tq = np.arange(T)[:, None], np.arange(T)[None]
    dist = np.where(tk // 64 == tq // 64, np.abs(tq - tk), tq - tk)
    seen = tk // 64 <= tq // 64
    decay = np.zeros((RET_HEADS, P, 384), np.float32)
    for h in range(RET_HEADS):
        full = np.where(seen, (1.0 - 2.0 ** (-5.0 - h)) ** dist, 0.0) / 16.0
        decay[h] = np.concatenate([full[:128], full[128:, 128:]], axis=1)
    return con, mask, tab, decay


def kernel(**inputs):
    import concourse.bacc as _bacc
    from concourse.bass_utils import run_bass_kernel_spmd as _run

    inp = {k: np.asarray(v) for k, v in inputs.items()}
    con, mask, tab, decay = _constants()
    w_dt = np.stack([inp["w_in0"][128 * k:128 * k + 128, 9216:9248] for k in range(16)], axis=1)
    arrays = {f"w_{name}": _stream(name, inp) for name in ORDER}
    arrays |= {"w_dt": w_dt, "vecs": _vectors(inp), "consts": con, "mla_mask": mask, "ret_tab": tab,
               "ret_decay": decay, "pos": np.ascontiguousarray(np.broadcast_to(inp["positions"], (P, T))),
               "x": inp["x"], "mem": inp["mem"]}
    nc = _bacc.Bacc("TRN2", target_bir_lowering=False, num_devices=1)
    arrays = {f"in_{k}": np.ascontiguousarray(v) for k, v in arrays.items()}
    aps = {k[3:]: nc.dram_tensor(k, v.shape, mybir.dt.from_np(v.dtype), kind="ExternalInput").ap()
           for k, v in arrays.items()}
    out = nc.dram_tensor("out_y", (1, T, D), F32, kind="ExternalOutput").ap()
    streams = {name: aps.pop(f"w_{name}") for name in ORDER}
    build(nc, streams, out=out, **aps)
    r = _run(nc, [arrays], core_ids=[0])
    return r.results[0]["out_y"]
```

```python
from contextlib import ExitStack

import numpy as np
import concourse.bass as bass
from concourse import mybir

P = 128
T = 256
D = 2048
KT = D // P
EPS = 1e-6
HALF = 8
F32 = mybir.dt.float32
F32R = mybir.dt.float32r
I32 = mybir.dt.int32
ALU = mybir.AluOpType
ACT = mybir.ActivationFunctionType
AX = mybir.AxisListType

GROUPS = 4
SSD_HEADS = 32
MEM_SCALE = 128 ** -0.5
MLA_SCALE = 192 ** -0.5
RET_HEADS = 8
FF_BLOCKS = 4

PHASES = {
    "mem": ([16] * 8, 2),
    "gate": ([16] * 4, 8),
    "gate_out": ([16] * 4, 2),
    "ssd": ([16] * 12, 4),
    "out0": ([10] * 8, 4),
    "latent": ([16] * 4, 2),
    "latent_tail": ([16] * 3, 1),
    "memq": ([16] * 4, 2),
    "mla": ([6, 6, 6, 8, 4, 4, 16, 16], 8),
    "out1": ([10] * 8, 4),
    "ret_a": ([16] * 12, 4),
    "ret_out_a": ([16] * 4, 4),
    "ret_b": ([16] * 12, 4),
    "ret_out_b": ([16] * 4, 4),
}
for _b in range(FF_BLOCKS):
    PHASES[f"up{_b}"] = ([16] * 4, 4)
    PHASES[f"down{_b}"] = ([16] * 4, 4)
ORDER = list(PHASES)

VEC = {}
_at = 0
for _name, _n in (("mem_norm", 16), ("norm0", 16), ("norm1", 16), ("final", 16), ("norm1_2", 16), ("norm2_2", 16),
                  ("final_2", 16), ("final_norm1_2", 16), ("q_norm", 6), ("kv_norm", 4), ("gn_gain", 32), ("gate_conv", 24),
                  ("ssd_conv", GROUPS * 30), ("ssd_d", 16), ("ssd_norm", 16), ("dt_bias", 32), ("a_log", 32),
                  ("inv_freq", 1), ("sin_sign", 1)):
    VEC[_name] = (_at, _at + _n)
    _at += _n
NVEC = _at

CONST = {}
_at = 0
for _name, _n in (("ident", 128), ("ones", 128), ("upto", 128), ("after", 128)):
    CONST[_name] = (_at, _at + _n)
    _at += _n
NCONST = _at


class Count:

    def __init__(self, first, per=0, i=0):
        self.first, self.per, self.i = first, per, i

    def __call__(self, j, lead=0):
        return self.i * self.per + (self.first + j + lead)

    def slot(self, j, n):
        assert self.per % n == 0
        return (self.first + j) % n

    def half(self, j, h, lead=0):
        return self.i * (2 * self.per) + (2 * (self.first + j) + h + 1 + lead)

    def filled(self, j):
        assert self.per % 4 == 0
        return self.i * (self.per * 4) + 16 * ((self.first + j) // 4 + 1)


def build(nc, streams, w_dt, vecs, consts, mla_mask, ret_tab, ret_decay, pos, x, mem, out, debug=None, stop=None):
    ctx = ExitStack()
    with ctx:
        def sb(name, shape, dt=F32):
            return ctx.enter_context(nc.sbuf_tensor(name, shape, dt))

        def sem(name):
            return ctx.enter_context(nc.semaphore(name))

        NB = 2
        raw = sb("raw", [P, 4, 16, 128])
        w_hi = sb("w_hi", [P, 4, 8, 128], F32R)
        w_lo = sb("w_lo", [P, 4, 8, 128], F32R)
        hs = sb("hs", [P, 16, 2, T], F32R)
        ys = sb("ys", [P, 20, 2, T], F32R)
        lat = sb("lat", [P, 10, 2, T], F32R)
        xT = sb("xT", [P, 16, T])
        kv = sb("kv", [P, 2048])
        half = sb("half", [P, NB, T])
        wdt = sb("wdt", [P, 16, 32])
        small = sb("small", [P, 224])
        vec = sb("vec", [P, NVEC])
        con = sb("con", [P, NCONST])
        GEN = 4610
        gen = sb("gen", [P, GEN])
        pj = ctx.enter_context(nc.psum_tensor("pj", [P, 2, 512], F32))
        mx = ctx.enter_context(nc.psum_tensor("mx", [P, 6, 512], F32))
        kv_spill = nc.dram_tensor("kv_spill", [2, P, 2048], F32).ap()
        x_spill = nc.dram_tensor("x_spill", [P, 16 * T], F32).ap()

        ident, ones, upto, after = (con[:, CONST[n][0]:CONST[n][1]] for n in ("ident", "ones", "upto", "after"))
        keys = kv[:, 0:1024].rearrange("p (n t) -> p n t", n=4)
        values = kv[:, 1024:2048].rearrange("p (m c) -> p m c", m=2)
        xflat = xT[:].rearrange("p a b -> p (a b)")

        def V(name, k=0):
            a = VEC[name][0] + k
            return vec[:, a:a + 1]

        def carve(start, sizes):
            views, at = [], start
            for n in sizes:
                if at < GEN and at + n > GEN:
                    at = GEN
                views.append(gen[:, at:at + n] if at + n <= GEN else xflat[:, at - GEN:at - GEN + n])
                at += n
            assert at <= GEN + 16 * T, at
            return views

        outs_per = {"gate_out": 8, "out0": 4, "out1": 4, "ret_out_a": 4, "ret_out_b": 4, "mla": 10}
        first_panel, first_out = {}, {}
        p0 = o0 = 0
        for name in ORDER:
            first_panel[name], first_out[name] = p0, o0
            sizes, n = PHASES[name]
            p0 += len(sizes) * n
            o0 += outs_per.get(name, len(sizes)) * n

        def panels(name, i=0):
            return Count(first_panel[name], len(PHASES[name][0]) if PHASES[name][1] > 1 else 0, i)

        def outputs(name, i=0):
            return Count(first_out[name], outs_per.get(name, len(PHASES[name][0])) if PHASES[name][1] > 1 else 0, i)

        def size_ahead(name, j, ahead):
            sizes, n = PHASES[name]
            if j + ahead < len(sizes):
                return sizes[j + ahead]
            j, k = j + ahead - len(sizes), ORDER.index(name) + 1
            return max(sizes[j] if n > 1 else 0, PHASES[ORDER[k]][0][j] if k < len(ORDER) else 0)

        def part(name, i, j, h):
            ahead = 2 - h
            c, n = panels(name, i), size_ahead(name, j, ahead)
            if isinstance(i, int) and c(j, ahead) >= total_live:
                return None
            k = cut((j + ahead) % len(PHASES[name][0]), n)
            return c, j + ahead, 2 * c.slot(j + ahead, 2) + h, k if h else 0, max(n, k + 1) if h else min(n, k)

        def cut(j, n):
            return n // 2 if j >= 2 and n <= HALF else HALF

        loaded = [sem(f"weights_loaded{s}") for s in range(4)]
        hi_ready = sem("weights_hi_ready")
        split_ready = sem("weights_split_ready")
        half_started = sem("half_started")
        output_ready = sem("output_ready")
        half_copied = sem("half_copied")
        evacuated = sem("evacuated")

        names = """mem_rows x_rows tables mem_squares mem_var mem_rsqrt mem_scaled x_squares x_var x_rsqrt x_scaled
            transposed part_hi part_taken v_rows v_rows_taken kv_spilled kv_free kv_loaded
            gate_tanh y_gate dt_logits dt_exp_in dt_exp dt_ready dte_logits dte_ready
            x_tile x_square x_spilled x_loaded acc_ready stat_ready var_ready rsqrt_ready h_f32 h_hi h_ready
            conv_done conv_tanh bc_ready cb_ready cb_taken brow_ready seg_rhs seg_ready decay_ready mix_ready ydiag_ready
            xs_ready xs_rows xdt_ready state_ready state_copied yoff_ready eq_lhs eq_logits eq_ready
            z_tanh mz_tanh ssd_gated ssd_squares y_ssd
            mem_scores mem_shift mem_probs mem_scaled_probs mem_pt mem_pt_copied mem_values mem_pv y_mem
            pos_loaded angle_ready sin_ready mask_loaded latent_ready latent_squares lat_ready krope_ready
            qk_ready mla_vt mla_vrow mla_scores mla_shift mla_probs mla_probs_scaled mla_pt mla_pt_copied mla_pv mla_tanh y_mla
            ret_tab_loaded decay_loaded decay_used ret_qk ret_vt ret_vrow ret_scores ret_mixed ret_pv ret_o
            ret_vcent ret_squares ret_tanh y_ret y_up fin_scale fin_rows fin_act fin_dve out_done""".split()
        S = {n: sem(n) for n in names}

        block = ctx.enter_context(nc.Block())
        live = ORDER if stop is None else ORDER[:ORDER.index(stop) + 1]
        total_live = first_panel[live[-1]] + len(PHASES[live[-1]][0]) * PHASES[live[-1]][1]

        def run(engine, name, body, first=0):
            n = PHASES[name][1]
            last = n - 1 if name == live[-1] else n
            if last - first == 1:
                body(first)
            else:
                with engine.Fori(first, last) as i:
                    body(i)
            if last < n:
                body(last)

        MEMH = {"ssd": 0, "memq": 4}
        NORM = {"ssd": 0, "b_latent": 4, "kv": 5, "q": 6, "b_final": 7, "b_ret": 8, "ret_a": 9, "ret_b": 13, "b_mlp": 17,
                "b_out": 18}
        RES = ["gate_out", "out0", "out1", "ret_out_a", "ret_out_b"] + [f"down{b}" for b in range(FF_BLOCKS)]
        RES = {n: 16 * k for k, n in enumerate(RES)}
        LAST = f"down{FF_BLOCKS - 1}"
        NEXT = {"out0": ([None], "norm1"), "out1": ([None, "final"], "final_norm1_2"), "ret_out_b": ([None], "norm2_2"),
                LAST: ([None], None)}
        SQ = {n: 16 * k for k, n in enumerate(NEXT)}

        rows = gen[:, 0:4096].rearrange("p (r c) -> p r c", r=2)
        mem_rows = xflat.rearrange("p (r c) -> p r c", r=2)
        vt = [gen[:, 4096:4352], gen[:, 4352:4608]]
        z_g, c_g, v_g, b_g, th_g, u_g, a_g, e_g, s_g = carve(0, [256] * 5 + [260] + [256] * 3)
        res = carve(0, [256, 256])
        sq, acc = [carve(512, [256, 256]), carve(1536, [256, 256])], carve(1024, [256, 256])
        nv, ny, nt, rstd_sq = carve(1794, [258, 258, 258, 258])
        rstd_final, = carve(4352, [258])
        rstd = wdt[:].rearrange("p a b -> p (a b)")[:, 0:258]
        ss, var4, rs4, tmp4 = small[:, 0:4], small[:, 4:8], small[:, 8:12], small[:, 12:16]
        mstat = small[:, 16:24]
        pstat = small[:, 24:48]
        dt = small[:, 48:112].rearrange("p (c h) -> p c h", c=2)
        da = small[:, 112:176].rearrange("p (c h) -> p c h", c=2)
        dte = small[:, 176:208]
        dtw = [w.rearrange("p (c h) -> p c h", c=2) for w in carve(2600, [64] * 8)]
        ea, = carve(3200, [32])

        (cp0, cp1, cv0, cv1, th0, th1, bT, cT, r0, r1, cbm, brow, xs_) = carve(
            0, [260, 260, 256, 256, 256, 256, 256, 256, 512, 512, 256, 128, 1024])
        *em, xdt0, xdt1, sz_ = carve(GEN, [512] * 6 + [1024])
        probs_s, pt_s, mq_s, vh_s = xdt0, xdt1, xdt1[:, 0:256], sz_[:, 256:512]
        state, eqx, mo_s, xdte = r0, r1, bT, gen[:, 1032:1544]
        cp, cv, th, rr, xdt = (cp0, cp1), (cv0, cv1), (th0, th1), (r0, r1), (xdt0, xdt1)
        xs = xs_.rearrange("p (a t) -> p a t", a=4)
        sz = sz_.rearrange("p (a t) -> p a t", a=4)
        ssq = xflat[:, 2048:3072].rearrange("p (a t) -> p a t", a=4)

        cosT, sinT, krA, krB, latr = carve(0, [256, 256, 256, 256, 2560])
        lraw = latr.rearrange("p (a t) -> p a t", a=10)
        lnv, lny, lnt, lrstd = carve(3584, [256] * 4)
        mq_m, mz_m, mt_m, vh_m, p_m, pt_m = carve(GEN, [512, 512, 512, 512, 1024, 1024])
        lsq = xflat[:, 0:2560].rearrange("p (a t) -> p a t", a=10)
        qn_, kn_, vt_, vrow_, zz_, zt_, qr, qro = carve(1024, [512] * 6 + [256] + [256])
        mask, s_, pt_ = carve(GEN + 256, [384, 768, 768])
        qn, kn, vtm = ([w[:, 0:256], w[:, 256:512]] for w in (qn_, kn_, vt_))

        ang, kk_, tt_ = lnv, lny, lnt
        pos_i = lrstd.bitcast(I32)

        rq, t12, q_r, k_r, vt_r, sd, dec, cs_r, th_r = carve(0, [512, 512, 512, 512, 512, 384, 384, 512, 512])
        o_r = kv[:, 0:1024].rearrange("p (a t) -> p a t", a=4)
        vrow_r = kv[:, 1024:2048].rearrange("p (k c) -> p k c", k=2)
        sg_r = gen[:, 1024:2048].rearrange("p (a t) -> p a t", a=4)
        sq_r = gen[:, 0:1024].rearrange("p (a t) -> p a t", a=4)

        v_sum, v_mean = small[:, 208:216], small[:, 216:218]

        up_t = carve(0, [256, 256, 256, 256])

        def fin_bank(g):
            return mx[:, g] if g < 6 else pj[:, g - 6]

        @block.sync
        def _(sp):
            def load(name, i, j, reused=True):
                c = panels(name, i)
                sizes = PHASES[name][0]
                a, b = 128 * sum(sizes[:j]), 128 * sum(sizes[:j + 1])
                if reused:
                    sp.wait_ge(split_ready, c.half(j - 4, 1))
                sp.dma_start(raw[:, c.slot(j, 4), 0:sizes[j], :].rearrange("p t c -> p (t c)"),
                             streams[name][i, :, a:b]).then_inc(loaded[c.slot(j, 4)], 16)

            for name in live:
                count = len(PHASES[name][0])
                if name == "mem":
                    for j in range(count):
                        load(name, 0, j, j >= 4)
                    load_rest = 1
                else:
                    load_rest = 0
                run(sp, name, lambda i: [load(name, i, j) for j in range(count)], load_rest)
            if debug is None:
                for r in range(2):
                    sp.wait_ge(S["fin_act"], 2 * r + 2)
                    sp.wait_ge(S["fin_dve"], 2 * r + 2)
                    sp.dma_start(out[0, 128 * r:128 * r + 128], rows[:, r]).then_inc(S["out_done"], 16)
            else:
                sp.wait_ge(S["x_tile"], RES[live[-1]] + 16)
                sp.dma_start(debug, xflat).then_inc(S["out_done"], 16)
            sp.wait_ge(S["out_done"], 32 if debug is None else 16)

        @block.gpsimd
        def _(pool):
            pool.nop().then_inc(S["kv_free"], 1)

            def spill(i):
                pool.wait_ge(S["v_rows_taken"], i * 4 + 4)
                pool.dma_start(kv_spill[i], kv[:]).then_inc(S["kv_spilled"], 16)
                pool.wait_ge(S["kv_spilled"], i * 16 + 16)
                pool.nop().then_inc(S["kv_free"], 1)
            run(pool, "mem", spill)
            if "ssd" in live:
                pool.wait_ge(S["x_tile"], 16)
                pool.dma_start(x_spill, xflat).then_inc(S["x_spilled"], 16)
                pool.wait_ge(S["x_spilled"], 16)
                pool.wait_ge(S["y_mem"], 4)
                pool.dma_start(kv[:], kv_spill[0]).then_inc(S["kv_loaded"], 16)
            if "latent" in live:
                pool.wait_ge(S["y_ssd"], 4)
                pool.dma_start(xflat, x_spill).then_inc(S["x_loaded"], 16)
                pool.dma_start(pos_i, pos).then_inc(S["pos_loaded"], 16)
                pool.wait_ge(S["h_ready"], 16)
                pool.dma_start(x_spill, xflat).then_inc(S["x_spilled"], 16)
                pool.wait_ge(S["x_spilled"], 32)
                pool.wait_ge(S["lat_ready"], 2)
                pool.dma_start(mask, mla_mask).then_inc(S["mask_loaded"], 16)
                pool.wait_ge(S["y_mla"], 8)
                pool.dma_start(xflat, x_spill).then_inc(S["x_loaded"], 16)
            if "ret_a" in live:
                pool.dma_start(cs_r, ret_tab).then_inc(S["ret_tab_loaded"], 16)
                pool.dma_start(dec, ret_decay[0]).then_inc(S["decay_loaded"], 16)
                last = 8 if "ret_b" in live else 4
                with pool.Fori(1, last) as h:
                    pool.wait_ge(S["decay_used"], h * 1)
                    pool.dma_start(dec, ret_decay[h]).then_inc(S["decay_loaded"], 16)
                pool.wait_ge(S["decay_loaded"], 16 * last)
            if "ssd" in live:
                pool.wait_ge(S["kv_loaded"], 16)

        @block.scalar
        def _(act):
            A = nc.scalar.activation

            def split(name, i, j, h):
                it = part(name, i, j, h)
                if it:
                    c, p, s, a, b = it
                    act.wait_ge(loaded[c.slot(p, 4)], c.filled(p))
                    act.wait_ge(half_started, c.half(p - 2, h, 1))
                    A(w_hi[:, s, 0:b - a, :], raw[:, c.slot(p, 4), a:b, :], ACT.Copy).then_inc(hi_ready, 1)

            def copy_half(name, i, o, weight=1):
                c = outputs(name, i)
                act.wait_ge(output_ready, c(o, 1))
                A(half[:, c.slot(o, NB)], pj[:, c.slot(o, NB), 0:T], ACT.Copy).then_inc(half_copied, weight)

            def rsqrt(k, v, y):
                act.wait_ge(S["var_ready"], k)
                A(y, v, ACT.Ln)
                act.drain()
                A(y, y, ACT.Exp, scale=-0.5).then_inc(S["rsqrt_ready"], 1)

            act.dma_start(mem_rows, mem.rearrange("b (r p) c -> p (b r) c", p=P)).then_inc(S["mem_rows"], 16)
            act.dma_start(vec[:], vecs).then_inc(S["tables"], 16)
            act.dma_start(con[:], consts).then_inc(S["tables"], 16)
            act.dma_start(rows, x.rearrange("b (r p) c -> p (b r) c", p=P)).then_inc(S["x_rows"], 16)
            act.dma_start(wdt[:], w_dt).then_inc(S["tables"], 16)
            for k, (src, loaded_, sq_, var_, rs_, dst, w) in enumerate((
                    (mem_rows, "mem_rows", "mem_squares", "mem_var", "mem_rsqrt", ys, "mem_norm"),
                    (rows, "x_rows", "x_squares", "x_var", "x_rsqrt", hs, "norm0"))):
                act.wait_ge(S[loaded_], 16)
                for r in range(2):
                    junk = hs[:, 8 * k + 4 * r:8 * k + 4 * r + 4].rearrange("p a b c -> p (a b c)")
                    A(junk, src[:, r], ACT.Square, accum_out=ss[:, 2 * k + r:2 * k + r + 1])
                act.drain().then_inc(S[sq_], 1)
                if k == 0:
                    for s in range(3):
                        act.wait_ge(loaded[s // 2], 16)
                        A(w_hi[:, s], raw[:, s // 2, HALF * (s % 2):HALF * (s % 2) + HALF],
                          ACT.Copy).then_inc(hi_ready, 1)
                    act.wait_ge(S["tables"], 48)
                act.wait_ge(S[var_], 1)
                A(rs4[:, 2 * k:2 * k + 2], var4[:, 2 * k:2 * k + 2], ACT.Ln)
                act.drain()
                A(rs4[:, 2 * k:2 * k + 2], rs4[:, 2 * k:2 * k + 2], ACT.Exp, scale=-0.5).then_inc(S[rs_], 1)
                for g in range(8):
                    act.wait_ge(S["transposed"], 16 * k + g + 1)
                    for u in range(2):
                        c = 2 * g + u
                        A(dst[:, c, 0], mx[:, (16 * k + g) % 6, T * u:T * (u + 1)], ACT.Copy,
                          scale=V(w, c)).then_inc(S["part_hi"], 1)

            def mem_body(i):
                for j in range(8):
                    split("mem", i, j, 1)
                    split("mem", i, j, 0)
                    copy_half("mem", i, j)
                    if j >= 5:
                        value_rows(i, j - 5)
                value_rows(i, 3)

            def value_rows(i, n):
                act.wait_ge(S["v_rows"], i * 4 + n + 1)
                A(values[:, :, 128 * n:128 * n + 128], mx[:, n, 0:256].rearrange("p (m c) -> p m c", m=2),
                  ACT.Copy).then_inc(S["v_rows_taken"], 1)
            run(act, "mem", mem_body)

            def gate_body(i):
                for j in range(4):
                    split("gate", i, j, 1)
                    if j == 1:
                        act.wait_ge(evacuated, outputs("gate", i)(0, 1 + NB))
                        A(th_g, z_g, ACT.Tanh, scale=0.5).then_inc(S["gate_tanh"], 1)
                    split("gate", i, j, 0)
                    copy_half("gate", i, j)
            run(act, "gate", gate_body)

            act.wait_ge(S["dt_exp_in"], 1)
            A(dtw[2], dtw[1], ACT.Exp)
            A(ea, vec[:, VEC["a_log"][0]:VEC["a_log"][1]], ACT.Exp)
            act.drain().then_inc(S["dt_exp"], 1)

            def gate_out_body(i):
                for j in range(4):
                    split("gate_out", i, j, 1)
                    split("gate_out", i, j, 0)
                    copy_half("gate_out", i, 2 * j)
                    copy_half("gate_out", i, 2 * j + 1)
            run(act, "gate_out", gate_out_body)
            act.wait_ge(S["dte_logits"], 1)
            A(dte, mx[:, 1, 0:32], ACT.Exp).then_inc(S["dte_ready"], 1)

            def residual(name, ppo):
                gains, column_gain = NEXT.get(name, ([], None))

                def body(i):
                    for j in range(len(PHASES[name][0])):
                        split(name, i, j, 1)
                        split(name, i, j, 0)
                        if j % ppo == ppo - 1:
                            o = j // ppo
                            copy_half(name, i, o)
                            if gains:
                                act.wait_ge(S["x_tile"], i * 4 + (RES[name] + o + 1))
                            for k, gain in enumerate(gains):
                                ins = A(sq[k][o % 2], xT[:, i * 4 + o], ACT.Square, scale=dyn(gain, i, o))
                                if k == len(gains) - 1:
                                    ins.then_inc(S["x_square"], 1)
                            if column_gain:
                                A(hs[:, i * 4 + o, 0], xT[:, i * 4 + o], ACT.Copy,
                                  scale=dyn(column_gain, i, o)).then_inc(S["h_hi"], 1)
                run(act, name, body)

            def dyn(gain, i, o):
                return 1.0 if gain is None else vec[:, bass.ds(i * 4 + (VEC[gain][0] + o), 1)]

            def mem_exp(c, heads, scores, probs, vh, values_):
                for u in range(heads):
                    A(vh[u].rearrange("p (m c) -> p m c", m=2), values_(u), ACT.Copy)
                    act.wait_ge(S["mem_shift"], c(u, 1))
                    for q in range(2):
                        A(probs[u][:, T * q:T * q + T], scores(u)[:, T * q:T * q + T], ACT.Exp, scale=MEM_SCALE,
                          bias=mstat[:, 4 * u + q:4 * u + q + 1], accum_out=mstat[:, 4 * u + 2 + q:4 * u + 3 + q])
                    act.drain().then_inc(S["mem_probs"], 1)

            def ssd_body(i):
                O = outputs("ssd", i)
                M = Count(0, 1, i)
                for j in range(12):
                    split("ssd", i, j, 1)
                    if 1 <= j <= 4:
                        act.wait_ge(S["seg_ready"], i * 4 + j)
                        A(em[j - 1], mx[:, 1 + (j - 1) % 2], ACT.Exp).then_inc(S["decay_ready"], 1)
                    if 2 <= j <= 7:
                        act.wait_ge(S["conv_done"], i * 6 + (j - 1))
                        A(th[j % 2], cv[j % 2], ACT.Tanh).then_inc(S["conv_tanh"], 1)
                    if j == 2:
                        mem_exp(M, 1, lambda u: mx[:, 3], [probs_s], [vh_s],
                                lambda u: values[:, :, bass.ds(i * 128, 128)])
                    if j == 4:
                        act.wait_ge(S["mem_pt"], M(0, 1))
                        A(pt_s, mx[:, 4], ACT.Copy).then_inc(S["mem_pt_copied"], 1)
                    if j == 5:
                        act.wait_ge(S["cb_ready"], i * 1 + 1)
                        A(brow, mx[:, 0, 256:384], ACT.Copy).then_inc(S["brow_ready"], 1)
                    if j == 6:
                        act.wait_ge(S["eq_logits"], i * 1 + 1)
                        A(eqx, mx[:, 2], ACT.Exp).then_inc(S["eq_ready"], 1)
                    if j >= 8:
                        act.wait_ge(evacuated, O(j - 1, 1 + NB))
                        A(sz[:, j - 8], cp[j % 2][:, 3:259], ACT.Tanh, scale=0.5).then_inc(S["z_tanh"], 1)
                    if j == 10:
                        act.wait_ge(S["state_ready"], i * 1 + 1)
                        A(state, mx[:, 5], ACT.Copy).then_inc(S["state_copied"], 1)
                    if j == 11:
                        act.wait_ge(S["ssd_gated"], i * 1 + 1)
                        A(ssq, xs, ACT.Square).then_inc(S["ssd_squares"], 1)
                    split("ssd", i, j, 0)
                    copy_half("ssd", i, j)
                act.wait_ge(evacuated, O(11, 1 + NB))
                A(th0, cv0, ACT.Tanh, scale=0.5).then_inc(S["mz_tanh"], 1)
                rsqrt(i * 1 + 1, em[0][:, 0:256], em[0][:, 256:512])
            if "ssd" in live:
                act.wait_ge(S["x_spilled"], 16)
                run(act, "ssd", ssd_body)
            if "out0" in live:
                residual("out0", 2)
            if "latent" in live:
                rsqrt(NORM["b_latent"] + 1, nv, ny)

                def copy_body(name):
                    def body(i):
                        for j in range(len(PHASES[name][0])):
                            split(name, i, j, 1)
                            split(name, i, j, 0)
                            copy_half(name, i, j)
                    return body
                run(act, "latent", copy_body("latent"))
                act.wait_ge(S["angle_ready"], 1)
                A(sinT, ang, ACT.Sin)
                A(cosT, ang, ACT.Sin, scale=0.5)
                act.drain().then_inc(S["sin_ready"], 1)
                run(act, "latent_tail", copy_body("latent_tail"))

                def memq_body(i):
                    O = outputs("memq", i)
                    M = Count(4, 2, i)
                    for j in range(4):
                        split("memq", i, j, 1)
                        if j == 3:
                            mem_exp(M, 2, lambda u: mx[:, u], [p_m[:, 0:512], p_m[:, 512:1024]],
                                    [vh_m[:, 0:256], vh_m[:, 256:512]],
                                    lambda u: values[:, :, bass.ds(i * 256 + 128 * u, 128)])
                        split("memq", i, j, 0)
                        copy_half("memq", i, j)
                    act.wait_ge(evacuated, O(3, 1 + NB))
                    A(mt_m, mz_m, ACT.Tanh, scale=0.5).then_inc(S["mz_tanh"], 1)
                    for u in range(2):
                        act.wait_ge(S["mem_pt"], M(u, 1))
                        A(pt_m[:, 512 * u:512 * u + 512], mx[:, 2 + u], ACT.Copy).then_inc(S["mem_pt_copied"], 1)
                act.wait_ge(S["x_spilled"], 32)
                act.wait_ge(S["kv_loaded"], 16)
                run(act, "memq", memq_body)
                act.wait_ge(S["latent_ready"], 1)
                A(lsq, lraw, ACT.Square).then_inc(S["latent_squares"], 1)
                rsqrt(NORM["kv"] + 1, lnv, lny)
                rsqrt(NORM["q"] + 1, lnv, lny)
            if "mla" in live:
                def mla_body(i):
                    O = outputs("mla", i)
                    for j in range(8):
                        split("mla", i, j, 1)
                        if j == 6:
                            act.wait_ge(S["mla_shift"], i * 1 + 1)
                            for u in range(2):
                                for q, a, b in ((0, 0, 128), (1, 128, 384)):
                                    k = 2 * u + q
                                    e = s_[:, 384 * u + a:384 * u + b]
                                    A(e, e, ACT.Exp, scale=MLA_SCALE, bias=pstat[:, k:k + 1],
                                      accum_out=pstat[:, 4 + k:5 + k])
                            act.drain().then_inc(S["mla_probs"], 1)
                        if j == 7:
                            act.wait_ge(S["mla_vt"], i * 1 + 1)
                            A(vrow_, mx[:, 2], ACT.Copy).then_inc(S["mla_vrow"], 1)
                            act.wait_ge(S["mla_pt"], i * 1 + 1)
                            A(pt_.rearrange("p (u c) -> p u c", u=2), mx[:, 3:5, 0:384],
                              ACT.Copy).then_inc(S["mla_pt_copied"], 1)
                        split("mla", i, j, 0)
                        if j == 3:
                            copy_half("mla", i, 3)
                            copy_half("mla", i, 4)
                        elif j == 7:
                            copy_half("mla", i, 8, 2)
                        else:
                            copy_half("mla", i, j if j < 3 else j + 1)
                    act.wait_ge(evacuated, O(8, 2 + NB))
                    A(zt_, zz_, ACT.Tanh, scale=0.5).then_inc(S["mla_tanh"], 1)
                run(act, "mla", mla_body)
            if "out1" in live:
                residual("out1", 2)
            if "ret_a" in live:
                rsqrt(NORM["b_final"] + 1, nv, ny)
                rsqrt(NORM["b_ret"] + 1, nv, ny)

            def ret_body(name, first):
                def body(i):
                    O = outputs(name, i)
                    for j in range(12):
                        split(name, i, j, 1)
                        if 6 <= j <= 9:
                            n = j - 6
                            act.wait_ge(S["ret_vt"], i * 4 + (4 * first + n + 1))
                            for k in range(2):
                                ins = A(vrow_r[:, k, 128 * n:128 * n + 128], mx[:, 1 + n % 2, 128 * k:128 * k + 128],
                                        ACT.Copy, scale=rstd[:, 256 + k:257 + k],
                                        accum_out=v_sum[:, 4 * k + n:4 * k + n + 1])
                            ins.then_inc(S["ret_vrow"], 1)
                        if j == 10:
                            act.wait_ge(S["ret_pv"], i * 1 + (first + 1))
                            o_psum = mx[:, 3:5].rearrange("p b c -> p (b c)")
                            A(gen[:, 0:1024], o_psum, ACT.Square).then_inc(S["ret_squares"], 1)
                            A(kv[:, 0:1024], o_psum, ACT.Copy).then_inc(S["ret_o"], 1)
                        if j >= 9:
                            n = j - 9
                            act.wait_ge(evacuated, O(j - 1, 1 + NB))
                            A(th_r[:, T * (n % 2):T * (n % 2) + T], sg_r[:, n], ACT.Tanh,
                              scale=0.5).then_inc(S["ret_tanh"], 1)
                        if j == 11:
                            rsqrt(i * 1 + (NORM[name] + 1), vt_r[:, 0:256], vt_r[:, 256:512])
                        split(name, i, j, 0)
                        copy_half(name, i, j)
                    act.wait_ge(evacuated, O(11, 1 + NB))
                    A(th_r[:, T:2 * T], sg_r[:, 3], ACT.Tanh, scale=0.5).then_inc(S["ret_tanh"], 1)
                run(act, name, body)

            for ph, first in (("ret_a", 0), ("ret_b", 4)):
                if ph in live:
                    ret_body(ph, first)
                    residual("ret_out" + ph[3:], 1)
            if "up0" in live:
                rsqrt(NORM["b_mlp"] + 1, nv, ny)
            for b in range(FF_BLOCKS):
                if f"up{b}" in live:
                    def up_body(i):
                        for j in range(4):
                            split(f"up{b}", i, j, 1)
                            split(f"up{b}", i, j, 0)
                            copy_half(f"up{b}", i, j)
                    run(act, f"up{b}", up_body)
                    residual(f"down{b}", 1)
            if debug is None:
                rsqrt(NORM["b_out"] + 1, nv[:, 256:258], ny[:, 256:258])
                act.wait_ge(S["fin_scale"], 1)
                for g in range(1, 8, 2):
                    act.wait_ge(S["fin_rows"], g + 1)
                    A(rows[:, g // 4, 512 * (g % 4):512 * (g % 4) + 512], fin_bank(g), ACT.Copy,
                      scale=rstd[:, 256 + g // 4:257 + g // 4]).then_inc(S["fin_act"], 1)
        @block.vector
        def _(dve):
            v = nc.vector
            TT, TS, STT = v.tensor_tensor, v.tensor_scalar, v.scalar_tensor_tensor

            def split(name, i, j, h):
                it = part(name, i, j, h)
                if it:
                    c, p, s, a, b = it
                    dve.wait_ge(hi_ready, c.half(p, h))
                    TT(w_lo[:, s, 0:b - a, :], raw[:, c.slot(p, 4), a:b, :], w_hi[:, s, 0:b - a, :].bitcast(F32),
                       ALU.subtract).then_inc(split_ready, 1)

            def evac(name, i, o, dst, weight=1, scale=None, via=None):
                c = outputs(name, i)
                dve.wait_ge(half_copied, c(o, 1))
                k = c.slot(o, NB)
                if scale is None:
                    TT(dst, pj[:, k, T:2 * T], half[:, k], ALU.add).then_inc(evacuated, weight)
                else:
                    via = dst if via is None else via
                    TT(via, pj[:, k, T:2 * T], half[:, k], ALU.add)
                    dve.drain()
                    TT(dst, via, scale, ALU.mult).then_inc(evacuated, weight)

            def hi_lo(dst, src):
                dve.drain()
                v.tensor_copy(dst[0], src)
                dve.drain()
                return TT(dst[1], src, dst[0].bitcast(F32), ALU.subtract)

            def newton(vv, y, t, out_, s=1.0):
                TT(t, y, y, ALU.mult)
                dve.drain()
                TT(t, t, vv, ALU.mult)
                dve.drain()
                TS(t, t, -0.5, 1.5, ALU.mult, ALU.add)
                dve.drain()
                ins = TT(out_, y, t, ALU.mult)
                dve.drain()
                return ins

            def inverse_rms(k, bank, n, vv, y, t, out_, a=0, b=T):
                dve.wait_ge(S["stat_ready"], k)
                TS(vv, mx[:, bank, a:b], 1.0 / n, EPS, ALU.mult, ALU.add).then_inc(S["var_ready"], 1)
                dve.wait_ge(S["rsqrt_ready"], k)
                newton(vv, y, t, out_)

            v.nop().then_inc(evacuated, NB)
            for k, (sq_, var_, rs_, rows_, scaled) in enumerate((
                    ("mem_squares", "mem_var", "mem_rsqrt", mem_rows, "mem_scaled"),
                    ("x_squares", "x_var", "x_rsqrt", rows, "x_scaled"))):
                a, b = 2 * k, 2 * k + 2
                dve.wait_ge(S[sq_], 1)
                TS(var4[:, a:b], ss[:, a:b], 1.0 / D, EPS, ALU.mult, ALU.add).then_inc(S[var_], 1)
                if k == 0:
                    for s in range(3):
                        dve.wait_ge(hi_ready, s + 1)
                        TT(w_lo[:, s], raw[:, s // 2, HALF * (s % 2):HALF * (s % 2) + HALF], w_hi[:, s].bitcast(F32),
                           ALU.subtract).then_inc(split_ready, 1)
                else:
                    dve.wait_ge(S["transposed"], 16)
                dve.wait_ge(S[rs_], 1)
                newton(var4[:, a:b], rs4[:, a:b], tmp4[:, a:b], rs4[:, a:b])
                for r in range(2):
                    ins = TS(rows_[:, r], rows_[:, r], rs4[:, a + r:a + r + 1], None, ALU.mult)
                ins.then_inc(S[scaled], 1)
                if k == 0:
                    for g in range(8):
                        for u in range(2):
                            c = 2 * g + u
                            dve.wait_ge(S["part_hi"], 2 * g + 2)
                            STT(out=ys[:, c, 1], in0=mx[:, g % 6, T * u:T * u + T], scalar=V("mem_norm", c),
                                in1=ys[:, c, 0].bitcast(F32), op0=ALU.mult,
                                op1=ALU.subtract).then_inc(S["part_taken"], 1)
                    for g in range(8):
                        dve.wait_ge(S["transposed"], 8 + g + 1)
                        v.tensor_copy(xT[:, 2 * g:2 * g + 2].rearrange("p a t -> p (a t)"),
                                      mx[:, (8 + g) % 6]).then_inc(S["part_taken"], 2)
            for g in range(8):
                for u in range(2):
                    c = 2 * g + u
                    dve.wait_ge(S["part_hi"], 16 + 2 * g + 2)
                    STT(out=hs[:, c, 1], in0=mx[:, (16 + g) % 6, T * u:T * u + T], scalar=V("norm0", c),
                        in1=hs[:, c, 0].bitcast(F32), op0=ALU.mult, op1=ALU.subtract).then_inc(S["part_taken"], 1)

            def mem_body(i):
                for j in range(8):
                    split("mem", i, j, 1)
                    if j == 0:
                        dve.wait_ge(S["kv_free"], i * 1 + 1)
                    if j >= 6:
                        dve.wait_ge(S["v_rows"], i * 4 + (j - 5))
                    split("mem", i, j, 0)
                    evac("mem", i, j, keys[:, j] if j < 4 else vt[j % 2])
            run(dve, "mem", mem_body)

            v.memset(u_g[:, 0:2], 0.0)
            a, b, c = (vec[:, VEC[n][0]:VEC[n][1]] for n in ("final", "norm1_2", "final_norm1_2"))
            TT(c, a, b, ALU.mult)
            a_v = VEC["ssd_conv"][0]
            TS(vec[:, a_v:a_v + 30 * GROUPS], vec[:, a_v:a_v + 30 * GROUPS], 0.5, None, ALU.mult)

            def gate_body(i):
                w0 = VEC["gate_conv"][0]

                def tap(k):
                    return vec[:, bass.ds(i * 3 + (w0 + k), 1)]
                split("gate", i, 0, 1)
                split("gate", i, 0, 0)
                evac("gate", i, 0, z_g)
                split("gate", i, 1, 1)
                split("gate", i, 1, 0)
                evac("gate", i, 1, c_g)
                dve.wait_ge(S["gate_tanh"], i * 1 + 1)
                STT(out=s_g, in0=th_g, scalar=1.0, in1=z_g, op0=ALU.add, op1=ALU.mult)
                split("gate", i, 2, 1)
                split("gate", i, 2, 0)
                evac("gate", i, 2, v_g)
                dve.drain()
                TT(u_g[:, 2:258], c_g, v_g, ALU.mult)
                split("gate", i, 3, 1)
                dve.drain()
                TS(a_g, u_g[:, 0:256], tap(0), None, ALU.mult)
                dve.drain()
                STT(out=e_g, in0=u_g[:, 1:257], scalar=tap(1), in1=a_g, op0=ALU.mult, op1=ALU.add)
                dve.drain()
                STT(out=a_g, in0=u_g[:, 2:258], scalar=tap(2), in1=e_g, op0=ALU.mult, op1=ALU.add)
                split("gate", i, 3, 0)
                evac("gate", i, 3, b_g)
                dve.drain()
                STT(out=e_g, in0=a_g, scalar=0.5, in1=b_g, op0=ALU.mult, op1=ALU.mult)
                dve.drain()
                TT(a_g, e_g, s_g, ALU.mult)
                hi_lo((ys[:, i, 0], ys[:, i, 1]), a_g).then_inc(S["y_gate"], 1)
            run(dve, "gate", gate_body)

            zt, mn, ex, den, s1, zz, pp, tt = dtw
            dve.wait_ge(S["dt_logits"], 1)
            b0 = VEC["dt_bias"][0]
            TT(zt, mx[:, 0, 0:64].rearrange("p (c h) -> p c h", c=2),
               vec[:, b0:b0 + 32].unsqueeze(1).to_broadcast([P, 2, 32]), ALU.add)
            dve.drain()
            TS(tt, zt, -1.0, None, ALU.mult)
            dve.drain()
            TT(mn, zt, tt, ALU.min).then_inc(S["dt_exp_in"], 1)
            dve.wait_ge(S["dt_exp"], 1)
            TS(den, ex, 2.0, None, ALU.add)
            dve.drain()
            v.reciprocal(den, den)
            dve.drain()
            TT(s1, ex, den, ALU.mult)
            dve.drain()
            TT(zz, s1, s1, ALU.mult)
            dve.drain()
            TS(pp, zz, 1.0 / 15, None, ALU.mult)
            dve.drain()
            for k in (13, 11, 9, 7, 5, 3):
                STT(out=pp, in0=pp, scalar=1.0 / k, in1=zz, op0=ALU.add, op1=ALU.mult)
                dve.drain()
            STT(out=pp, in0=pp, scalar=1.0, in1=s1, op0=ALU.add, op1=ALU.mult)
            TS(zt, zt, 0.0, None, ALU.max)
            dve.drain()
            STT(out=dt, in0=pp, scalar=2.0, in1=zt, op0=ALU.mult, op1=ALU.add)
            dve.drain()
            STT(out=da, in0=dt, scalar=-1.0, in1=ea.unsqueeze(1).to_broadcast([P, 2, 32]), op0=ALU.mult,
                op1=ALU.mult).then_inc(S["dt_ready"], 1)

            def residual(name, ppo, opp=1):
                gains, column_gain = NEXT.get(name, ([], None))
                n_out = outs_per.get(name, len(PHASES[name][0]))
                for k in range(len(gains)):
                    dve.drain()
                    v.memset(acc[k], 0.0)

                def body(i):
                    def column(gain, o):
                        return vec[:, bass.ds(i * 4 + (VEC[gain][0] + o), 1)]
                    for j in range(len(PHASES[name][0])):
                        o = j // ppo * opp
                        split(name, i, j, 1)
                        split(name, i, j, 0)
                        if j % ppo == ppo - 1:
                            for u in range(opp):
                                if u:
                                    dve.drain()
                                evac(name, i, o + u, res[(o + u) % 2])
                                dve.drain()
                                xo = xT[:, i * n_out + (o + u)]
                                TT(xo, xo, res[(o + u) % 2], ALU.add).then_inc(S["x_tile"], 1)
                        if j % ppo == ppo - 1 and gains:
                            dve.wait_ge(S["x_square"], i * 4 + (SQ[name] + o + 1))
                            for k in range(len(gains)):
                                TT(acc[k], acc[k], sq[k][o % 2], ALU.add)
                            if column_gain:
                                dve.wait_ge(S["h_hi"], i * 4 + (SQ[name] + o + 1))
                                STT(out=hs[:, i * 4 + o, 1], in0=xT[:, i * 4 + o], scalar=column(column_gain, o),
                                    in1=hs[:, i * 4 + o, 0].bitcast(F32), op0=ALU.mult,
                                    op1=ALU.subtract).then_inc(S["h_ready"], 1)
                            if name == LAST:
                                TS(xT[:, i * 4 + o], xT[:, i * 4 + o], column("final_2", o), None,
                                   ALU.mult).then_inc(S["h_ready"], 1)
                run(dve, name, body)
                if gains:
                    dve.drain().then_inc(S["acc_ready"], 1)

            if "gate_out" in live:
                residual("gate_out", 1, 2)

            def softmax_shift(M, heads, scores):
                for u in range(heads):
                    dve.wait_ge(S["mem_scores"], M(u, 1))
                    v.reduce_max(mstat[:, 4 * u:4 * u + 2], scores(u).rearrange("p (q k) -> p q k", q=2), AX.X)
                    dve.drain()
                    TS(mstat[:, 4 * u:4 * u + 2], mstat[:, 4 * u:4 * u + 2], -MEM_SCALE, None,
                       ALU.mult).then_inc(S["mem_shift"], 1)

            def softmax_scale(M, heads, probs):
                for u in range(heads):
                    dve.wait_ge(S["mem_probs"], M(u, 1))
                    v.reciprocal(mstat[:, 4 * u + 2:4 * u + 4], mstat[:, 4 * u + 2:4 * u + 4])
                    dve.drain()
                    for q in range(2):
                        ins = TS(probs[u][:, T * q:T * q + T], probs[u][:, T * q:T * q + T],
                                 mstat[:, 4 * u + 2 + q:4 * u + 3 + q], None, ALU.mult)
                    ins.then_inc(S["mem_scaled_probs"], 1)

            def rope(dst, tmp):
                for h in range(4):
                    a, b = 32 * h, 32 * (h ^ 1)
                    TT(tmp[a:a + 32], dst[b:b + 32], sinT[b:b + 32], ALU.mult)
                dve.drain()
                TT(dst, dst, cosT, ALU.mult)
                dve.drain()
                ins = TT(dst, dst, tmp, ALU.add)
                dve.drain()
                return ins

            if "ssd" in live:
                dve.drain()
                v.memset(cp0[:, 0:3], 0.0)
                v.memset(cp1[:, 0:3], 0.0)

            def ssd_body(i):
                w0 = VEC["ssd_conv"][0]
                M = Count(0, 1, i)
                xdt_v = [w.rearrange("p (h d) -> p h d", h=8) for w in xdt]

                def conv(n):
                    src, t3, t2 = cp[n % 2], cv[n % 2], th[n % 2]

                    def w(k):
                        return vec[:, bass.ds(i * 30 + (w0 + 5 * n + k), 1)]
                    dve.drain()
                    TS(t2, src[:, 0:256], w(0), w(4), ALU.mult, ALU.add)
                    dve.drain()
                    STT(out=t3, in0=src[:, 1:257], scalar=w(1), in1=t2, op0=ALU.mult, op1=ALU.add)
                    dve.drain()
                    STT(out=t2, in0=src[:, 2:258], scalar=w(2), in1=t3, op0=ALU.mult, op1=ALU.add)
                    dve.drain()
                    STT(out=t3, in0=src[:, 3:259], scalar=w(3), in1=t2, op0=ALU.mult,
                        op1=ALU.add).then_inc(S["conv_done"], 1)

                def silu(n):
                    dve.wait_ge(S["conv_tanh"], i * 6 + (n + 1))
                    dst = (bT, cT, xs[:, 0], xs[:, 1], xs[:, 2], xs[:, 3])[n]
                    ins = STT(out=dst, in0=th[n % 2], scalar=1.0, in1=cv[n % 2], op0=ALU.add, op1=ALU.mult)
                    if n == 1:
                        ins.then_inc(S["bc_ready"], 1)
                    if n == 5:
                        ins.then_inc(S["xs_ready"], 1)

                def seg_rhs(r):
                    if r >= 2:
                        dve.wait_ge(S["seg_ready"], i * 4 + r - 1)
                    TT(rr[r % 2].rearrange("p (h q) -> p h q", h=4),
                       da[:, r // 2, bass.ds(i * 8 + 4 * (r % 2), 4)].unsqueeze(2).to_broadcast([P, 4, 128]),
                       upto.unsqueeze(1).to_broadcast([P, 4, 128]), ALU.mult).then_inc(S["seg_rhs"], 1)

                def mix(r):
                    dve.wait_ge(S["decay_ready"], i * 4 + r + 1)
                    e = em[r].rearrange("p (h q) -> p h q", h=4)
                    c = r // 2
                    TT(e, e, cbm[:, 128 * c:128 * c + 128].unsqueeze(1).to_broadcast([P, 4, 128]),
                       ALU.mult).then_inc(S["mix_ready"], 1)

                def z_gate(n):
                    dve.wait_ge(S["z_tanh"], i * 4 + n + 1)
                    STT(out=sz[:, n], in0=sz[:, n], scalar=1.0, in1=cp[n % 2][:, 3:259], op0=ALU.add, op1=ALU.mult)

                for j in range(12):
                    split("ssd", i, j, 1)
                    if j <= 3:
                        seg_rhs(j)
                    if 3 <= j <= 8:
                        silu(j - 3)
                    if 2 <= j <= 7:
                        conv(j - 2)
                    if j == 2:
                        softmax_shift(M, 1, lambda u: mx[:, 3])
                    if j == 3:
                        softmax_scale(M, 1, [probs_s])
                    if j == 4:
                        dve.wait_ge(S["seg_ready"], i * 4 + 3)
                        TT(r0.rearrange("p (h d) -> p h d", h=8),
                           da[:, 1, bass.ds(i * 8, 8)].unsqueeze(2).to_broadcast([P, 8, 64]),
                           ones[:, 0:64].unsqueeze(1).to_broadcast([P, 8, 64]), ALU.mult).then_inc(S["eq_lhs"], 1)
                    if j == 5:
                        dve.wait_ge(S["mem_pv"], M(0, 1))
                        TS(mo_s, mx[:, 3, 0:256], 0.5, None, ALU.mult)
                        dve.wait_ge(S["brow_ready"], i * 1 + 1)
                        TT(cbm.rearrange("p (c q) -> p c q", c=2), mx[:, 0, 0:256].rearrange("p (c q) -> p c q", c=2),
                           upto.unsqueeze(1).to_broadcast([P, 2, 128]), ALU.mult).then_inc(S["cb_taken"], 1)
                        dve.drain()
                    if j in (6, 7):
                        mix(2 * (j - 6))
                        mix(2 * (j - 6) + 1)
                    if j == 9:
                        dve.wait_ge(S["xs_rows"], i * 1 + 1)
                        for c, bank in ((0, 5), (1, 0)):
                            TT(xdt_v[c], mx[:, bank].rearrange("p (h d) -> p h d", h=8),
                               dt[:, c, bass.ds(i * 8, 8)].unsqueeze(2).to_broadcast([P, 8, 64]), ALU.mult)
                        dve.drain()
                        TT(xdte.rearrange("p (h d) -> p h d", h=8), xdt_v[0],
                           dte[:, bass.ds(i * 8, 8)].unsqueeze(2).to_broadcast([P, 8, 64]),
                           ALU.mult).then_inc(S["xdt_ready"], 1)
                    if j >= 8:
                        z_gate(j - 8)
                    if j == 10:
                        dve.wait_ge(S["ydiag_ready"], i * 4 + 4)
                        d0 = VEC["ssd_d"][0]
                        for n in range(4):
                            for c in range(2):
                                w = xs[:, n, 128 * c:128 * c + 128]
                                STT(out=w, in0=w, scalar=vec[:, bass.ds(i * 4 + (d0 + n), 1)],
                                    in1=mx[:, 3 + c, 128 * n:128 * n + 128], op0=ALU.mult, op1=ALU.add)
                    if j == 11:
                        dve.wait_ge(S["yoff_ready"], i * 1 + 1)
                        dve.wait_ge(S["eq_ready"], i * 1 + 1)
                        TT(eqx, mx[:, 0], eqx, ALU.mult)
                        dve.drain()
                        TT(xs[:, :, 128:256], xs[:, :, 128:256], eqx.rearrange("p (a q) -> p a q", a=4), ALU.add)
                        dve.drain()
                        STT(out=xs_, in0=xs_, scalar=0.5, in1=sz_, op0=ALU.mult,
                            op1=ALU.mult).then_inc(S["ssd_gated"], 1)
                    split("ssd", i, j, 0)
                    evac("ssd", i, j, mq_s if j == 0 else cv0 if j == 11 else cp[(j - 1) % 2][:, 3:259])
                dve.wait_ge(S["mz_tanh"], i * 1 + 1)
                STT(out=th0, in0=th0, scalar=1.0, in1=cv0, op0=ALU.add, op1=ALU.mult)
                dve.drain()
                TT(cv1, mo_s, th0, ALU.mult)
                hi_lo((ys[:, i, 0], ys[:, i, 1]), cv1).then_inc(S["y_mem"], 1)
                nrm = [em[k // 2][:, 256 * (k % 2):256 * (k % 2) + 256] for k in range(4)]
                inverse_rms(i * 1 + 1, 5, 512, *nrm)
                n0 = VEC["ssd_norm"][0]
                for n in range(4):
                    STT(out=xs[:, n], in0=xs[:, n], scalar=vec[:, bass.ds(i * 4 + (n0 + n), 1)], in1=nrm[3],
                        op0=ALU.mult, op1=ALU.mult)
                hi_lo((ys[:, bass.ds(i * 4 + 4, 4), 0], ys[:, bass.ds(i * 4 + 4, 4), 1]), xs).then_inc(S["y_ssd"], 1)
            if "ssd" in live:
                dve.wait_ge(S["x_spilled"], 16)
                run(dve, "ssd", ssd_body)
            if "out0" in live:
                dve.wait_ge(S["x_loaded"], 16)
                residual("out0", 2)
            if "latent" in live:
                inverse_rms(NORM["b_latent"] + 1, 0, D, nv, ny, nt, rstd, b=258)

                def latent_body(i):
                    for j in range(4):
                        split("latent", i, j, 1)
                        split("latent", i, j, 0)
                        evac("latent", i, j, lraw[:, i * 4 + j], scale=rstd[:, 0:T], via=(krA, krB)[j % 2])
                run(dve, "latent", latent_body)
                dve.wait_ge(S["pos_loaded"], 16)
                v.tensor_copy(tt_, pos_i)
                dve.drain()
                TS(ang, tt_, V("inv_freq"), None, ALU.mult)
                dve.drain()
                TS(kk_, ang, float(np.float32(1 / (2 * np.pi))), 12582912.0, ALU.mult, ALU.add)
                dve.drain()
                TS(kk_, kk_, -12582912.0, None, ALU.add)
                two_pi = 2 * np.pi
                c1 = 6.28125
                c2 = float(np.float32(np.round((two_pi - c1) * 2 ** 22) / 2 ** 22))
                c3 = float(np.float32(two_pi - c1 - c2))
                for cc in (c1, c2, c3):
                    dve.drain()
                    STT(out=ang, in0=kk_, scalar=-cc, in1=ang, op0=ALU.mult, op1=ALU.add)
                dve.drain()
                pi = float(np.nextafter(np.float32(np.pi), np.float32(0)))
                TS(ang, ang, pi, -pi, ALU.min, ALU.max).then_inc(S["angle_ready"], 1)
                dve.wait_ge(S["sin_ready"], 1)
                TT(cosT, cosT, cosT, ALU.mult)
                TS(sinT, sinT, V("sin_sign"), None, ALU.mult)
                dve.drain()
                TS(cosT, cosT, -2.0, 1.0, ALU.mult, ALU.add)
                dve.drain()
                for j in range(3):
                    split("latent_tail", 0, j, 1)
                    split("latent_tail", 0, j, 0)
                    evac("latent_tail", 0, j, lraw[:, 8 + j] if j < 2 else krA, scale=rstd[:, 0:T])
                dve.drain()
                rope(krA, lnv)
                v.tensor_copy(krB[64:128], krA[64:128])
                v.memset(krB[0:64], 0.0)
                dve.drain()
                v.memset(krA[64:128], 0.0).then_inc(S["krope_ready"], 1)
                dve.wait_ge(S["x_spilled"], 32)

                def memq_body(i):
                    M = Count(4, 2, i)
                    for j in range(4):
                        split("memq", i, j, 1)
                        if j == 3:
                            softmax_shift(M, 2, lambda u: mx[:, u])
                            softmax_scale(M, 2, [p_m[:, 0:512], p_m[:, 512:1024]])
                        split("memq", i, j, 0)
                        evac("memq", i, j, (mq_m, mz_m)[j // 2][:, T * (j % 2):T * (j % 2) + T], scale=rstd[:, 0:T])
                    dve.wait_ge(S["mz_tanh"], i * 1 + 5)
                    STT(out=mz_m, in0=mt_m, scalar=1.0, in1=mz_m, op0=ALU.add, op1=ALU.mult)
                    dve.drain()
                    dve.wait_ge(S["mem_pv"], M(1, 1))
                    STT(out=mt_m.rearrange("p (u t) -> p u t", u=2), in0=mx[:, 4:6, 0:256], scalar=0.5,
                        in1=mz_m.rearrange("p (u t) -> p u t", u=2), op0=ALU.mult, op1=ALU.mult)
                    yy = ys[:, bass.ds(i * 2, 2)]
                    hi_lo((yy[:, :, 0], yy[:, :, 1]), mt_m.rearrange("p (u t) -> p u t", u=2)
                          ).then_inc(S["y_mem"], 2)
                run(dve, "memq", memq_body)
                dve.drain().then_inc(S["latent_ready"], 1)
                for k, (name, a, b) in enumerate((("kv", 0, 4), ("q", 4, 10))):
                    inverse_rms(NORM[name] + 1, k, 128 * (b - a), lnv, lny, lnt, lrstd)
                    for c in range(a, b):
                        STT(out=lraw[:, c], in0=lraw[:, c], scalar=V(name + "_norm", c - a), in1=lrstd, op0=ALU.mult,
                            op1=ALU.mult)
                    hi_lo((lat[:, a:b, 0], lat[:, a:b, 1]), lraw[:, a:b]).then_inc(S["lat_ready"], 1)

            if "mla" in live:
                dve.wait_ge(S["mask_loaded"], 16)
                s3 = s_.rearrange("p (u c) -> p u c", u=2)

                def mla_body(i):
                    for j in range(8):
                        split("mla", i, j, 1)
                        if j == 3:
                            dve.drain()
                            rope(qr, qro)
                        if j == 5:
                            dve.wait_ge(S["mla_scores"], i * 1 + 1)
                            TT(s3, mx[:, 0:2, 0:384], mask.unsqueeze(1).to_broadcast([P, 2, 384]), ALU.add)
                            dve.drain()
                            pm = pstat[:, 0:4].rearrange("p (u q) -> p u q", u=2)
                            v.reduce_max(pm[:, :, 0], s3[:, :, 0:128], AX.X)
                            v.reduce_max(pm[:, :, 1], s3[:, :, 128:384], AX.X)
                            dve.drain()
                            TS(pstat[:, 0:4], pstat[:, 0:4], -MLA_SCALE, None, ALU.mult).then_inc(S["mla_shift"], 1)
                        if j == 6:
                            dve.wait_ge(S["mla_probs"], i * 1 + 1)
                            v.reciprocal(pstat[:, 8:12], pstat[:, 4:8])
                            dve.drain()
                            for u in range(2):
                                for q, a, b in ((0, 0, 128), (1, 128, 384)):
                                    k = 8 + 2 * u + q
                                    e = s_[:, 384 * u + a:384 * u + b]
                                    ins = TS(e, e, pstat[:, k:k + 1], None, ALU.mult)
                            ins.then_inc(S["mla_probs_scaled"], 1)
                        split("mla", i, j, 0)
                        if j == 3:
                            evac("mla", i, 3, kn[0])
                            evac("mla", i, 4, kn[1])
                            dve.drain().then_inc(S["qk_ready"], 1)
                        elif j == 7:
                            evac("mla", i, 8, zz_[:, 256:512], 2, scale=rstd[:, 0:T])
                        else:
                            evac("mla", i, j if j < 3 else j + 1,
                                 (qn[0], qn[1], qr, None, vtm[0], vtm[1], zz_[:, 0:256])[j],
                                 scale=rstd[:, 0:T] if j == 6 else None)
                    dve.wait_ge(S["mla_tanh"], i * 1 + 1)
                    STT(out=zz_, in0=zt_, scalar=1.0, in1=zz_, op0=ALU.add, op1=ALU.mult)
                    dve.drain()
                    dve.wait_ge(S["mla_pv"], i * 1 + 1)
                    STT(out=zt_, in0=mx[:, 5], scalar=0.5, in1=zz_, op0=ALU.mult, op1=ALU.mult)
                    yy = ys[:, bass.ds(i * 2 + 4, 2)]
                    hi_lo((yy[:, :, 0], yy[:, :, 1]), zt_.rearrange("p (u t) -> p u t", u=2)).then_inc(S["y_mla"], 1)
                run(dve, "mla", mla_body)
            if "out1" in live:
                dve.wait_ge(S["x_loaded"], 32)
                residual("out1", 2)
            if "ret_a" in live:
                inverse_rms(NORM["b_final"] + 1, 0, D, nv, ny, nt, rstd_final, b=258)
                dve.wait_ge(S["stat_ready"], NORM["b_ret"] + 1)
                TT(nt, rstd_final, rstd_final, ALU.mult)
                dve.drain()
                STT(out=nv, in0=mx[:, 1, 0:258], scalar=1.0 / D, in1=nt, op0=ALU.mult, op1=ALU.mult)
                dve.drain()
                TS(nv, nv, EPS, None, ALU.add).then_inc(S["var_ready"], 1)
                dve.wait_ge(S["rsqrt_ready"], NORM["b_ret"] + 1)
                newton(nv, ny, nt, rstd)
                TT(rstd, rstd, rstd_final, ALU.mult)
                dve.wait_ge(S["ret_tab_loaded"], 16)
                dve.drain()
                for k in range(2):
                    TT(cs_r[:, T * k:T * k + T], cs_r[:, T * k:T * k + T], rstd[:, 0:T], ALU.mult)

            def ret_body(name, first):
                def body(i):
                    def rotate(src, dst):
                        dve.drain()
                        a, b = src[:, 0:256], src[:, 256:512]
                        t1, t2 = t12[:, 0:256], t12[:, 256:512]
                        c_, s1_ = cs_r[:, 0:256], cs_r[:, 256:512]
                        TT(t1, a, c_, ALU.mult)
                        TT(t2, b, s1_, ALU.mult)
                        dve.drain()
                        TT(dst[:, 0:256], t1, t2, ALU.subtract)
                        dve.drain()
                        TT(t1, a, s1_, ALU.mult)
                        TT(t2, b, c_, ALU.mult)
                        dve.drain()
                        return TT(dst[:, 256:512], t1, t2, ALU.add)

                    def gate(n):
                        dve.wait_ge(S["ret_tanh"], i * 4 + (4 * first + n + 1))
                        STT(out=sg_r[:, n], in0=th_r[:, T * (n % 2):T * (n % 2) + T], scalar=1.0, in1=sg_r[:, n],
                            op0=ALU.add, op1=ALU.mult)

                    for j in range(12):
                        split(name, i, j, 1)
                        if j == 2:
                            rotate(rq, q_r)
                            dve.drain()
                        if j == 4:
                            rotate(rq, k_r).then_inc(S["ret_qk"], 1)
                        if j in (6, 7):
                            dve.wait_ge(S["ret_vt"], i * 4 + (4 * first + j - 5))
                        if j == 7:
                            dve.wait_ge(S["ret_scores"], i * 1 + (first + 1))
                            dve.wait_ge(S["decay_loaded"], i * 16 + 16 * (first + 1))
                            TT(sd, mx[:, 0, 0:384], dec, ALU.mult).then_inc(S["decay_used"], 1)
                        if j == 9:
                            dve.wait_ge(S["ret_vrow"], i * 4 + (4 * first + 4))
                            v.reduce_sum(v_mean, v_sum.rearrange("p (k n) -> p k n", k=2), AX.X)
                            dve.drain()
                            TS(v_mean, v_mean, -1.0 / 512, None, ALU.mult)
                            dve.drain()
                            for k in range(2):
                                ins = TS(vrow_r[:, k], vrow_r[:, k], v_mean[:, k:k + 1], None, ALU.add)
                            ins.then_inc(S["ret_vcent"], 1)
                        if j >= 9:
                            gate(j - 9)
                        if first == 0 and j % 3 == 0:
                            xo = xT[:, i * 4 + j // 3]
                            STT(out=xo, in0=xo, scalar=vec[:, bass.ds(i * 4 + (VEC["final"][0] + j // 3), 1)],
                                in1=rstd_final[:, 0:T], op0=ALU.mult, op1=ALU.mult)
                        if j == 11:
                            inverse_rms(i * 1 + (NORM[name] + 1), 5, 512, vt_r[:, 0:256], vt_r[:, 256:512],
                                        rq[:, 0:256], rq[:, 256:512])
                            dve.wait_ge(S["ret_o"], i * 1 + (first + 1))
                            g0 = VEC["gn_gain"][0] + 4 * first
                            for n in range(4):
                                STT(out=o_r[:, n], in0=o_r[:, n], scalar=vec[:, bass.ds(i * 4 + (g0 + n), 1)],
                                    in1=rq[:, 256:512], op0=ALU.mult, op1=ALU.mult)
                        dst = (rq[:, 0:256], rq[:, 256:512], rq[:, 0:256], rq[:, 256:512],
                               vt_r[:, 0:256], vt_r[:, 256:512], vt_r[:, 0:256], vt_r[:, 256:512],
                               sg_r[:, 0], sg_r[:, 1], sg_r[:, 2], sg_r[:, 3])[j]
                        split(name, i, j, 0)
                        evac(name, i, j, dst, scale=rstd[:, 0:T] if j >= 8 else None)
                    gate(3)
                    dve.drain()
                    STT(out=o_r, in0=o_r, scalar=0.5, in1=sg_r, op0=ALU.mult, op1=ALU.mult)
                    yy = ys[:, bass.ds(i * 4, 4)]
                    hi_lo((yy[:, :, 0], yy[:, :, 1]), o_r).then_inc(S["y_ret"], 1)
                run(dve, name, body)

            for ph, first in (("ret_a", 0), ("ret_b", 4)):
                if ph in live:
                    ret_body(ph, first)
                    residual("ret_out" + ph[3:], 1)
            if "up0" in live:
                inverse_rms(NORM["b_mlp"] + 1, 0, D, nv, ny, nt, rstd, b=258)
                TT(rstd_sq, rstd, rstd, ALU.mult)
            for b in range(FF_BLOCKS):
                if f"up{b}" in live:
                    def up_body(i):
                        for j in range(4):
                            split(f"up{b}", i, j, 1)
                            split(f"up{b}", i, j, 0)
                            evac(f"up{b}", i, j, up_t[j % 2])
                            dve.drain()
                            STT(out=up_t[2 + j % 2], in0=up_t[j % 2], scalar=0.0, in1=up_t[j % 2], op0=ALU.max,
                                op1=ALU.mult)
                            dve.drain()
                            TT(up_t[2 + j % 2], up_t[2 + j % 2], rstd_sq[:, 0:T], ALU.mult)
                            yy = ys[:, i * 4 + j]
                            hi_lo((yy[:, 0], yy[:, 1]), up_t[2 + j % 2]).then_inc(S["y_up"], 1)
                    run(dve, f"up{b}", up_body)
                    residual(f"down{b}", 1)
            if debug is None:
                inverse_rms(NORM["b_out"] + 1, 0, D, *(w[:, 256:258] for w in (nv, ny, nt, rstd)), a=256, b=258)
                dve.drain().then_inc(S["fin_scale"], 1)
                for g in range(0, 8, 2):
                    dve.wait_ge(S["fin_rows"], g + 1)
                    TS(rows[:, g // 4, 512 * (g % 4):512 * (g % 4) + 512], fin_bank(g),
                       rstd[:, 256 + g // 4:257 + g // 4], None, ALU.mult).then_inc(S["fin_dve"], 1)
        @block.tensor
        def _(pe):
            mm = nc.tensor.matmul

            def panel(name, i, j, pieces):
                c, O = panels(name, i), outputs(name, i)
                s = 2 * c.slot(j, 2)
                sizes = PHASES[name][0]
                started = 2 if j and sizes[j - 1] <= cut(j - 1, sizes[j - 1]) else 1
                half_ = cut(j, sizes[j])
                pe.wait_ge(split_ready, c.half(j, 0))
                for o, moving, at, opens, closes, weight in pieces:
                    k = O.slot(o, NB)
                    if opens:
                        pe.wait_ge(evacuated, O(o, 1))
                    for t, m in enumerate(moving):
                        h = int(at + t >= half_)
                        u = at + t - h * half_
                        if h and u == 0:
                            pe.wait_ge(split_ready, c.half(j, 1))
                        ins = mm(pj[:, k], w_hi[:, s + h, u], m, start=opens and t == 0, stop=False)
                        if u == 0:
                            ins.then_inc(half_started, 1 if h else started)
                        ins = mm(pj[:, k, 0:T], w_lo[:, s + h, u], m[:, 0], start=False,
                                 stop=closes and t == len(moving) - 1)
                    if closes:
                        ins.then_inc(output_ready, weight)

            def tiles(src, a, b):
                return [src[:, k] for k in range(a, b)]

            def whole(name, i, j, src, o=None):
                panel(name, i, j, [(j if o is None else o, tiles(src, 0, 16), 0, True, True, 1)])

            def transpose_to(dst, src):
                return nc.tensor.transpose(dst, src, ident)

            pe.wait_ge(S["tables"], 48)
            pe.wait_ge(S["mem_scaled"], 1)
            for g in range(24):
                if g == 8:
                    pe.wait_ge(S["x_rows"], 16)
                if g == 16:
                    pe.wait_ge(S["x_scaled"], 1)
                if g >= 6:
                    pe.wait_ge(S["part_taken"], 2 * (g - 6) + 2)
                src = mem_rows if g < 8 else rows
                for u in range(2):
                    for r in range(2):
                        c = 2 * (g % 8) + u
                        ins = transpose_to(mx[:, g % 6, T * u + 128 * r:T * u + 128 * r + 128],
                                           src[:, r, 128 * c:128 * c + 128])
                ins.then_inc(S["transposed"], 1)

            def mem_body(i):
                O = outputs("mem", i)

                def value_rows(n):
                    pe.wait_ge(evacuated, O(4 + n, 1 + NB))
                    for m in range(2):
                        ins = transpose_to(mx[:, n, 128 * m:128 * m + 128], vt[n % 2][:, 128 * m:128 * m + 128])
                    ins.then_inc(S["v_rows"], 1)
                for j in range(8):
                    whole("mem", i, j, ys)
                    if j >= 5:
                        value_rows(j - 5)
                value_rows(3)
            pe.wait_ge(S["part_taken"], 48)
            run(pe, "mem", mem_body)

            def gate_body(i):
                for j in range(4):
                    whole("gate", i, j, hs)
            run(pe, "gate", gate_body)

            for r in range(2):
                for k in range(16):
                    for part in range(2):
                        ins = mm(mx[:, 0, 32 * r:32 * r + 32],
                                 hs[:, k, part, 128 * r:128 * r + 128].bitcast(F32), wdt[:, k],
                                 start=k == 0 and part == 0, stop=k == 15 and part == 1)
            ins.then_inc(S["dt_logits"], 1)

            def gate_out_body(i):
                for j in range(4):
                    panel("gate_out", i, j, [(2 * j + u, tiles(ys, 0, 8), 8 * u, True, True, 1) for u in range(2)])
            pe.wait_ge(S["y_gate"], 8)
            run(pe, "gate_out", gate_out_body)
            pe.wait_ge(S["dt_ready"], 1)
            mm(mx[:, 1, 0:32], after, da[:, 0], start=True, stop=True).then_inc(S["dte_logits"], 1)

            def residual(name, ppo, src):
                def body(i):
                    for j in range(len(PHASES[name][0])):
                        n = PHASES[name][0][j]
                        a = (j % ppo) * n
                        panel(name, i, j, [(j // ppo, tiles(src, a, a + n), 0, j % ppo == 0, j % ppo == ppo - 1, 1)])
                run(pe, name, body)

            def square_sum(n=1):
                square_sum.n += 1
                pe.wait_ge(S["acc_ready"], square_sum.n)
                for k in range(n):
                    for r in range(2):
                        mm(mx[:, k, T + r:T + r + 1], acc[k][:, 128 * r:128 * r + 128], ones[:, 0:1], start=True,
                           stop=True)
                    mm(mx[:, k, 0:T], ones, acc[k], start=True, stop=True).then_inc(S["stat_ready"], 1)

            def mem_scores(q_, key_, bank):
                for q in range(2):
                    ins = mm(mx[:, bank, T * q:T * q + T], q_[:, 128 * q:128 * q + 128], key_, start=True, stop=True)
                ins.then_inc(S["mem_scores"], 1)

            def mem_pt(probs, bank):
                for k in range(2):
                    for q in range(2):
                        ins = transpose_to(mx[:, bank, T * k + 128 * q:T * k + 128 * q + 128],
                                           probs[:, T * q + 128 * k:T * q + 128 * k + 128])
                ins.then_inc(S["mem_pt"], 1)

            def mem_pv(vh, pt, bank):
                for k in range(2):
                    ins = mm(mx[:, bank, 0:T], vh[:, 128 * k:128 * k + 128], pt[:, T * k:T * k + T], start=k == 0,
                             stop=k == 1)
                ins.then_inc(S["mem_pv"], 1)

            def ssd_body(i):
                O = outputs("ssd", i)
                M = Count(0, 1, i)

                def seg(r):
                    pe.wait_ge(S["seg_rhs"], i * 4 + r + 1)
                    if r >= 2:
                        pe.wait_ge(S["decay_ready"], i * 4 + r - 1)
                    mm(mx[:, 1 + r % 2], after, rr[r % 2], start=True, stop=True).then_inc(S["seg_ready"], 1)

                def ydiag(r):
                    pe.wait_ge(S["mix_ready"], i * 4 + r + 1)
                    for h in range(4):
                        hh = 4 * (r % 2) + h
                        ins = mm(mx[64 * (h % 2):64 * (h % 2) + 64, 3 + r // 2, 128 * (hh // 2):128 * (hh // 2) + 128],
                                 xdt[r // 2][:, 64 * hh:64 * hh + 64], em[r][:, 128 * h:128 * h + 128],
                                 start=True, stop=True)
                    ins.then_inc(S["ydiag_ready"], 1)

                for j in range(12):
                    whole("ssd", i, j, hs)
                    if j <= 3:
                        seg(j)
                    if j == 1:
                        pe.wait_ge(evacuated, O(0, 1 + NB))
                        mem_scores(mq_s, keys[:, i], 3)
                    if j == 3:
                        pe.wait_ge(S["mem_scaled_probs"], M(0, 1))
                        mem_pt(probs_s, 4)
                    if j == 4:
                        pe.wait_ge(S["bc_ready"], i * 1 + 1)
                        for c in range(2):
                            mm(mx[:, 0, 128 * c:128 * c + 128], bT[:, 128 * c:128 * c + 128],
                               cT[:, 128 * c:128 * c + 128], start=True, stop=True)
                        transpose_to(mx[:, 0, 256:384], bT[:, 0:128]).then_inc(S["cb_ready"], 1)
                        pe.wait_ge(S["mem_pt_copied"], M(0, 1))
                        mem_pv(vh_s, pt_s, 3)
                    if j == 5:
                        pe.wait_ge(S["eq_lhs"], i * 1 + 1)
                        pe.wait_ge(S["decay_ready"], i * 4 + 4)
                        for n in range(4):
                            ins = mm(mx[:, 2, 128 * n:128 * n + 128], r0[:, 128 * n:128 * n + 128], upto, start=True,
                                     stop=True)
                        ins.then_inc(S["eq_logits"], 1)
                    if j == 8:
                        pe.wait_ge(S["xs_ready"], i * 1 + 1)
                        pe.wait_ge(S["cb_taken"], i * 1 + 1)
                        for c, bank in ((0, 5), (1, 0)):
                            for n in range(4):
                                ins = transpose_to(mx[:, bank, 128 * n:128 * n + 128],
                                                   xs[:, n, 128 * c:128 * c + 128])
                        ins.then_inc(S["xs_rows"], 1)
                    if j == 9:
                        pe.wait_ge(S["xdt_ready"], i * 1 + 1)
                        for r in range(4):
                            ydiag(r)
                        mm(mx[:, 5], brow, xdte, start=True, stop=True).then_inc(S["state_ready"], 1)
                    if j == 10:
                        pe.wait_ge(S["state_copied"], i * 1 + 1)
                        for n in range(4):
                            ins = mm(mx[:, 0, 128 * n:128 * n + 128], state[:, 128 * n:128 * n + 128], cT[:, 128:256],
                                     start=True, stop=True)
                        ins.then_inc(S["yoff_ready"], 1)
                pe.wait_ge(S["ssd_squares"], i * 1 + 1)
                for n in range(4):
                    ins = mm(mx[:, 5, 0:T], ones, ssq[:, n], start=n == 0, stop=n == 3)
                ins.then_inc(S["stat_ready"], 1)
            if "ssd" in live:
                pe.wait_ge(S["dte_ready"], 1)
                run(pe, "ssd", ssd_body)
            square_sum.n = 0
            if "out0" in live:
                pe.wait_ge(S["y_ssd"], 4)
                residual("out0", 2, ys)
            if "latent" in live:
                square_sum()
                pe.wait_ge(S["h_ready"], 16)

                def latent_body(i):
                    for j in range(4):
                        whole("latent", i, j, hs)
                run(pe, "latent", latent_body)
                for j in range(3):
                    whole("latent_tail", 0, j, hs)

                def memq_body(i):
                    O = outputs("memq", i)
                    M = Count(4, 2, i)
                    for j in range(4):
                        whole("memq", i, j, hs)
                        if j == 2:
                            pe.wait_ge(evacuated, O(1, 1 + NB))
                            for u in range(2):
                                mem_scores(mq_m[:, T * u:T * u + T], keys[:, i * 2 + u], u)
                    for u in range(2):
                        pe.wait_ge(S["mem_scaled_probs"], M(u, 1))
                        mem_pt(p_m[:, 512 * u:512 * u + 512], 2 + u)
                    for u in range(2):
                        pe.wait_ge(S["mem_pt_copied"], M(u, 1))
                        mem_pv(vh_m[:, T * u:T * u + T], pt_m[:, 512 * u:512 * u + 512], 4 + u)
                pe.wait_ge(S["kv_loaded"], 16)
                run(pe, "memq", memq_body)
                pe.wait_ge(S["latent_squares"], 1)
                for k, (a, b) in enumerate(((0, 4), (4, 10))):
                    for c in range(a, b):
                        ins = mm(mx[:, k, 0:T], ones, lsq[:, c], start=c == a, stop=c == b - 1)
                    ins.then_inc(S["stat_ready"], 1)
            if "mla" in live:
                def mla_body(i):
                    O = outputs("mla", i)
                    kv_t, q_t = tiles(lat, 0, 4), tiles(lat, 4, 10)
                    for j in range(8):
                        panel("mla", i, j, (
                            [(0, q_t, 0, True, True, 1)], [(1, q_t, 0, True, True, 1)], [(2, q_t, 0, True, True, 1)],
                            [(3, kv_t, 0, True, True, 1), (4, kv_t, 4, True, True, 1)],
                            [(5, kv_t, 0, True, True, 1)], [(6, kv_t, 0, True, True, 1)],
                            [(7, tiles(hs, 0, 16), 0, True, True, 1)], [(8, tiles(hs, 0, 16), 0, True, True, 2)])[j])
                        if j == 4:
                            pe.wait_ge(S["qk_ready"], i * 1 + 1)
                            for u, kr_ in enumerate((krA, krB)):
                                for q, a, n in ((0, 0, 128), (1, 128, 256)):
                                    dst = mx[:, u, a:a + n]
                                    mm(dst, qn[u][:, 128 * q:128 * q + 128], kn[u][:, 0:n], start=True, stop=False)
                                    ins = mm(dst, qr[:, 128 * q:128 * q + 128], kr_[:, 0:n], start=False, stop=True)
                            ins.then_inc(S["mla_scores"], 1)
                        if j in (5, 6):
                            u = j - 5
                            pe.wait_ge(evacuated, O(5 + u, 1 + NB))
                            for k in range(2):
                                ins = transpose_to(mx[:, 2, T * u + 128 * k:T * u + 128 * k + 128],
                                                   vtm[u][:, 128 * k:128 * k + 128])
                            if u == 1:
                                ins.then_inc(S["mla_vt"], 1)
                        if j == 6:
                            pe.wait_ge(S["mla_probs_scaled"], i * 1 + 1)
                            for u in range(2):
                                for a in (0, 128, 256):
                                    ins = transpose_to(mx[:, 3 + u, a:a + 128], s_[:, 384 * u + a:384 * u + a + 128])
                            ins.then_inc(S["mla_pt"], 1)
                    pe.wait_ge(S["mla_vrow"], i * 1 + 1)
                    pe.wait_ge(S["mla_pt_copied"], i * 1 + 1)
                    for u in range(2):
                        mm(mx[:, 5, T * u:T * u + T], vrow_[:, T * u:T * u + 128], pt_[:, 384 * u:384 * u + 256],
                           start=True, stop=False)
                        ins = mm(mx[:, 5, T * u + 128:T * u + 256], vrow_[:, T * u + 128:T * u + 256],
                                 pt_[:, 384 * u + 256:384 * u + 384], start=False, stop=True)
                    ins.then_inc(S["mla_pv"], 1)
                pe.wait_ge(S["lat_ready"], 2)
                pe.wait_ge(S["krope_ready"], 1)
                run(pe, "mla", mla_body)
            if "out1" in live:
                pe.wait_ge(S["y_mla"], 8)
                residual("out1", 2, ys)
            if "ret_a" in live:
                square_sum(2)
                pe.wait_ge(S["h_ready"], 32)

            def ret_body(name, first):
                def body(i):
                    O = outputs(name, i)
                    for j in range(12):
                        whole(name, i, j, hs)
                        if 5 <= j <= 8:
                            n = j - 5
                            pe.wait_ge(evacuated, O(4 + n, 1 + NB))
                            if n >= 2:
                                pe.wait_ge(S["ret_vrow"], i * 4 + (4 * first + n - 1))
                            for k in range(2):
                                ins = transpose_to(mx[:, 1 + n % 2, 128 * k:128 * k + 128],
                                                   vt_r[:, T * (n % 2) + 128 * k:T * (n % 2) + 128 * k + 128])
                            ins.then_inc(S["ret_vt"], 1)
                        if j == 6:
                            pe.wait_ge(S["ret_qk"], i * 1 + (first + 1))
                            for k, a, n in ((0, 0, 256), (1, 256, 128)):
                                for d in range(2):
                                    ins = mm(mx[:, 0, a:a + n], k_r[:, T * d + 128 * k:T * d + 128 * k + 128],
                                             q_r[:, T * d + T - n:T * d + T], start=d == 0, stop=d == 1)
                            ins.then_inc(S["ret_scores"], 1)
                        if j == 9:
                            pe.wait_ge(S["ret_vcent"], i * 1 + (first + 1))
                            pe.wait_ge(S["decay_used"], i * 1 + (first + 1))
                            for n in range(4):
                                dst = mx[:, 3 + n // 2, T * (n % 2):T * (n % 2) + T]
                                mm(dst, vrow_r[:, 0, 128 * n:128 * n + 128], sd[:, 0:256], start=True, stop=False)
                                ins = mm(dst[:, 128:256], vrow_r[:, 1, 128 * n:128 * n + 128], sd[:, 256:384],
                                         start=False, stop=True)
                            ins.then_inc(S["ret_pv"], 1)
                        if j == 10:
                            pe.wait_ge(S["ret_squares"], i * 1 + (first + 1))
                            for n in range(4):
                                ins = mm(mx[:, 5, 0:T], ones, sq_r[:, n], start=n == 0, stop=n == 3)
                            ins.then_inc(S["stat_ready"], 1)
                run(pe, name, body)

            for ph, first in (("ret_a", 0), ("ret_b", 4)):
                if ph in live:
                    ret_body(ph, first)
                    pe.wait_ge(S["y_ret"], first + 4)
                    residual("ret_out" + ph[3:], 1, ys)
            for b in range(FF_BLOCKS):
                if f"up{b}" in live:
                    if b == 0:
                        square_sum()
                        pe.wait_ge(S["h_ready"], 48)

                    def up_body(i):
                        for j in range(4):
                            whole(f"up{b}", i, j, hs)
                    run(pe, f"up{b}", up_body)
                    pe.wait_ge(S["y_up"], 16 * b + 16)
                    residual(f"down{b}", 1, ys)
            if debug is None:
                square_sum()
                pe.wait_ge(S["h_ready"], 64)
                pe.wait_ge(evacuated, Count(first_out[LAST])(16, NB))
                pe.wait_ge(S["var_ready"], NORM["b_out"] + 1)
                for g in range(8):
                    for u in range(4):
                        c = 4 * (g % 4) + u
                        ins = transpose_to(fin_bank(g)[:, 128 * u:128 * u + 128],
                                           xT[:, c, 128 * (g // 4):128 * (g // 4) + 128])
                    ins.then_inc(S["fin_rows"], 1)


def _tiles(w, rows, cols):
    return [w[128 * r:128 * r + 128, c:c + 128] for c in cols for r in rows]


def _stream(name, inp):
    w_in0, w_out0, w_in1, w_out1 = inp["w_in0"], inp["w_out0"], inp["w_in1"], inp["w_out1"]
    n = PHASES[name][1]
    k16 = range(16)
    its = []
    ret_in, ret_out = inp["ret_w_in_2"][0], inp["ret_w_out_2"][0]
    up, down = inp["mlp_w_up_2"][0], inp["mlp_w_down_2"][0]
    for i in range(n):
        if name == "mem":
            cols = range(0, 512, 128)
            its.append(_tiles(inp[f"mem_k{1 - i}"], k16, cols) + _tiles(inp[f"mem_v{1 - i}"], k16, cols))
        elif name == "gate":
            its.append(_tiles(w_in0, k16, [s * 1024 + 128 * i for s in (3, 1, 2, 0)]))
        elif name == "gate_out":
            its.append(_tiles(w_out0, range(8), range(1024 * i, 1024 * i + 1024, 128)))
        elif name == "ssd":
            xbc = 4096 + 2048
            its.append(_tiles(w_in0, k16, [9248 + 128 * i, xbc + 2048 + 128 * i, xbc + 2560 + 128 * i]
                              + [xbc + 512 * i + 128 * t for t in range(4)]
                              + [4096 + 512 * i + 128 * t for t in range(4)] + [9760 + 128 * i]))
        elif name == "out0":
            its.append(_tiles(w_out0, list(range(24, 28)) + list(range(8, 24)), range(512 * i, 512 * i + 512, 128)))
        elif name == "latent":
            its.append(_tiles(w_in1, k16, [(768 if i == 0 else 0) + 128 * t for t in range(4)]))
        elif name == "latent_tail":
            kr = np.concatenate([w_in1[:, 1280:1344]] * 2, axis=1)
            its.append(_tiles(w_in1, k16, [512, 640]) + _tiles(kr, k16, [0]))
        elif name == "memq":
            its.append(_tiles(w_in1, k16, [3392 + 256 * i, 3520 + 256 * i, 3904 + 256 * i, 4032 + 256 * i]))
        elif name == "mla":
            uq, ukv = inp["mla_w_uq"], inp["mla_w_ukv"]
            qc, kc = 384 * i, 512 * i
            qr = np.concatenate([uq[:, qc + 128:qc + 192], uq[:, qc + 320:qc + 384]], axis=1)
            its.append(_tiles(uq, range(6), [qc, qc + 192]) + _tiles(qr, range(6), [0])
                       + _tiles(ukv, range(4), [kc, kc + 256, kc + 128, kc + 384])
                       + _tiles(w_in1, k16, [1344 + 256 * i, 1472 + 256 * i]))
        elif name == "out1":
            its.append(_tiles(w_out1, list(range(16, 20)) + list(range(16)), range(512 * i, 512 * i + 512, 128)))
        elif name in ("ret_a", "ret_b"):
            h = i + (4 if name == "ret_b" else 0)
            its.append(_tiles(ret_in, k16, [256 * h, 256 * h + 128, 2048 + 256 * h, 2176 + 256 * h]
                              + [4096 + 512 * h + 128 * t for t in range(4)]
                              + [8192 + 512 * h + 128 * t for t in range(4)]))
        elif name in ("ret_out_a", "ret_out_b"):
            r = 16 if name == "ret_out_b" else 0
            its.append(_tiles(ret_out, range(r, r + 16), range(512 * i, 512 * i + 512, 128)))
        elif name.startswith("up"):
            b = int(name[2:])
            its.append(_tiles(up, k16, [2048 * b + 512 * i + 128 * t for t in range(4)]))
        else:
            b = int(name[4:])
            its.append(_tiles(down, range(16 * b, 16 * b + 16), range(512 * i, 512 * i + 512, 128)))
    out = np.empty((n, P, sum(PHASES[name][0]) * 128), np.float32)
    for i, parts in enumerate(its):
        for t, w in enumerate(parts):
            out[i, :, 128 * t:128 * t + 128] = w
    return out


def _columns(v):
    return np.asarray(v).reshape(-1, P).T


def _vectors(inp):
    out = np.zeros((P, NVEC), np.float32)

    def put(name, cols):
        a, b = VEC[name]
        out[:, a:b] = cols
    for name, src in (("mem_norm", "mem_norm_w"), ("norm0", "norm0_w"), ("norm1", "norm1_w"), ("final", "final_norm_w"),
                      ("norm1_2", "norm1_2"), ("norm2_2", "norm2_2"), ("final_2", "final_norm_2"),
                      ("final_norm1_2", "final_norm_w"),
                      ("q_norm", "mla_q_norm_w"), ("kv_norm", "mla_kv_norm_w"), ("gn_gain", "ret_gn_gain_2"),
                      ("ssd_norm", "ssd_norm_w")):
        put(name, _columns(inp[src].reshape(-1)))
    gate = inp["sc_conv_w"]
    put("gate_conv", np.stack([_columns(gate[k]) for k in range(3)], axis=2).reshape(P, 24))
    taps = np.stack([_columns(inp["ssd_conv_w"][k]) for k in range(4)] + [_columns(inp["ssd_conv_b"])], axis=2)
    groups = [[16 + g, 20 + g] + [4 * g + t for t in range(4)] for g in range(GROUPS)]
    put("ssd_conv", np.concatenate([taps[:, t].reshape(P, 5) for g in groups for t in g], axis=1))
    put("ssd_d", _columns(np.repeat(inp["ssd_d"], 64)))
    put("dt_bias", np.broadcast_to(inp["ssd_dt_bias"], (P, 32)))
    put("a_log", np.broadcast_to(inp["ssd_a_log"], (P, 32)))
    inv = (10000.0 ** (-np.arange(32, dtype=np.float32) / np.float32(32))).astype(np.float32)
    put("inv_freq", np.tile(inv, 4)[:, None])
    put("sin_sign", np.where(np.arange(P) % 64 < 32, 1.0, -1.0)[:, None])
    return out


def _constants():
    k, q = np.arange(P)[:, None], np.arange(P)[None, :]
    con = np.zeros((P, NCONST), np.float32)
    for name, m in (("ident", k == q), ("ones", k == k), ("upto", k <= q), ("after", k > q)):
        con[:, CONST[name][0]:CONST[name][1]] = m
    causal = np.where(q <= k, 0.0, -1e30).astype(np.float32)
    mask = np.concatenate([causal, np.zeros((P, 128), np.float32), causal], axis=1)
    half_ = np.arange(0, 256, 2, dtype=np.float32)
    inv = (np.float32(10000.0) ** (-half_ / np.float32(256))).astype(np.float32)
    ang = (inv[:, None] * np.arange(T, dtype=np.float32)[None]).astype(np.float32).astype(np.float64)
    tab = np.concatenate([np.cos(ang), np.sin(ang)], axis=1).astype(np.float32)
    tk, tq = np.arange(T)[:, None], np.arange(T)[None]
    dist = np.where(tk // 64 == tq // 64, np.abs(tq - tk), tq - tk)
    seen = tk // 64 <= tq // 64
    decay = np.zeros((RET_HEADS, P, 384), np.float32)
    for h in range(RET_HEADS):
        full = np.where(seen, (1.0 - 2.0 ** (-5.0 - h)) ** dist, 0.0) / 16.0
        decay[h] = np.concatenate([full[:128], full[128:, 128:]], axis=1)
    return con, mask, tab, decay


def kernel(**inputs):
    import concourse.bacc as _bacc
    from concourse.bass_utils import run_bass_kernel_spmd as _run

    inp = {k: np.asarray(v) for k, v in inputs.items()}
    con, mask, tab, decay = _constants()
    w_dt = np.stack([inp["w_in0"][128 * k:128 * k + 128, 9216:9248] for k in range(16)], axis=1)
    arrays = {f"w_{name}": _stream(name, inp) for name in ORDER}
    arrays |= {"w_dt": w_dt, "vecs": _vectors(inp), "consts": con, "mla_mask": mask, "ret_tab": tab,
               "ret_decay": decay, "pos": np.ascontiguousarray(np.broadcast_to(inp["positions"], (P, T))),
               "x": inp["x"], "mem": inp["mem"]}
    nc = _bacc.Bacc("TRN2", target_bir_lowering=False, num_devices=1)
    arrays = {f"in_{k}": np.ascontiguousarray(v) for k, v in arrays.items()}
    aps = {k[3:]: nc.dram_tensor(k, v.shape, mybir.dt.from_np(v.dtype), kind="ExternalInput").ap()
           for k, v in arrays.items()}
    out = nc.dram_tensor("out_y", (1, T, D), F32, kind="ExternalOutput").ap()
    streams = {name: aps.pop(f"w_{name}") for name in ORDER}
    build(nc, streams, out=out, **aps)
    r = _run(nc, [arrays], core_ids=[0])
    return r.results[0]["out_y"]
```

```python
from contextlib import ExitStack

import numpy as np
import concourse.bass as bass
from concourse import mybir

P = 128
T = 256
D = 2048
EPS = 1e-6
AHEAD = 2
HALF = 8
F32 = mybir.dt.float32
F32R = mybir.dt.float32r
I32 = mybir.dt.int32
ALU = mybir.AluOpType
ACT = mybir.ActivationFunctionType
AX = mybir.AxisListType

GROUPS = 4
MEM_SCALE = 128 ** -0.5
MLA_SCALE = 192 ** -0.5
RET_HEADS = 8
FF_BLOCKS = 4

PHASES = {
    "mem": ([16] * 8, 2),
    "gate": ([16] * 4, 8),
    "gate_out": ([16] * 4, 2),
    "ssd": ([16] * 12, 4),
    "out0": ([10] * 8, 4),
    "latent": ([16] * 4, 2),
    "latent_tail": ([16] * 3, 1),
    "memq": ([16] * 4, 2),
    "mla": ([6, 6, 6, 8, 4, 4, 16, 16], 8),
    "out1": ([10] * 8, 4),
    "ret_a": ([16] * 12, 4),
    "ret_out_a": ([16] * 4, 4),
    "ret_b": ([16] * 12, 4),
    "ret_out_b": ([16] * 4, 4),
}
for _b in range(FF_BLOCKS):
    PHASES[f"up{_b}"] = ([16] * 4, 4)
    PHASES[f"down{_b}"] = ([16] * 4, 4)
ORDER = list(PHASES)

VEC = {}
_at = 0
for _name, _n in (("mem_norm", 16), ("norm0", 16), ("norm1", 16), ("final", 16), ("norm1_2", 16), ("norm2_2", 16),
                  ("final_2", 16), ("final_norm1_2", 16), ("kv_norm", 4), ("q_norm", 6), ("gn_gain", 32), ("gate_conv", 24),
                  ("ssd_conv", GROUPS * 30), ("ssd_d", 16), ("ssd_norm", 16), ("dt_bias", 32), ("a_log", 32),
                  ("inv_freq", 1), ("sin_sign", 1)):
    VEC[_name] = (_at, _at + _n)
    _at += _n
NVEC = _at

CONST = {}
_at = 0
for _name, _n in (("ident", 128), ("ones", 128), ("upto", 128), ("after", 128)):
    CONST[_name] = (_at, _at + _n)
    _at += _n
NCONST = _at


class Count:

    def __init__(self, first, per=0, i=0):
        self.first, self.per, self.i = first, per, i

    def __call__(self, j, lead=0):
        return self.i * self.per + (self.first + j + lead)

    def slot(self, j, n):
        assert self.per % n == 0
        return (self.first + j) % n

    def half(self, j, h, lead=0):
        return self.i * (2 * self.per) + (2 * (self.first + j) + h + 1 + lead)

    def filled(self, j):
        assert self.per % 4 == 0
        return self.i * (self.per * 4) + 16 * ((self.first + j) // 4 + 1)


def build(nc, streams, w_dt, vecs, consts, mla_mask, ret_tab, ret_decay, pos, x, mem, out):
    ctx = ExitStack()
    with ctx:
        def sb(name, shape, dt=F32):
            return ctx.enter_context(nc.sbuf_tensor(name, shape, dt))

        def sem(name):
            return ctx.enter_context(nc.semaphore(name))

        NB = 2
        raw = sb("raw", [P, 4, 16, 128])
        w_hi = sb("w_hi", [P, 4, 8, 128], F32R)
        w_lo = sb("w_lo", [P, 4, 8, 128], F32R)
        hs = sb("hs", [P, 16, 2, T], F32R)
        ys = sb("ys", [P, 20, 2, T], F32R)
        lat = sb("lat", [P, 10, 2, T], F32R)
        xT = sb("xT", [P, 16, T])
        kv = sb("kv", [P, 2048])
        half = sb("half", [P, NB, T])
        wdt = sb("wdt", [P, 16, 32])
        small = sb("small", [P, 224])
        vec = sb("vec", [P, NVEC])
        con = sb("con", [P, NCONST])
        GEN = 4610
        gen = sb("gen", [P, GEN])
        pj = ctx.enter_context(nc.psum_tensor("pj", [P, 2, 512], F32))
        mx = ctx.enter_context(nc.psum_tensor("mx", [P, 6, 512], F32))
        kv_spill = nc.dram_tensor("kv_spill", [2, P, 2048], F32).ap()
        x_spill = nc.dram_tensor("x_spill", [P, 16 * T], F32).ap()

        ident, ones, upto, after = (con[:, CONST[n][0]:CONST[n][1]] for n in ("ident", "ones", "upto", "after"))
        keys = kv[:, 0:1024].rearrange("p (n t) -> p n t", n=4)
        values = kv[:, 1024:2048].rearrange("p (m c) -> p m c", m=2)
        xflat = xT[:].rearrange("p a b -> p (a b)")

        def V(name, k=0):
            a = VEC[name][0] + k
            return vec[:, a:a + 1]

        def carve(start, sizes):
            views, at = [], start
            for n in sizes:
                if at < GEN and at + n > GEN:
                    at = GEN
                views.append(gen[:, at:at + n] if at + n <= GEN else xflat[:, at - GEN:at - GEN + n])
                at += n
            assert at <= GEN + 16 * T, at
            return views

        outs_per = {"gate_out": 8, "out0": 4, "out1": 4, "ret_out_a": 4, "ret_out_b": 4, "mla": 10}
        first_panel, first_out = {}, {}
        p0 = o0 = 0
        for name in ORDER:
            first_panel[name], first_out[name] = p0, o0
            sizes, n = PHASES[name]
            p0 += len(sizes) * n
            o0 += outs_per.get(name, len(sizes)) * n

        def panels(name, i=0):
            return Count(first_panel[name], len(PHASES[name][0]) if PHASES[name][1] > 1 else 0, i)

        def outputs(name, i=0):
            return Count(first_out[name], outs_per.get(name, len(PHASES[name][0])) if PHASES[name][1] > 1 else 0, i)

        def size_ahead(name, j):
            sizes, n = PHASES[name]
            if j + AHEAD < len(sizes):
                return sizes[j + AHEAD]
            j, k = j + AHEAD - len(sizes), ORDER.index(name) + 1
            return max(sizes[j] if n > 1 else 0, PHASES[ORDER[k]][0][j] if k < len(ORDER) else 0)

        def part(name, i, j, h):
            c, n = panels(name, i), size_ahead(name, j)
            if isinstance(i, int) and c(j, AHEAD) >= total_panels:
                return None
            k = cut((j + AHEAD) % len(PHASES[name][0]), n)
            return c, j + AHEAD, 2 * c.slot(j + AHEAD, 2) + h, k if h else 0, max(n, k + 1) if h else min(n, k)

        def cut(j, n):
            return n // 2 if j >= 2 and n <= HALF else HALF

        loaded = [sem(f"weights_loaded{s}") for s in range(4)]
        hi_ready = sem("weights_hi_ready")
        split_ready = sem("weights_split_ready")
        half_started = sem("half_started")
        output_ready = sem("output_ready")
        half_copied = sem("half_copied")
        evacuated = sem("evacuated")

        names = """mem_rows x_rows tables mem_squares mem_var mem_rsqrt mem_scaled x_squares x_var x_rsqrt x_scaled
            transposed part_hi part_taken v_rows v_rows_taken kv_spilled kv_free kv_loaded gate_tanh
            y_gate dt_logits dt_exp_in dt_exp dt_ready dte_logits dte_ready x_tile x_square
            x_spilled x_loaded acc_ready stat_ready var_ready rsqrt_ready h_hi h_ready conv_begun
            conv_done conv_tanh bc_ready cb_ready cb_taken brow_ready seg_rhs seg_ready decay_ready
            mix_ready ydiag_ready xs_ready xs_rows xdt_ready state_ready state_copied yoff_ready
            eq_lhs eq_logits eq_ready z_tanh mz_tanh ssd_gated ssd_squares y_ssd mem_scores
            mem_shift mem_probs mem_scaled_probs mem_pt mem_pt_copied mem_pv y_mem pos_loaded
            angle_ready sin_ready mask_loaded latent_ready latent_squares lat_ready krope_ready
            rope_turned qk_ready mla_vt mla_vrow mla_scores mla_shift mla_probs mla_probs_scaled
            mla_pt mla_pt_copied mla_pv mla_tanh y_mla ret_tab_loaded decay_loaded decay_used ret_qk
            ret_vt ret_vrow ret_scores ret_pv ret_o ret_vcent ret_squares ret_tanh y_ret y_up
            fin_scale fin_rows fin_act fin_dve out_done""".split()
        S = {n: sem(n) for n in names}

        block = ctx.enter_context(nc.Block())
        total_panels = p0

        def run(engine, name, body, first=0):
            n = PHASES[name][1]
            last = n - 1 if name == ORDER[-1] else n
            if last - first == 1:
                body(first)
            else:
                with engine.Fori(first, last) as i:
                    body(i)
            if last < n:
                body(last)

        NORM = {"ssd": 0, "b_latent": 4, "kv": 5, "q": 6, "b_final": 7, "b_ret": 8, "ret_a": 9, "ret_b": 13, "b_mlp": 17,
                "b_out": 18}
        RES = ["gate_out", "out0", "out1", "ret_out_a", "ret_out_b"] + [f"down{b}" for b in range(FF_BLOCKS)]
        RES = {n: 16 * k for k, n in enumerate(RES)}
        LAST = f"down{FF_BLOCKS - 1}"
        NEXT = {"out0": ([None], "norm1"), "out1": ([None, "final"], "final_norm1_2"), "ret_out_b": ([None], "norm2_2"),
                LAST: ([None], None)}
        SQ = {n: 16 * k for k, n in enumerate(NEXT)}

        rows = gen[:, 0:4096].rearrange("p (r c) -> p r c", r=2)
        mem_rows = xflat.rearrange("p (r c) -> p r c", r=2)
        vt = [gen[:, 4096:4352], gen[:, 4352:4608]]
        z_g, c_g, v_g, b_g, th_g, u_g, a_g, e_g, s_g = carve(0, [256] * 5 + [260] + [256] * 3)
        res = carve(0, [256, 256])
        sq, acc = [carve(512, [256, 256]), carve(1536, [256, 256])], carve(1024, [256, 256])
        nv, ny, nt, rstd_sq = carve(1794, [258, 258, 258, 258])
        rstd_final, = carve(4352, [258])
        rstd = wdt[:].rearrange("p a b -> p (a b)")[:, 0:258]
        ss, var4, rs4, tmp4 = small[:, 0:4], small[:, 4:8], small[:, 8:12], small[:, 12:16]
        mstat = small[:, 16:24]
        pstat = small[:, 24:48]
        dt = small[:, 48:112].rearrange("p (c h) -> p c h", c=2)
        da = small[:, 112:176].rearrange("p (c h) -> p c h", c=2)
        dte = small[:, 176:208]
        dtw = [w.rearrange("p (c h) -> p c h", c=2) for w in carve(2600, [64] * 8)]
        ea, = carve(3200, [32])

        (cp0, cp1, cv0, cv1, th0, th1, bT, cT, r0, r1, cbm, brow, xs_) = carve(
            0, [260, 260, 256, 256, 256, 256, 256, 256, 512, 512, 256, 128, 1024])
        em2, em3, sz_, em0, em1, xdt0, xdt1 = carve(GEN, [512, 512, 1024, 512, 512, 512, 512])
        em = [em0, em1, em2, em3]
        probs_s, pt_s, mq_s, vh_s = xdt0, xdt1, xdt1[:, 0:256], sz_[:, 256:512]
        state, eqx, mo_s, xdte = r0, r1, bT, gen[:, 1032:1544]
        cp, cv, th, rr, xdt = (cp0, cp1), (cv0, cv1), (th0, th1), (r0, r1), (xdt0, xdt1)
        xs = xs_.rearrange("p (a t) -> p a t", a=4)
        sz = sz_.rearrange("p (a t) -> p a t", a=4)
        ssq = xflat[:, 3072:4096].rearrange("p (a t) -> p a t", a=4)

        cosT, sinT, krA, krB, latr = carve(0, [256, 256, 256, 256, 2560])
        lraw = latr.rearrange("p (a t) -> p a t", a=10)
        lnv, lny, lnt, lrstd = carve(3584, [256] * 4)
        mq_m, mz_m, mt_m, vh_m, p_m, pt_m = carve(GEN, [512, 512, 512, 512, 1024, 1024])
        lsq = xflat[:, 0:2560].rearrange("p (a t) -> p a t", a=10)
        norm_q = lnv, lny, lnt, lrstd
        norm_kv = [xflat[:, 2560 + 256 * k:2816 + 256 * k] for k in range(4)]
        rope_t = xflat[:, 3584:3840]
        qn_, kn_, vt_, vrow_, zz_, zt_, qr, qro = carve(1024, [512] * 6 + [256] + [256])
        mask, s_, pt_ = carve(GEN + 2048, [384, 768, 768])
        qn, kn, vtm = ([w[:, 0:256], w[:, 256:512]] for w in (qn_, kn_, vt_))

        ang, kk_, tt_ = lnv, lny, lnt
        pos_i = lrstd.bitcast(I32)

        rq, t12, q_r, k_r, vt_r, sd, dec, cs_r, th_r = carve(0, [512, 512, 512, 512, 512, 384, 384, 512, 512])
        o_r = kv[:, 0:1024].rearrange("p (a t) -> p a t", a=4)
        vrow_r = kv[:, 1024:2048].rearrange("p (k c) -> p k c", k=2)
        sg_r = gen[:, 1024:2048].rearrange("p (a t) -> p a t", a=4)
        sq_r = gen[:, 0:1024].rearrange("p (a t) -> p a t", a=4)

        v_sum, v_mean = small[:, 208:216], small[:, 216:218]

        up_t = carve(0, [256, 256, 256, 256])

        def fin_bank(g):
            return mx[:, g] if g < 6 else pj[:, g - 6]

        @block.sync
        def _(sp):
            def load(name, i, j, reused=True):
                c = panels(name, i)
                sizes = PHASES[name][0]
                a, b = 128 * sum(sizes[:j]), 128 * sum(sizes[:j + 1])
                if reused:
                    sp.wait_ge(split_ready, c.half(j - 4, 1))
                sp.dma_start(raw[:, c.slot(j, 4), 0:sizes[j], :].rearrange("p t c -> p (t c)"),
                             streams[name][i, :, a:b]).then_inc(loaded[c.slot(j, 4)], 16)

            sp.dma_start(mem_rows, mem.rearrange("b (r p) c -> p (b r) c", p=P)).then_inc(S["mem_rows"], 16)
            for name in ORDER:
                count = len(PHASES[name][0])
                if name == "mem":
                    for j in range(count):
                        load(name, 0, j, j >= 4)
                    load_rest = 1
                else:
                    load_rest = 0
                run(sp, name, lambda i: [load(name, i, j) for j in range(count)], load_rest)
            for r in range(2):
                sp.wait_ge(S["fin_act"], 2 * r + 2)
                sp.wait_ge(S["fin_dve"], 2 * r + 2)
                sp.dma_start(out[0, 128 * r:128 * r + 128], rows[:, r]).then_inc(S["out_done"], 16)
            sp.wait_ge(S["out_done"], 32)

        @block.gpsimd
        def _(pool):
            pool.nop().then_inc(S["kv_free"], 1)

            def spill(i):
                pool.wait_ge(S["v_rows_taken"], i * 4 + 4)
                pool.dma_start(kv_spill[i], kv[:]).then_inc(S["kv_spilled"], 16)
                pool.wait_ge(S["kv_spilled"], i * 16 + 16)
                pool.nop().then_inc(S["kv_free"], 1)
            run(pool, "mem", spill)
            pool.wait_ge(S["x_tile"], 16)
            pool.dma_start(x_spill, xflat).then_inc(S["x_spilled"], 16)
            pool.wait_ge(S["x_spilled"], 16)
            pool.wait_ge(S["ssd_gated"], 4)
            pool.dma_start(xflat[:, 0:2048], x_spill[:, 0:2048]).then_inc(S["x_loaded"], 16)
            pool.wait_ge(S["x_loaded"], 16)
            pool.wait_ge(S["y_ssd"], 4)
            pool.dma_start(xflat[:, 2048:], x_spill[:, 2048:]).then_inc(S["x_loaded"], 16)
            pool.wait_ge(S["y_mem"], 4)
            pool.dma_start(kv[:], kv_spill[0]).then_inc(S["kv_loaded"], 16)
            pool.dma_start(pos_i, pos).then_inc(S["pos_loaded"], 16)
            pool.wait_ge(S["h_ready"], 16)
            pool.dma_start(x_spill, xflat).then_inc(S["x_spilled"], 16)
            pool.wait_ge(S["x_spilled"], 32)
            pool.wait_ge(S["y_mem"], 8)
            pool.dma_start(mask, mla_mask).then_inc(S["mask_loaded"], 16)
            pool.dma_start(xflat[:, 0:2048], x_spill[:, 0:2048]).then_inc(S["x_loaded"], 16)
            pool.wait_ge(S["x_loaded"], 48)

            def mla_body(i):
                pool.wait_ge(evacuated, outputs("mla", i)(2, 1 + NB))
                for h in range(4):
                    a, b = 32 * h, 32 * (h ^ 1)
                    ins = nc.gpsimd.tensor_tensor(qro[a:a + 32], qr[b:b + 32], sinT[b:b + 32], ALU.mult)
                ins.then_inc(S["rope_turned"], 1)
            run(pool, "mla", mla_body)
            pool.wait_ge(S["y_mla"], 8)
            pool.dma_start(xflat[:, 2048:], x_spill[:, 2048:]).then_inc(S["x_loaded"], 16)
            pool.dma_start(cs_r, ret_tab).then_inc(S["ret_tab_loaded"], 16)
            pool.dma_start(dec, ret_decay[0]).then_inc(S["decay_loaded"], 16)
            last = RET_HEADS
            with pool.Fori(1, last) as h:
                pool.wait_ge(S["decay_used"], h * 1)
                pool.dma_start(dec, ret_decay[h]).then_inc(S["decay_loaded"], 16)
            pool.wait_ge(S["decay_loaded"], 16 * last)
            pool.wait_ge(S["kv_loaded"], 16)

        @block.scalar
        def _(act):
            A = nc.scalar.activation

            def split(name, i, j, h):
                it = part(name, i, j, h)
                if it:
                    c, p, s, a, b = it
                    act.wait_ge(loaded[c.slot(p, 4)], c.filled(p))
                    if h == 0 or (name in ("out0", "out1") and j % 2 == 0):
                        act.wait_ge(half_started, c.half(p - 2, h, 1))
                    A(w_hi[:, s, 0:b - a, :], raw[:, c.slot(p, 4), a:b, :], ACT.Copy).then_inc(hi_ready, 1)

            def copy_half(name, i, o, weight=1):
                c = outputs(name, i)
                act.wait_ge(output_ready, c(o, 1))
                A(half[:, c.slot(o, NB)], pj[:, c.slot(o, NB), 0:T], ACT.Copy).then_inc(half_copied, weight)

            def rsqrt(k, v, y):
                act.wait_ge(S["var_ready"], k)
                A(y, v, ACT.Ln)
                act.drain()
                A(y, y, ACT.Exp, scale=-0.5).then_inc(S["rsqrt_ready"], 1)

            act.dma_start(vec[:], vecs).then_inc(S["tables"], 16)
            act.dma_start(con[:], consts).then_inc(S["tables"], 16)
            act.dma_start(wdt[:], w_dt).then_inc(S["tables"], 16)
            act.dma_start(rows, x.rearrange("b (r p) c -> p (b r) c", p=P)).then_inc(S["x_rows"], 16)

            def row_square(k, src, r):
                junk = hs[:, 8 * k + 4 * r:8 * k + 4 * r + 4].rearrange("p a b c -> p (a b c)")
                A(junk, src[:, r], ACT.Square, accum_out=ss[:, 2 * k + r:2 * k + r + 1])

            def row_rsqrt(k, var, rsqrt_):
                act.wait_ge(S[var], 1)
                A(rs4[:, 2 * k:2 * k + 2], var4[:, 2 * k:2 * k + 2], ACT.Ln)
                act.drain()
                A(rs4[:, 2 * k:2 * k + 2], rs4[:, 2 * k:2 * k + 2], ACT.Exp, scale=-0.5).then_inc(S[rsqrt_], 1)

            def hi_columns(g, dst, w):
                act.wait_ge(S["transposed"], g + 1)
                for u in range(2):
                    c = 2 * (g % 8) + u
                    A(dst[:, c, 0], mx[:, g % 6, T * u:T * (u + 1)], ACT.Copy, scale=V(w, c)).then_inc(S["part_hi"], 1)

            act.wait_ge(S["mem_rows"], 16)
            for r in range(2):
                row_square(0, mem_rows, r)
            act.drain().then_inc(S["mem_squares"], 1)
            row_rsqrt(0, "mem_var", "mem_rsqrt")
            for s in range(4):
                act.wait_ge(loaded[s // 2], 16)
                A(w_hi[:, s], raw[:, s // 2, HALF * (s % 2):HALF * (s % 2) + HALF], ACT.Copy).then_inc(hi_ready, 1)
            act.wait_ge(S["tables"], 48)
            for g in range(8):
                hi_columns(g, ys, "mem_norm")

            def mem_body(i):
                for j in range(8):
                    split("mem", i, j, 0)
                    copy_half("mem", i, j)
                    split("mem", i, j, 1)
                    if i == 0 and j < 2:
                        act.wait_ge(S["x_rows"], 16)
                        row_square(1, rows, j)
                        if j == 1:
                            act.drain().then_inc(S["x_squares"], 1)
                    if i == 0 and j == 2:
                        row_rsqrt(1, "x_var", "x_rsqrt")
                    if i == 1 and j < 4:
                        hi_columns(16 + 2 * j, hs, "norm0")
                        hi_columns(17 + 2 * j, hs, "norm0")
                    if j >= 5:
                        value_rows(i, j - 5)
                value_rows(i, 3)

            def value_rows(i, n):
                act.wait_ge(S["v_rows"], i * 4 + n + 1)
                A(values[:, :, 128 * n:128 * n + 128], mx[:, n, 0:256].rearrange("p (m c) -> p m c", m=2),
                  ACT.Copy).then_inc(S["v_rows_taken"], 1)
            for i in range(2):
                mem_body(i)

            def gate_body(i):
                for j in range(4):
                    if j == 1:
                        act.wait_ge(evacuated, outputs("gate", i)(0, 1 + NB))
                        A(th_g, z_g, ACT.Tanh, scale=0.5).then_inc(S["gate_tanh"], 1)
                    split("gate", i, j, 0)
                    copy_half("gate", i, j)
                    split("gate", i, j, 1)
            run(act, "gate", gate_body)

            act.wait_ge(S["dt_exp_in"], 1)
            A(dtw[2], dtw[1], ACT.Exp)
            A(ea, vec[:, VEC["a_log"][0]:VEC["a_log"][1]], ACT.Exp)
            act.drain().then_inc(S["dt_exp"], 1)

            def gate_out_body(i):
                for j in range(4):
                    split("gate_out", i, j, 0)
                    copy_half("gate_out", i, 2 * j)
                    copy_half("gate_out", i, 2 * j + 1)
                    split("gate_out", i, j, 1)
            run(act, "gate_out", gate_out_body)
            act.wait_ge(S["dte_logits"], 1)
            A(dte, mx[:, 1, 0:32], ACT.Exp).then_inc(S["dte_ready"], 1)

            def residual(name, ppo):
                gains, column_gain = NEXT.get(name, ([], None))

                def body(i):
                    for j in range(len(PHASES[name][0])):
                        split(name, i, j, 0)
                        if j % ppo == ppo - 1:
                            o = j // ppo
                            copy_half(name, i, o)
                        split(name, i, j, 1)
                        if j % ppo == ppo - 1:
                            if gains:
                                act.wait_ge(S["x_tile"], i * 4 + (RES[name] + o + 1))
                            for k, gain in enumerate(gains):
                                ins = A(sq[k][o % 2], xT[:, i * 4 + o], ACT.Square, scale=dyn(gain, i, o))
                                if k == len(gains) - 1:
                                    ins.then_inc(S["x_square"], 1)
                            if column_gain:
                                A(hs[:, i * 4 + o, 0], xT[:, i * 4 + o], ACT.Copy,
                                  scale=dyn(column_gain, i, o)).then_inc(S["h_hi"], 1)
                run(act, name, body)

            def dyn(gain, i, o):
                return 1.0 if gain is None else vec[:, bass.ds(i * 4 + (VEC[gain][0] + o), 1)]

            def mem_exp(c, heads, scores, probs, vh, values_):
                for u in range(heads):
                    A(vh[u].rearrange("p (m c) -> p m c", m=2), values_(u), ACT.Copy)
                    act.wait_ge(S["mem_shift"], c(u, 1))
                    for q in range(2):
                        A(probs[u][:, T * q:T * q + T], scores(u)[:, T * q:T * q + T], ACT.Exp, scale=MEM_SCALE,
                          bias=mstat[:, 4 * u + q:4 * u + q + 1], accum_out=mstat[:, 4 * u + 2 + q:4 * u + 3 + q])
                    act.drain().then_inc(S["mem_probs"], 1)

            def ssd_body(i):
                O = outputs("ssd", i)
                M = Count(0, 1, i)
                for j in range(12):
                    if 2 <= j <= 7:
                        w = VEC["ssd_conv"][0] + 5 * (j - 2)
                        act.wait_ge(evacuated, O(j - 1, 1 + NB))
                        A(th[j % 2], cp[j % 2][:, 0:256], ACT.Identity, scale=vec[:, bass.ds(i * 30 + w, 1)],
                          bias=vec[:, bass.ds(i * 30 + (w + 4), 1)]).then_inc(S["conv_begun"], 1)
                    if 2 <= j <= 5:
                        act.wait_ge(S["seg_ready"], i * 4 + (j - 1))
                        A(em[j - 2], mx[:, 1 + j % 2], ACT.Exp).then_inc(S["decay_ready"], 1)
                    if j == 2:
                        mem_exp(M, 1, lambda u: mx[:, 3], [probs_s], [vh_s],
                                lambda u: values[:, :, bass.ds(i * 128, 128)])
                    if j == 5:
                        act.wait_ge(S["mem_pt"], M(0, 1))
                        A(pt_s, mx[:, 4], ACT.Copy).then_inc(S["mem_pt_copied"], 1)
                    if j == 5:
                        act.wait_ge(S["cb_ready"], i * 1 + 1)
                        A(brow, mx[:, 0, 256:384], ACT.Copy).then_inc(S["brow_ready"], 1)
                    if j == 7:
                        act.wait_ge(S["eq_logits"], i * 1 + 1)
                        A(eqx, mx[:, 2], ACT.Exp).then_inc(S["eq_ready"], 1)
                    if j >= 8:
                        act.wait_ge(evacuated, O(j - 1, 1 + NB))
                        A(sz[:, j - 8], cp[j % 2][:, 3:259], ACT.Tanh, scale=0.5).then_inc(S["z_tanh"], 1)
                    if j == 10:
                        act.wait_ge(S["state_ready"], i * 1 + 1)
                        A(state, mx[:, 5], ACT.Copy).then_inc(S["state_copied"], 1)
                    if j == 11:
                        act.wait_ge(S["ssd_gated"], i * 1 + 1)
                        A(ssq, xs, ACT.Square).then_inc(S["ssd_squares"], 1)
                    split("ssd", i, j, 0)
                    if 2 <= j <= 7:
                        act.wait_ge(S["conv_done"], i * 6 + (j - 1))
                        A(th[j % 2], cv[j % 2], ACT.Tanh).then_inc(S["conv_tanh"], 1)
                    copy_half("ssd", i, j)
                    split("ssd", i, j, 1)
                act.wait_ge(evacuated, O(11, 1 + NB))
                A(th0, cv0, ACT.Tanh, scale=0.5).then_inc(S["mz_tanh"], 1)
                rsqrt(i * 1 + 1, em[0][:, 0:256], em[0][:, 256:512])
            act.wait_ge(S["x_spilled"], 16)
            run(act, "ssd", ssd_body)
            residual("out0", 2)
            rsqrt(NORM["b_latent"] + 1, nv, ny)

            def copy_body(name):
                def body(i):
                    for j in range(len(PHASES[name][0])):
                        split(name, i, j, 0)
                        copy_half(name, i, j)
                        split(name, i, j, 1)
                return body
            run(act, "latent", copy_body("latent"))
            act.wait_ge(S["angle_ready"], 1)
            A(sinT, ang, ACT.Sin)
            A(cosT, ang, ACT.Sin, scale=0.5)
            act.drain().then_inc(S["sin_ready"], 1)
            for j in range(3):
                if j == 2:
                    act.wait_ge(S["x_spilled"], 32)
                    act.wait_ge(S["latent_ready"], 1)
                    A(lsq, lraw, ACT.Square).then_inc(S["latent_squares"], 1)
                split("latent_tail", 0, j, 0)
                copy_half("latent_tail", 0, j)
                split("latent_tail", 0, j, 1)
            rsqrt(NORM["kv"] + 1, *norm_kv[0:2])
            rsqrt(NORM["q"] + 1, *norm_q[0:2])

            def memq_body(i):
                O = outputs("memq", i)
                M = Count(4, 2, i)
                for j in range(4):
                    if j == 3:
                        mem_exp(M, 2, lambda u: mx[:, u], [p_m[:, 0:512], p_m[:, 512:1024]],
                                [vh_m[:, 0:256], vh_m[:, 256:512]],
                                lambda u: values[:, :, bass.ds(i * 256 + 128 * u, 128)])
                    split("memq", i, j, 0)
                    copy_half("memq", i, j)
                    if j < 3:
                        split("memq", i, j, 1)
                act.wait_ge(evacuated, O(3, 1 + NB))
                A(mt_m, mz_m, ACT.Tanh, scale=0.5).then_inc(S["mz_tanh"], 1)
                for u in range(2):
                    act.wait_ge(S["mem_pt"], M(u, 1))
                    A(pt_m[:, 512 * u:512 * u + 512], mx[:, 2 + u], ACT.Copy).then_inc(S["mem_pt_copied"], 1)
                split("memq", i, 3, 1)
            act.wait_ge(S["kv_loaded"], 16)
            run(act, "memq", memq_body)
            def mla_body(i):
                O = outputs("mla", i)
                for j in range(8):
                    if j == 6:
                        act.wait_ge(S["mla_shift"], i * 1 + 1)
                        for u in range(2):
                            for q, a, b in ((0, 0, 128), (1, 128, 384)):
                                k = 2 * u + q
                                e = s_[:, 384 * u + a:384 * u + b]
                                A(e, e, ACT.Exp, scale=MLA_SCALE, bias=pstat[:, k:k + 1],
                                  accum_out=pstat[:, 4 + k:5 + k])
                        act.drain().then_inc(S["mla_probs"], 1)
                    if j == 7:
                        act.wait_ge(S["mla_vt"], i * 1 + 1)
                        A(vrow_, mx[:, 2], ACT.Copy).then_inc(S["mla_vrow"], 1)
                        act.wait_ge(S["mla_pt"], i * 1 + 1)
                        A(pt_.rearrange("p (u c) -> p u c", u=2), mx[:, 3:5, 0:384],
                          ACT.Copy).then_inc(S["mla_pt_copied"], 1)
                    if j != 3:
                        split("mla", i, j, 0)
                    if j == 3:
                        copy_half("mla", i, 3)
                        copy_half("mla", i, 4)
                        split("mla", i, j, 0)
                    elif j == 7:
                        copy_half("mla", i, 8, 2)
                    else:
                        copy_half("mla", i, j if j < 3 else j + 1)
                    split("mla", i, j, 1)
                act.wait_ge(evacuated, O(8, 2 + NB))
                A(zt_, zz_, ACT.Tanh, scale=0.5).then_inc(S["mla_tanh"], 1)
            run(act, "mla", mla_body)
            residual("out1", 2)
            rsqrt(NORM["b_final"] + 1, nv, ny)
            rsqrt(NORM["b_ret"] + 1, nv, ny)

            def ret_body(name, first):
                def body(i):
                    O = outputs(name, i)
                    for j in range(12):
                        if 6 <= j <= 9:
                            n = j - 6
                            act.wait_ge(S["ret_vt"], i * 4 + (4 * first + n + 1))
                            for k in range(2):
                                ins = A(vrow_r[:, k, 128 * n:128 * n + 128], mx[:, 1 + n % 2, 128 * k:128 * k + 128],
                                        ACT.Copy, scale=rstd[:, 256 + k:257 + k],
                                        accum_out=v_sum[:, 4 * k + n:4 * k + n + 1])
                            ins.then_inc(S["ret_vrow"], 1)
                        if j == 10:
                            act.wait_ge(S["ret_pv"], i * 1 + (first + 1))
                            o_psum = mx[:, 3:5].rearrange("p b c -> p (b c)")
                            A(gen[:, 0:1024], o_psum, ACT.Square).then_inc(S["ret_squares"], 1)
                            A(kv[:, 0:1024], o_psum, ACT.Copy).then_inc(S["ret_o"], 1)
                        if j >= 9:
                            n = j - 9
                            act.wait_ge(evacuated, O(j - 1, 1 + NB))
                            A(th_r[:, T * (n % 2):T * (n % 2) + T], sg_r[:, n], ACT.Tanh,
                              scale=0.5).then_inc(S["ret_tanh"], 1)
                        if j == 11:
                            rsqrt(i * 1 + (NORM[name] + 1), vt_r[:, 0:256], vt_r[:, 256:512])
                        split(name, i, j, 0)
                        copy_half(name, i, j)
                        split(name, i, j, 1)
                    act.wait_ge(evacuated, O(11, 1 + NB))
                    A(th_r[:, T:2 * T], sg_r[:, 3], ACT.Tanh, scale=0.5).then_inc(S["ret_tanh"], 1)
                run(act, name, body)

            for ph, first in (("ret_a", 0), ("ret_b", 4)):
                ret_body(ph, first)
                residual("ret_out" + ph[3:], 1)
            rsqrt(NORM["b_mlp"] + 1, nv, ny)
            for b in range(FF_BLOCKS):
                def up_body(i):
                    for j in range(4):
                        split(f"up{b}", i, j, 0)
                        copy_half(f"up{b}", i, j)
                        split(f"up{b}", i, j, 1)
                run(act, f"up{b}", up_body)
                residual(f"down{b}", 1)
            rsqrt(NORM["b_out"] + 1, nv[:, 256:258], ny[:, 256:258])
            act.wait_ge(S["fin_scale"], 1)
            for g in range(1, 8, 2):
                act.wait_ge(S["fin_rows"], g + 1)
                A(rows[:, g // 4, 512 * (g % 4):512 * (g % 4) + 512], fin_bank(g), ACT.Copy,
                  scale=rstd[:, 256 + g // 4:257 + g // 4]).then_inc(S["fin_act"], 1)
        @block.vector
        def _(dve):
            v = nc.vector
            TT, TS, STT = v.tensor_tensor, v.tensor_scalar, v.scalar_tensor_tensor

            def split(name, i, j, h):
                it = part(name, i, j, h)
                if it:
                    c, p, s, a, b = it
                    dve.wait_ge(hi_ready, c.half(p, h))
                    TT(w_lo[:, s, 0:b - a, :], raw[:, c.slot(p, 4), a:b, :], w_hi[:, s, 0:b - a, :].bitcast(F32),
                       ALU.subtract).then_inc(split_ready, 1)

            def evac(name, i, o, dst, weight=1, scale=None, via=None):
                c = outputs(name, i)
                dve.wait_ge(half_copied, c(o, 1))
                k = c.slot(o, NB)
                if scale is None:
                    TT(dst, pj[:, k, T:2 * T], half[:, k], ALU.add).then_inc(evacuated, weight)
                else:
                    via = dst if via is None else via
                    TT(via, pj[:, k, T:2 * T], half[:, k], ALU.add)
                    dve.drain()
                    TT(dst, via, scale, ALU.mult).then_inc(evacuated, weight)

            def hi_lo(dst, src):
                dve.drain()
                v.tensor_copy(dst[0], src)
                dve.drain()
                return TT(dst[1], src, dst[0].bitcast(F32), ALU.subtract)

            def newton(vv, y, t, out_, s=1.0):
                TT(t, y, y, ALU.mult)
                dve.drain()
                TT(t, t, vv, ALU.mult)
                dve.drain()
                TS(t, t, -0.5, 1.5, ALU.mult, ALU.add)
                dve.drain()
                ins = TT(out_, y, t, ALU.mult)
                dve.drain()
                return ins

            def variance(k, bank, n, vv, a=0, b=T):
                dve.wait_ge(S["stat_ready"], k)
                TS(vv, mx[:, bank, a:b], 1.0 / n, EPS, ALU.mult, ALU.add).then_inc(S["var_ready"], 1)

            def inverse_rms(k, bank, n, vv, y, t, out_, a=0, b=T):
                variance(k, bank, n, vv, a, b)
                dve.wait_ge(S["rsqrt_ready"], k)
                newton(vv, y, t, out_)

            v.nop().then_inc(evacuated, NB)

            def row_variance(k, squares, var):
                dve.wait_ge(S[squares], 1)
                TS(var4[:, 2 * k:2 * k + 2], ss[:, 2 * k:2 * k + 2], 1.0 / D, EPS, ALU.mult,
                   ALU.add).then_inc(S[var], 1)

            def row_inverse(k, rsqrt):
                dve.wait_ge(S[rsqrt], 1)
                newton(*(w[:, 2 * k:2 * k + 2] for w in (var4, rs4, tmp4, rs4)))

            def row_scale(k, src, r):
                return TS(src[:, r], src[:, r], rs4[:, 2 * k + r:2 * k + r + 1], None, ALU.mult)

            def lo_columns(g, dst, w):
                for u in range(2):
                    c = 2 * (g % 8) + u
                    dve.wait_ge(S["part_hi"], 16 * (g >= 16) + 2 * (g % 8) + 2)
                    STT(out=dst[:, c, 1], in0=mx[:, g % 6, T * u:T * u + T], scalar=V(w, c),
                        in1=dst[:, c, 0].bitcast(F32), op0=ALU.mult, op1=ALU.subtract).then_inc(S["part_taken"], 1)

            row_variance(0, "mem_squares", "mem_var")
            row_inverse(0, "mem_rsqrt")
            for r in range(2):
                ins = row_scale(0, mem_rows, r)
            ins.then_inc(S["mem_scaled"], 1)
            for s in range(4):
                dve.wait_ge(hi_ready, s + 1)
                TT(w_lo[:, s], raw[:, s // 2, HALF * (s % 2):HALF * (s % 2) + HALF], w_hi[:, s].bitcast(F32),
                   ALU.subtract).then_inc(split_ready, 1)
            for g in range(8):
                lo_columns(g, ys, "mem_norm")

            def mem_body(i):
                for j in range(8):
                    if j == 0:
                        dve.wait_ge(S["kv_free"], i * 1 + 1)
                    if j >= 6:
                        dve.wait_ge(S["v_rows"], i * 4 + (j - 5))
                    split("mem", i, j, 0)
                    evac("mem", i, j, keys[:, j] if j < 4 else vt[j % 2])
                    split("mem", i, j, 1)
                    for g in (8 + 8 * i + 2 * j, 9 + 8 * i + 2 * j) if j < 4 else ():
                        if i == 0:
                            dve.wait_ge(S["transposed"], g + 1)
                            v.tensor_copy(xT[:, 2 * g - 16:2 * g - 14].rearrange("p a t -> p (a t)"),
                                          mx[:, g % 6]).then_inc(S["part_taken"], 2)
                        else:
                            lo_columns(g, hs, "norm0")
                    if i == 0 and j == 2:
                        row_variance(1, "x_squares", "x_var")
                    if i == 0 and j == 3:
                        row_inverse(1, "x_rsqrt")
                    if i == 0 and j in (4, 5):
                        ins = row_scale(1, rows, j - 4)
                        if j == 5:
                            ins.then_inc(S["x_scaled"], 1)
            for i in range(2):
                mem_body(i)

            v.memset(u_g[:, 0:2], 0.0)
            a, b, c = (vec[:, VEC[n][0]:VEC[n][1]] for n in ("final", "norm1_2", "final_norm1_2"))
            TT(c, a, b, ALU.mult)
            a_v = VEC["ssd_conv"][0]
            TS(vec[:, a_v:a_v + 30 * GROUPS], vec[:, a_v:a_v + 30 * GROUPS], 0.5, None, ALU.mult)

            def gate_body(i):
                w0 = VEC["gate_conv"][0]

                def tap(k):
                    return vec[:, bass.ds(i * 3 + (w0 + k), 1)]
                split("gate", i, 0, 0)
                evac("gate", i, 0, z_g)
                split("gate", i, 0, 1)
                split("gate", i, 1, 0)
                evac("gate", i, 1, c_g)
                split("gate", i, 1, 1)
                dve.wait_ge(S["gate_tanh"], i * 1 + 1)
                STT(out=s_g, in0=th_g, scalar=1.0, in1=z_g, op0=ALU.add, op1=ALU.mult)
                split("gate", i, 2, 0)
                evac("gate", i, 2, v_g)
                split("gate", i, 2, 1)
                dve.drain()
                TT(u_g[:, 2:258], c_g, v_g, ALU.mult)
                dve.drain()
                TS(a_g, u_g[:, 0:256], tap(0), None, ALU.mult)
                dve.drain()
                STT(out=e_g, in0=u_g[:, 1:257], scalar=tap(1), in1=a_g, op0=ALU.mult, op1=ALU.add)
                dve.drain()
                STT(out=a_g, in0=u_g[:, 2:258], scalar=tap(2), in1=e_g, op0=ALU.mult, op1=ALU.add)
                split("gate", i, 3, 0)
                evac("gate", i, 3, b_g)
                split("gate", i, 3, 1)
                dve.drain()
                STT(out=e_g, in0=a_g, scalar=0.5, in1=b_g, op0=ALU.mult, op1=ALU.mult)
                dve.drain()
                TT(a_g, e_g, s_g, ALU.mult)
                hi_lo((ys[:, i, 0], ys[:, i, 1]), a_g).then_inc(S["y_gate"], 1)
            run(dve, "gate", gate_body)

            zt, mn, ex, den, s1, zz, pp, tt = dtw
            dve.wait_ge(S["dt_logits"], 1)
            b0 = VEC["dt_bias"][0]
            TT(zt, mx[:, 0, 0:64].rearrange("p (c h) -> p c h", c=2),
               vec[:, b0:b0 + 32].unsqueeze(1).to_broadcast([P, 2, 32]), ALU.add)
            dve.drain()
            TS(tt, zt, -1.0, None, ALU.mult)
            dve.drain()
            TT(mn, zt, tt, ALU.min).then_inc(S["dt_exp_in"], 1)
            dve.wait_ge(S["dt_exp"], 1)
            TS(den, ex, 2.0, None, ALU.add)
            dve.drain()
            v.reciprocal(den, den)
            dve.drain()
            TT(s1, ex, den, ALU.mult)
            dve.drain()
            TT(zz, s1, s1, ALU.mult)
            dve.drain()
            TS(pp, zz, 1.0 / 15, None, ALU.mult)
            dve.drain()
            for k in (13, 11, 9, 7, 5, 3):
                STT(out=pp, in0=pp, scalar=1.0 / k, in1=zz, op0=ALU.add, op1=ALU.mult)
                dve.drain()
            STT(out=pp, in0=pp, scalar=1.0, in1=s1, op0=ALU.add, op1=ALU.mult)
            TS(zt, zt, 0.0, None, ALU.max)
            dve.drain()
            STT(out=dt, in0=pp, scalar=2.0, in1=zt, op0=ALU.mult, op1=ALU.add)
            dve.drain()
            STT(out=da, in0=dt, scalar=-1.0, in1=ea.unsqueeze(1).to_broadcast([P, 2, 32]), op0=ALU.mult,
                op1=ALU.mult).then_inc(S["dt_ready"], 1)

            def residual(name, ppo, opp=1, x_all=None):
                gains, column_gain = NEXT.get(name, ([], None))
                n_out = outs_per.get(name, len(PHASES[name][0]))
                for k in range(len(gains)):
                    dve.drain()
                    v.memset(acc[k], 0.0)

                def body(i):
                    def column(gain, o):
                        return vec[:, bass.ds(i * 4 + (VEC[gain][0] + o), 1)]
                    for j in range(len(PHASES[name][0])):
                        o = j // ppo * opp
                        split(name, i, j, 0)
                        if x_all and j == len(PHASES[name][0]) - 1:
                            dve.wait_ge(S["x_loaded"], x_all)
                        if j % ppo == ppo - 1:
                            for u in range(opp):
                                if u:
                                    dve.drain()
                                evac(name, i, o + u, res[(o + u) % 2])
                                dve.drain()
                                xo = xT[:, i * n_out + (o + u)]
                                TT(xo, xo, res[(o + u) % 2], ALU.add).then_inc(S["x_tile"], 1)
                        split(name, i, j, 1)
                        if j % ppo == ppo - 1 and gains:
                            dve.wait_ge(S["x_square"], i * 4 + (SQ[name] + o + 1))
                            for k in range(len(gains)):
                                TT(acc[k], acc[k], sq[k][o % 2], ALU.add)
                            if column_gain:
                                dve.wait_ge(S["h_hi"], i * 4 + (SQ[name] + o + 1))
                                STT(out=hs[:, i * 4 + o, 1], in0=xT[:, i * 4 + o], scalar=column(column_gain, o),
                                    in1=hs[:, i * 4 + o, 0].bitcast(F32), op0=ALU.mult,
                                    op1=ALU.subtract).then_inc(S["h_ready"], 1)
                            if name == LAST:
                                TS(xT[:, i * 4 + o], xT[:, i * 4 + o], column("final_2", o), None,
                                   ALU.mult).then_inc(S["h_ready"], 1)
                run(dve, name, body)
                if gains:
                    dve.drain().then_inc(S["acc_ready"], 1)

            residual("gate_out", 1, 2)

            def softmax_shift(M, heads, scores):
                for u in range(heads):
                    dve.wait_ge(S["mem_scores"], M(u, 1))
                    v.reduce_max(mstat[:, 4 * u:4 * u + 2], scores(u).rearrange("p (q k) -> p q k", q=2), AX.X)
                    dve.drain()
                    TS(mstat[:, 4 * u:4 * u + 2], mstat[:, 4 * u:4 * u + 2], -MEM_SCALE, None,
                       ALU.mult).then_inc(S["mem_shift"], 1)

            def softmax_scale(M, heads, probs):
                for u in range(heads):
                    dve.wait_ge(S["mem_probs"], M(u, 1))
                    v.reciprocal(mstat[:, 4 * u + 2:4 * u + 4], mstat[:, 4 * u + 2:4 * u + 4])
                    dve.drain()
                    for q in range(2):
                        ins = TS(probs[u][:, T * q:T * q + T], probs[u][:, T * q:T * q + T],
                                 mstat[:, 4 * u + 2 + q:4 * u + 3 + q], None, ALU.mult)
                    ins.then_inc(S["mem_scaled_probs"], 1)

            def rope(dst, tmp):
                for h in range(4):
                    a, b = 32 * h, 32 * (h ^ 1)
                    TT(tmp[a:a + 32], dst[b:b + 32], sinT[b:b + 32], ALU.mult)
                dve.drain()
                TT(dst, dst, cosT, ALU.mult)
                dve.drain()
                ins = TT(dst, dst, tmp, ALU.add)
                dve.drain()
                return ins

            dve.drain()
            v.memset(cp0[:, 0:3], 0.0)
            v.memset(cp1[:, 0:3], 0.0)

            def ssd_body(i):
                w0 = VEC["ssd_conv"][0]
                M = Count(0, 1, i)
                xdt_v = [w.rearrange("p (h d) -> p h d", h=8) for w in xdt]

                def conv(n):
                    src, t3, t2 = cp[n % 2], cv[n % 2], th[n % 2]

                    def w(k):
                        return vec[:, bass.ds(i * 30 + (w0 + 5 * n + k), 1)]
                    dve.wait_ge(S["conv_begun"], i * 6 + (n + 1))
                    STT(out=t3, in0=src[:, 1:257], scalar=w(1), in1=t2, op0=ALU.mult, op1=ALU.add)
                    dve.drain()
                    STT(out=t2, in0=src[:, 2:258], scalar=w(2), in1=t3, op0=ALU.mult, op1=ALU.add)
                    dve.drain()
                    STT(out=t3, in0=src[:, 3:259], scalar=w(3), in1=t2, op0=ALU.mult,
                        op1=ALU.add).then_inc(S["conv_done"], 1)

                def silu(n):
                    dve.wait_ge(S["conv_tanh"], i * 6 + (n + 1))
                    dst = (bT, cT, xs[:, 0], xs[:, 1], xs[:, 2], xs[:, 3])[n]
                    ins = STT(out=dst, in0=th[n % 2], scalar=1.0, in1=cv[n % 2], op0=ALU.add, op1=ALU.mult)
                    if n == 1:
                        ins.then_inc(S["bc_ready"], 1)
                    if n == 5:
                        ins.then_inc(S["xs_ready"], 1)

                def seg_rhs(r):
                    if r >= 2:
                        dve.wait_ge(S["seg_ready"], i * 4 + r - 1)
                    TT(rr[r % 2].rearrange("p (h q) -> p h q", h=4),
                       da[:, r // 2, bass.ds(i * 8 + 4 * (r % 2), 4)].unsqueeze(2).to_broadcast([P, 4, 128]),
                       upto.unsqueeze(1).to_broadcast([P, 4, 128]), ALU.mult).then_inc(S["seg_rhs"], 1)

                def mix(r):
                    dve.wait_ge(S["decay_ready"], i * 4 + r + 1)
                    e = em[r].rearrange("p (h q) -> p h q", h=4)
                    c = r // 2
                    TT(e, e, cbm[:, 128 * c:128 * c + 128].unsqueeze(1).to_broadcast([P, 4, 128]),
                       ALU.mult).then_inc(S["mix_ready"], 1)

                def z_gate(n):
                    dve.wait_ge(S["z_tanh"], i * 4 + n + 1)
                    STT(out=sz[:, n], in0=sz[:, n], scalar=1.0, in1=cp[n % 2][:, 3:259], op0=ALU.add, op1=ALU.mult)

                for j in range(12):
                    if j <= 3:
                        seg_rhs(j)
                    if 3 <= j <= 8:
                        silu(j - 3)
                    if 2 <= j <= 7:
                        conv(j - 2)
                    if j == 2:
                        softmax_shift(M, 1, lambda u: mx[:, 3])
                    if j == 3:
                        softmax_scale(M, 1, [probs_s])
                    if j == 5:
                        dve.wait_ge(S["seg_ready"], i * 4 + 3)
                        TT(r0.rearrange("p (h d) -> p h d", h=8),
                           da[:, 1, bass.ds(i * 8, 8)].unsqueeze(2).to_broadcast([P, 8, 64]),
                           ones[:, 0:64].unsqueeze(1).to_broadcast([P, 8, 64]), ALU.mult).then_inc(S["eq_lhs"], 1)
                    if j == 5:
                        dve.wait_ge(S["brow_ready"], i * 1 + 1)
                        TT(cbm.rearrange("p (c q) -> p c q", c=2), mx[:, 0, 0:256].rearrange("p (c q) -> p c q", c=2),
                           upto.unsqueeze(1).to_broadcast([P, 2, 128]), ALU.mult).then_inc(S["cb_taken"], 1)
                        dve.drain()
                    if j == 6:
                        dve.wait_ge(S["mem_pv"], M(0, 1))
                        TS(mo_s, mx[:, 3, 0:256], 0.5, None, ALU.mult)
                    if j in (6, 7):
                        mix(2 * (j - 6))
                        mix(2 * (j - 6) + 1)
                    if j == 9:
                        dve.wait_ge(S["xs_rows"], i * 1 + 1)
                        for c, bank in ((0, 5), (1, 0)):
                            TT(xdt_v[c], mx[:, bank].rearrange("p (h d) -> p h d", h=8),
                               dt[:, c, bass.ds(i * 8, 8)].unsqueeze(2).to_broadcast([P, 8, 64]), ALU.mult)
                        dve.drain()
                        TT(xdte.rearrange("p (h d) -> p h d", h=8), xdt_v[0],
                           dte[:, bass.ds(i * 8, 8)].unsqueeze(2).to_broadcast([P, 8, 64]),
                           ALU.mult).then_inc(S["xdt_ready"], 1)
                    if j >= 8:
                        z_gate(j - 8)
                    if j == 10:
                        dve.wait_ge(S["ydiag_ready"], i * 4 + 4)
                        d0 = VEC["ssd_d"][0]
                        for n in range(4):
                            for c in range(2):
                                w = xs[:, n, 128 * c:128 * c + 128]
                                STT(out=w, in0=w, scalar=vec[:, bass.ds(i * 4 + (d0 + n), 1)],
                                    in1=mx[:, 3 + c, 128 * n:128 * n + 128], op0=ALU.mult, op1=ALU.add)
                    if j == 11:
                        dve.wait_ge(S["yoff_ready"], i * 1 + 1)
                        dve.wait_ge(S["eq_ready"], i * 1 + 1)
                        TT(eqx, mx[:, 0], eqx, ALU.mult)
                        dve.drain()
                        TT(xs[:, :, 128:256], xs[:, :, 128:256], eqx.rearrange("p (a q) -> p a q", a=4), ALU.add)
                        dve.drain()
                        STT(out=xs_, in0=xs_, scalar=0.5, in1=sz_, op0=ALU.mult,
                            op1=ALU.mult).then_inc(S["ssd_gated"], 1)
                    split("ssd", i, j, 0)
                    evac("ssd", i, j, mq_s if j == 0 else cv0 if j == 11 else cp[(j - 1) % 2][:, 3:259])
                    split("ssd", i, j, 1)
                nrm = [em[k // 2][:, 256 * (k % 2):256 * (k % 2) + 256] for k in range(4)]
                variance(i * 1 + 1, 5, 512, nrm[0])
                dve.wait_ge(S["mz_tanh"], i * 1 + 1)
                STT(out=th0, in0=th0, scalar=1.0, in1=cv0, op0=ALU.add, op1=ALU.mult)
                dve.drain()
                TT(cv1, mo_s, th0, ALU.mult)
                hi_lo((ys[:, i, 0], ys[:, i, 1]), cv1).then_inc(S["y_mem"], 1)
                dve.wait_ge(S["rsqrt_ready"], i * 1 + 1)
                newton(*nrm)
                n0 = VEC["ssd_norm"][0]
                for n in range(4):
                    STT(out=xs[:, n], in0=xs[:, n], scalar=vec[:, bass.ds(i * 4 + (n0 + n), 1)], in1=nrm[3],
                        op0=ALU.mult, op1=ALU.mult)
                hi_lo((ys[:, bass.ds(i * 4 + 4, 4), 0], ys[:, bass.ds(i * 4 + 4, 4), 1]), xs).then_inc(S["y_ssd"], 1)
            dve.wait_ge(S["x_spilled"], 16)
            run(dve, "ssd", ssd_body)
            dve.wait_ge(S["x_loaded"], 16)
            residual("out0", 2, x_all=32)
            inverse_rms(NORM["b_latent"] + 1, 0, D, nv, ny, nt, rstd, b=258)

            def latent_body(i):
                for j in range(4):
                    split("latent", i, j, 0)
                    evac("latent", i, j, lraw[:, i * 4 + j], scale=rstd[:, 0:T], via=(krA, krB)[j % 2])
                    split("latent", i, j, 1)
            run(dve, "latent", latent_body)
            dve.wait_ge(S["pos_loaded"], 16)
            v.tensor_copy(tt_, pos_i)
            dve.drain()
            TS(ang, tt_, V("inv_freq"), None, ALU.mult)
            dve.drain()
            TS(kk_, ang, float(np.float32(1 / (2 * np.pi))), 12582912.0, ALU.mult, ALU.add)
            dve.drain()
            TS(kk_, kk_, -12582912.0, None, ALU.add)
            two_pi = 2 * np.pi
            c1 = 6.28125
            c2 = float(np.float32(np.round((two_pi - c1) * 2 ** 22) / 2 ** 22))
            c3 = float(np.float32(two_pi - c1 - c2))
            for cc in (c1, c2, c3):
                dve.drain()
                STT(out=ang, in0=kk_, scalar=-cc, in1=ang, op0=ALU.mult, op1=ALU.add)
            dve.drain()
            pi = float(np.nextafter(np.float32(np.pi), np.float32(0)))
            TS(ang, ang, pi, -pi, ALU.min, ALU.max).then_inc(S["angle_ready"], 1)
            dve.wait_ge(S["sin_ready"], 1)
            TT(cosT, cosT, cosT, ALU.mult)
            TS(sinT, sinT, V("sin_sign"), None, ALU.mult)
            dve.drain()
            TS(cosT, cosT, -2.0, 1.0, ALU.mult, ALU.add)
            dve.drain()
            for j in range(3):
                if j == 2:
                    dve.drain().then_inc(S["latent_ready"], 1)
                split("latent_tail", 0, j, 0)
                evac("latent_tail", 0, j, lraw[:, 8 + j] if j < 2 else krA, scale=rstd[:, 0:T])
                split("latent_tail", 0, j, 1)
            variance(NORM["kv"] + 1, 0, 512, norm_kv[0])
            variance(NORM["q"] + 1, 1, 768, norm_q[0])
            dve.drain()
            rope(krA, rope_t)
            v.tensor_copy(krB[64:128], krA[64:128])
            v.memset(krB[0:64], 0.0)
            dve.drain()
            v.memset(krA[64:128], 0.0).then_inc(S["krope_ready"], 1)
            dve.wait_ge(S["rsqrt_ready"], NORM["kv"] + 1)
            newton(*norm_kv)
            for c in range(4):
                STT(out=lraw[:, c], in0=lraw[:, c], scalar=V("kv_norm", c), in1=norm_kv[3], op0=ALU.mult,
                    op1=ALU.mult)
            hi_lo((lat[:, 0:4, 0], lat[:, 0:4, 1]), lraw[:, 0:4]).then_inc(S["lat_ready"], 1)
            dve.wait_ge(S["rsqrt_ready"], NORM["q"] + 1)
            newton(*norm_q)

            def normalise_q(c):
                STT(out=lraw[:, c], in0=lraw[:, c], scalar=vec[:, bass.ds(c + VEC["kv_norm"][0], 1)],
                    in1=lrstd, op0=ALU.mult, op1=ALU.mult)
                yy = lat[:, c]
                hi_lo((yy[:, 0], yy[:, 1]), lraw[:, c]).then_inc(S["lat_ready"], 1)

            def memq_body(i):
                M = Count(4, 2, i)
                for j in range(4):
                    if j < 3:
                        normalise_q(i * 3 + (4 + j))
                    if j == 3:
                        softmax_shift(M, 2, lambda u: mx[:, u])
                        softmax_scale(M, 2, [p_m[:, 0:512], p_m[:, 512:1024]])
                    split("memq", i, j, 0)
                    evac("memq", i, j, (mq_m, mz_m)[j // 2][:, T * (j % 2):T * (j % 2) + T], scale=rstd[:, 0:T])
                    if j < 3:
                        split("memq", i, j, 1)
                dve.wait_ge(S["mz_tanh"], i * 1 + 5)
                STT(out=mz_m, in0=mt_m, scalar=1.0, in1=mz_m, op0=ALU.add, op1=ALU.mult)
                dve.drain()
                dve.wait_ge(S["mem_pv"], M(1, 1))
                STT(out=mt_m.rearrange("p (u t) -> p u t", u=2), in0=mx[:, 4:6, 0:256], scalar=0.5,
                    in1=mz_m.rearrange("p (u t) -> p u t", u=2), op0=ALU.mult, op1=ALU.mult)
                yy = ys[:, bass.ds(i * 2, 2)]
                hi_lo((yy[:, :, 0], yy[:, :, 1]), mt_m.rearrange("p (u t) -> p u t", u=2)
                      ).then_inc(S["y_mem"], 2)
                split("memq", i, 3, 1)
            run(dve, "memq", memq_body)
            dve.wait_ge(S["mask_loaded"], 16)
            s3 = s_.rearrange("p (u c) -> p u c", u=2)

            def mla_body(i):
                for j in range(8):
                    if j == 5:
                        dve.wait_ge(S["mla_scores"], i * 1 + 1)
                        TT(s3, mx[:, 0:2, 0:384], mask.unsqueeze(1).to_broadcast([P, 2, 384]), ALU.add)
                        dve.drain()
                        pm = pstat[:, 0:4].rearrange("p (u q) -> p u q", u=2)
                        v.reduce_max(pm[:, :, 0], s3[:, :, 0:128], AX.X)
                        v.reduce_max(pm[:, :, 1], s3[:, :, 128:384], AX.X)
                        dve.drain()
                        TS(pstat[:, 0:4], pstat[:, 0:4], -MLA_SCALE, None, ALU.mult).then_inc(S["mla_shift"], 1)
                    if j == 6:
                        dve.wait_ge(S["mla_probs"], i * 1 + 1)
                        v.reciprocal(pstat[:, 8:12], pstat[:, 4:8])
                        dve.drain()
                        for u in range(2):
                            for q, a, b in ((0, 0, 128), (1, 128, 384)):
                                k = 8 + 2 * u + q
                                e = s_[:, 384 * u + a:384 * u + b]
                                ins = TS(e, e, pstat[:, k:k + 1], None, ALU.mult)
                        ins.then_inc(S["mla_probs_scaled"], 1)
                    if j != 3:
                        split("mla", i, j, 0)
                    if j == 3:
                        evac("mla", i, 3, kn[0])
                        evac("mla", i, 4, kn[1])
                        split("mla", i, j, 0)
                        dve.wait_ge(S["rope_turned"], i * 1 + 1)
                        TT(qr, qr, cosT, ALU.mult)
                        dve.drain()
                        TT(qr, qr, qro, ALU.add)
                        dve.drain().then_inc(S["qk_ready"], 1)
                    elif j == 7:
                        evac("mla", i, 8, zz_[:, 256:512], 2, scale=rstd[:, 0:T])
                    else:
                        evac("mla", i, j if j < 3 else j + 1,
                             (qn[0], qn[1], qr, None, vtm[0], vtm[1], zz_[:, 0:256])[j],
                             scale=rstd[:, 0:T] if j == 6 else None)
                    split("mla", i, j, 1)
                dve.wait_ge(S["mla_tanh"], i * 1 + 1)
                STT(out=zz_, in0=zt_, scalar=1.0, in1=zz_, op0=ALU.add, op1=ALU.mult)
                dve.drain()
                dve.wait_ge(S["mla_pv"], i * 1 + 1)
                STT(out=zt_, in0=mx[:, 5], scalar=0.5, in1=zz_, op0=ALU.mult, op1=ALU.mult)
                yy = ys[:, bass.ds(i * 2 + 4, 2)]
                hi_lo((yy[:, :, 0], yy[:, :, 1]), zt_.rearrange("p (u t) -> p u t", u=2)).then_inc(S["y_mla"], 1)
            run(dve, "mla", mla_body)
            dve.wait_ge(S["x_loaded"], 48)
            residual("out1", 2, x_all=64)
            inverse_rms(NORM["b_final"] + 1, 0, D, nv, ny, nt, rstd_final, b=258)
            dve.wait_ge(S["stat_ready"], NORM["b_ret"] + 1)
            TT(nt, rstd_final, rstd_final, ALU.mult)
            dve.drain()
            STT(out=nv, in0=mx[:, 1, 0:258], scalar=1.0 / D, in1=nt, op0=ALU.mult, op1=ALU.mult)
            dve.drain()
            TS(nv, nv, EPS, None, ALU.add).then_inc(S["var_ready"], 1)
            dve.wait_ge(S["rsqrt_ready"], NORM["b_ret"] + 1)
            newton(nv, ny, nt, rstd)
            TT(rstd, rstd, rstd_final, ALU.mult)
            dve.wait_ge(S["ret_tab_loaded"], 16)
            dve.drain()
            for k in range(2):
                TT(cs_r[:, T * k:T * k + T], cs_r[:, T * k:T * k + T], rstd[:, 0:T], ALU.mult)

            def ret_body(name, first):
                def body(i):
                    def rotate(src, dst):
                        dve.drain()
                        a, b = src[:, 0:256], src[:, 256:512]
                        t1, t2 = t12[:, 0:256], t12[:, 256:512]
                        c_, s1_ = cs_r[:, 0:256], cs_r[:, 256:512]
                        TT(t1, a, c_, ALU.mult)
                        TT(t2, b, s1_, ALU.mult)
                        dve.drain()
                        TT(dst[:, 0:256], t1, t2, ALU.subtract)
                        dve.drain()
                        TT(t1, a, s1_, ALU.mult)
                        TT(t2, b, c_, ALU.mult)
                        dve.drain()
                        return TT(dst[:, 256:512], t1, t2, ALU.add)

                    def gated(a, b):
                        dve.drain()
                        STT(out=o_r[:, a:b], in0=o_r[:, a:b], scalar=0.5, in1=sg_r[:, a:b], op0=ALU.mult, op1=ALU.mult)
                        yy = ys[:, bass.ds(i * 4 + a, b - a)]
                        return hi_lo((yy[:, :, 0], yy[:, :, 1]), o_r[:, a:b])

                    def gate(n):
                        dve.wait_ge(S["ret_tanh"], i * 4 + (4 * first + n + 1))
                        STT(out=sg_r[:, n], in0=th_r[:, T * (n % 2):T * (n % 2) + T], scalar=1.0, in1=sg_r[:, n],
                            op0=ALU.add, op1=ALU.mult)

                    for j in range(12):
                        if j == 2:
                            rotate(rq, q_r)
                            dve.drain()
                        if j == 4:
                            rotate(rq, k_r).then_inc(S["ret_qk"], 1)
                        if j in (6, 7):
                            dve.wait_ge(S["ret_vt"], i * 4 + (4 * first + j - 5))
                        if j == 7:
                            dve.wait_ge(S["ret_scores"], i * 1 + (first + 1))
                            dve.wait_ge(S["decay_loaded"], i * 16 + 16 * (first + 1))
                            TT(sd, mx[:, 0, 0:384], dec, ALU.mult).then_inc(S["decay_used"], 1)
                        if j == 9:
                            dve.wait_ge(S["ret_vrow"], i * 4 + (4 * first + 4))
                            v.reduce_sum(v_mean, v_sum.rearrange("p (k n) -> p k n", k=2), AX.X)
                            dve.drain()
                            TS(v_mean, v_mean, -1.0 / 512, None, ALU.mult)
                            dve.drain()
                            for k in range(2):
                                ins = TS(vrow_r[:, k], vrow_r[:, k], v_mean[:, k:k + 1], None, ALU.add)
                            ins.then_inc(S["ret_vcent"], 1)
                        if j >= 9:
                            gate(j - 9)
                        if first == 0 and j % 3 == 0:
                            xo = xT[:, i * 4 + j // 3]
                            STT(out=xo, in0=xo, scalar=vec[:, bass.ds(i * 4 + (VEC["final"][0] + j // 3), 1)],
                                in1=rstd_final[:, 0:T], op0=ALU.mult, op1=ALU.mult)
                        if j == 11:
                            inverse_rms(i * 1 + (NORM[name] + 1), 5, 512, vt_r[:, 0:256], vt_r[:, 256:512],
                                        rq[:, 0:256], rq[:, 256:512])
                            dve.wait_ge(S["ret_o"], i * 1 + (first + 1))
                            g0 = VEC["gn_gain"][0] + 4 * first
                            for n in range(4):
                                STT(out=o_r[:, n], in0=o_r[:, n], scalar=vec[:, bass.ds(i * 4 + (g0 + n), 1)],
                                    in1=rq[:, 256:512], op0=ALU.mult, op1=ALU.mult)
                        dst = (rq[:, 0:256], rq[:, 256:512], rq[:, 0:256], rq[:, 256:512],
                               vt_r[:, 0:256], vt_r[:, 256:512], vt_r[:, 0:256], vt_r[:, 256:512],
                               sg_r[:, 0], sg_r[:, 1], sg_r[:, 2], sg_r[:, 3])[j]
                        split(name, i, j, 0)
                        evac(name, i, j, dst, scale=rstd[:, 0:T] if j >= 8 else None)
                        split(name, i, j, 1)
                    gate(3)
                    gated(0, 4).then_inc(S["y_ret"], 1)
                run(dve, name, body)

            for ph, first in (("ret_a", 0), ("ret_b", 4)):
                ret_body(ph, first)
                residual("ret_out" + ph[3:], 1)
            inverse_rms(NORM["b_mlp"] + 1, 0, D, nv, ny, nt, rstd, b=258)
            TT(rstd_sq, rstd, rstd, ALU.mult)
            for b in range(FF_BLOCKS):
                def up_body(i):
                    for j in range(4):
                        split(f"up{b}", i, j, 0)
                        evac(f"up{b}", i, j, up_t[j % 2])
                        split(f"up{b}", i, j, 1)
                        dve.drain()
                        STT(out=up_t[2 + j % 2], in0=up_t[j % 2], scalar=0.0, in1=up_t[j % 2], op0=ALU.max,
                            op1=ALU.mult)
                        dve.drain()
                        TT(up_t[2 + j % 2], up_t[2 + j % 2], rstd_sq[:, 0:T], ALU.mult)
                        yy = ys[:, i * 4 + j]
                        hi_lo((yy[:, 0], yy[:, 1]), up_t[2 + j % 2]).then_inc(S["y_up"], 1)
                run(dve, f"up{b}", up_body)
                residual(f"down{b}", 1)
            inverse_rms(NORM["b_out"] + 1, 0, D, *(w[:, 256:258] for w in (nv, ny, nt, rstd)), a=256, b=258)
            dve.drain().then_inc(S["fin_scale"], 1)
            for g in range(0, 8, 2):
                dve.wait_ge(S["fin_rows"], g + 1)
                TS(rows[:, g // 4, 512 * (g % 4):512 * (g % 4) + 512], fin_bank(g),
                   rstd[:, 256 + g // 4:257 + g // 4], None, ALU.mult).then_inc(S["fin_dve"], 1)
        @block.tensor
        def _(pe):
            mm = nc.tensor.matmul

            def panel(name, i, j, pieces, before={}):
                c, O = panels(name, i), outputs(name, i)
                s = 2 * c.slot(j, 2)
                sizes = PHASES[name][0]
                started = 2 if j and sizes[j - 1] <= cut(j - 1, sizes[j - 1]) else 1
                half_ = cut(j, sizes[j])
                pe.wait_ge(split_ready, c.half(j, 0))
                for o, moving, at, opens, closes, weight in pieces:
                    k = O.slot(o, NB)
                    if opens:
                        pe.wait_ge(evacuated, O(o, 1))
                    for t, m in enumerate(moving):
                        h = int(at + t >= half_)
                        u = at + t - h * half_
                        if h and u == 0:
                            pe.wait_ge(split_ready, c.half(j, 1))
                        if at + t in before:
                            pe.wait_ge(*before[at + t])
                        ins = mm(pj[:, k], w_hi[:, s + h, u], m, start=opens and t == 0, stop=False)
                        if u == 0:
                            ins.then_inc(half_started, 1 if h else started)
                        ins = mm(pj[:, k, 0:T], w_lo[:, s + h, u], m[:, 0], start=False,
                                 stop=closes and t == len(moving) - 1)
                    if closes:
                        ins.then_inc(output_ready, weight)

            def tiles(src, a, b):
                return [src[:, k] for k in range(a, b)]

            def whole(name, i, j, src, o=None):
                panel(name, i, j, [(j if o is None else o, tiles(src, 0, 16), 0, True, True, 1)])

            def transpose_to(dst, src):
                return nc.tensor.transpose(dst, src, ident)

            def columns(g):
                if g >= 6:
                    pe.wait_ge(S["part_taken"], 2 * (g - 6) + 2)
                src = mem_rows if g < 8 else rows
                for u in range(2):
                    for r in range(2):
                        c = 2 * (g % 8) + u
                        ins = transpose_to(mx[:, g % 6, T * u + 128 * r:T * u + 128 * r + 128],
                                           src[:, r, 128 * c:128 * c + 128])
                ins.then_inc(S["transposed"], 1)
            pe.wait_ge(S["tables"], 48)
            pe.wait_ge(S["mem_scaled"], 1)
            for g in range(8):
                columns(g)

            def mem_body(i):
                O = outputs("mem", i)

                def value_rows(n):
                    pe.wait_ge(evacuated, O(4 + n, 1 + NB))
                    for m in range(2):
                        ins = transpose_to(mx[:, n, 128 * m:128 * m + 128], vt[n % 2][:, 128 * m:128 * m + 128])
                    ins.then_inc(S["v_rows"], 1)
                for j in range(8):
                    whole("mem", i, j, ys)
                    if j == 0:
                        if i == 0:
                            pe.wait_ge(S["x_rows"], 16)
                        else:
                            pe.wait_ge(S["x_scaled"], 1)
                            pe.wait_ge(S["v_rows_taken"], 4)
                    if j < 4:
                        columns(8 + 8 * i + 2 * j)
                        columns(9 + 8 * i + 2 * j)
                    if j == 5:
                        pe.wait_ge(S["part_taken"], 32 + 16 * i)
                    if j >= 5:
                        value_rows(j - 5)
                value_rows(3)
            pe.wait_ge(S["part_taken"], 16)
            for i in range(2):
                mem_body(i)

            def gate_body(i):
                for j in range(4):
                    whole("gate", i, j, hs)
            pe.wait_ge(S["part_taken"], 48)
            run(pe, "gate", gate_body)

            for r in range(2):
                for k in range(16):
                    for part in range(2):
                        ins = mm(mx[:, 0, 32 * r:32 * r + 32],
                                 hs[:, k, part, 128 * r:128 * r + 128].bitcast(F32), wdt[:, k],
                                 start=k == 0 and part == 0, stop=k == 15 and part == 1)
            ins.then_inc(S["dt_logits"], 1)

            def gate_out_body(i):
                for j in range(4):
                    panel("gate_out", i, j, [(2 * j + u, tiles(ys, 0, 8), 8 * u, True, True, 1) for u in range(2)])
            pe.wait_ge(S["y_gate"], 8)
            run(pe, "gate_out", gate_out_body)
            pe.wait_ge(S["dt_ready"], 1)
            mm(mx[:, 1, 0:32], after, da[:, 0], start=True, stop=True).then_inc(S["dte_logits"], 1)

            def residual(name, ppo, src, before):
                def body(i):
                    for j in range(len(PHASES[name][0])):
                        n = PHASES[name][0][j]
                        a = (j % ppo) * n
                        panel(name, i, j, [(j // ppo, tiles(src, a, a + n), 0, j % ppo == 0, j % ppo == ppo - 1, 1)],
                              {t - a: w for t, w in before.items() if a <= t < a + n})
                run(pe, name, body)

            def square_sum(n=1):
                square_sum.n += 1
                pe.wait_ge(S["acc_ready"], square_sum.n)
                for k in range(n):
                    for r in range(2):
                        mm(mx[:, k, T + r:T + r + 1], acc[k][:, 128 * r:128 * r + 128], ones[:, 0:1], start=True,
                           stop=True)
                    mm(mx[:, k, 0:T], ones, acc[k], start=True, stop=True).then_inc(S["stat_ready"], 1)

            def mem_scores(q_, key_, bank):
                for q in range(2):
                    ins = mm(mx[:, bank, T * q:T * q + T], q_[:, 128 * q:128 * q + 128], key_, start=True, stop=True)
                ins.then_inc(S["mem_scores"], 1)

            def mem_pt(probs, bank):
                for k in range(2):
                    for q in range(2):
                        ins = transpose_to(mx[:, bank, T * k + 128 * q:T * k + 128 * q + 128],
                                           probs[:, T * q + 128 * k:T * q + 128 * k + 128])
                ins.then_inc(S["mem_pt"], 1)

            def mem_pv(vh, pt, bank):
                for k in range(2):
                    ins = mm(mx[:, bank, 0:T], vh[:, 128 * k:128 * k + 128], pt[:, T * k:T * k + T], start=k == 0,
                             stop=k == 1)
                ins.then_inc(S["mem_pv"], 1)

            def ssd_body(i):
                O = outputs("ssd", i)
                M = Count(0, 1, i)

                def seg(r):
                    pe.wait_ge(S["seg_rhs"], i * 4 + r + 1)
                    if r >= 2:
                        pe.wait_ge(S["decay_ready"], i * 4 + r - 1)
                    mm(mx[:, 1 + r % 2], after, rr[r % 2], start=True, stop=True).then_inc(S["seg_ready"], 1)

                def ydiag(r):
                    pe.wait_ge(S["mix_ready"], i * 4 + r + 1)
                    for h in range(4):
                        hh = 4 * (r % 2) + h
                        ins = mm(mx[64 * (h % 2):64 * (h % 2) + 64, 3 + r // 2, 128 * (hh // 2):128 * (hh // 2) + 128],
                                 xdt[r // 2][:, 64 * hh:64 * hh + 64], em[r][:, 128 * h:128 * h + 128],
                                 start=True, stop=True)
                    ins.then_inc(S["ydiag_ready"], 1)

                for j in range(12):
                    whole("ssd", i, j, hs)
                    if 1 <= j <= 4:
                        seg(j - 1)
                    if j == 1:
                        pe.wait_ge(evacuated, O(0, 1 + NB))
                        mem_scores(mq_s, keys[:, i], 3)
                    if j == 5:
                        pe.wait_ge(S["mem_pt_copied"], M(0, 1))
                        mem_pv(vh_s, pt_s, 3)
                    if j == 4:
                        pe.wait_ge(S["bc_ready"], i * 1 + 1)
                        for c in range(2):
                            mm(mx[:, 0, 128 * c:128 * c + 128], bT[:, 128 * c:128 * c + 128],
                               cT[:, 128 * c:128 * c + 128], start=True, stop=True)
                        transpose_to(mx[:, 0, 256:384], bT[:, 0:128]).then_inc(S["cb_ready"], 1)
                        pe.wait_ge(S["mem_scaled_probs"], M(0, 1))
                        mem_pt(probs_s, 4)
                    if j == 6:
                        pe.wait_ge(S["eq_lhs"], i * 1 + 1)
                        pe.wait_ge(S["decay_ready"], i * 4 + 4)
                        for n in range(4):
                            ins = mm(mx[:, 2, 128 * n:128 * n + 128], r0[:, 128 * n:128 * n + 128], upto, start=True,
                                     stop=True)
                        ins.then_inc(S["eq_logits"], 1)
                    if j == 8:
                        pe.wait_ge(S["xs_ready"], i * 1 + 1)
                        pe.wait_ge(S["cb_taken"], i * 1 + 1)
                        for c, bank in ((0, 5), (1, 0)):
                            for n in range(4):
                                ins = transpose_to(mx[:, bank, 128 * n:128 * n + 128],
                                                   xs[:, n, 128 * c:128 * c + 128])
                        ins.then_inc(S["xs_rows"], 1)
                    if j == 9:
                        pe.wait_ge(S["xdt_ready"], i * 1 + 1)
                        for r in range(4):
                            ydiag(r)
                        mm(mx[:, 5], brow, xdte, start=True, stop=True).then_inc(S["state_ready"], 1)
                    if j == 10:
                        pe.wait_ge(S["state_copied"], i * 1 + 1)
                        for n in range(4):
                            ins = mm(mx[:, 0, 128 * n:128 * n + 128], state[:, 128 * n:128 * n + 128], cT[:, 128:256],
                                     start=True, stop=True)
                        ins.then_inc(S["yoff_ready"], 1)
                pe.wait_ge(S["ssd_squares"], i * 1 + 1)
                for n in range(4):
                    ins = mm(mx[:, 5, 0:T], ones, ssq[:, n], start=n == 0, stop=n == 3)
                ins.then_inc(S["stat_ready"], 1)
            pe.wait_ge(S["dte_ready"], 1)
            run(pe, "ssd", ssd_body)
            square_sum.n = 0
            pe.wait_ge(S["y_ssd"], 3)
            residual("out0", 2, ys, {3: (S["y_mem"], 4), 16: (S["y_ssd"], 4)})
            square_sum()
            pe.wait_ge(S["h_ready"], 16)

            def latent_body(i):
                for j in range(4):
                    whole("latent", i, j, hs)
            run(pe, "latent", latent_body)
            for j in range(3):
                whole("latent_tail", 0, j, hs)
            pe.wait_ge(S["latent_squares"], 1)
            for k, (a, b) in enumerate(((0, 4), (4, 10))):
                for c in range(a, b):
                    ins = mm(mx[:, k, 0:T], ones, lsq[:, c], start=c == a, stop=c == b - 1)
                ins.then_inc(S["stat_ready"], 1)

            def memq_body(i):
                O = outputs("memq", i)
                M = Count(4, 2, i)
                for j in range(4):
                    whole("memq", i, j, hs)
                    if j == 2:
                        pe.wait_ge(evacuated, O(1, 1 + NB))
                        for u in range(2):
                            mem_scores(mq_m[:, T * u:T * u + T], keys[:, i * 2 + u], u)
                for u in range(2):
                    pe.wait_ge(S["mem_scaled_probs"], M(u, 1))
                    mem_pt(p_m[:, 512 * u:512 * u + 512], 2 + u)
                for u in range(2):
                    pe.wait_ge(S["mem_pt_copied"], M(u, 1))
                    mem_pv(vh_m[:, T * u:T * u + T], pt_m[:, 512 * u:512 * u + 512], 4 + u)
            pe.wait_ge(S["kv_loaded"], 16)
            run(pe, "memq", memq_body)
            def mla_body(i):
                O = outputs("mla", i)
                kv_t, q_t = tiles(lat, 0, 4), tiles(lat, 4, 10)
                for j in range(8):
                    panel("mla", i, j, (
                        [(0, q_t, 0, True, True, 1)], [(1, q_t, 0, True, True, 1)], [(2, q_t, 0, True, True, 1)],
                        [(3, kv_t, 0, True, True, 1), (4, kv_t, 4, True, True, 1)],
                        [(5, kv_t, 0, True, True, 1)], [(6, kv_t, 0, True, True, 1)],
                        [(7, tiles(hs, 0, 16), 0, True, True, 1)], [(8, tiles(hs, 0, 16), 0, True, True, 2)])[j])
                    if j == 4:
                        pe.wait_ge(S["qk_ready"], i * 1 + 1)
                        for u, kr_ in enumerate((krA, krB)):
                            for q, a, n in ((0, 0, 128), (1, 128, 256)):
                                dst = mx[:, u, a:a + n]
                                mm(dst, qn[u][:, 128 * q:128 * q + 128], kn[u][:, 0:n], start=True, stop=False)
                                ins = mm(dst, qr[:, 128 * q:128 * q + 128], kr_[:, 0:n], start=False, stop=True)
                        ins.then_inc(S["mla_scores"], 1)
                    if j in (5, 6):
                        u = j - 5
                        pe.wait_ge(evacuated, O(5 + u, 1 + NB))
                        for k in range(2):
                            ins = transpose_to(mx[:, 2, T * u + 128 * k:T * u + 128 * k + 128],
                                               vtm[u][:, 128 * k:128 * k + 128])
                        if u == 1:
                            ins.then_inc(S["mla_vt"], 1)
                    if j == 6:
                        pe.wait_ge(S["mla_probs_scaled"], i * 1 + 1)
                        for u in range(2):
                            for a in (0, 128, 256):
                                ins = transpose_to(mx[:, 3 + u, a:a + 128], s_[:, 384 * u + a:384 * u + a + 128])
                        ins.then_inc(S["mla_pt"], 1)
                pe.wait_ge(S["mla_vrow"], i * 1 + 1)
                pe.wait_ge(S["mla_pt_copied"], i * 1 + 1)
                for u in range(2):
                    mm(mx[:, 5, T * u:T * u + T], vrow_[:, T * u:T * u + 128], pt_[:, 384 * u:384 * u + 256],
                       start=True, stop=False)
                    ins = mm(mx[:, 5, T * u + 128:T * u + 256], vrow_[:, T * u + 128:T * u + 256],
                             pt_[:, 384 * u + 256:384 * u + 384], start=False, stop=True)
                ins.then_inc(S["mla_pv"], 1)
            pe.wait_ge(S["lat_ready"], 7)
            pe.wait_ge(S["krope_ready"], 1)
            run(pe, "mla", mla_body)
            pe.wait_ge(S["y_mla"], 7)
            residual("out1", 2, ys, {18: (S["y_mla"], 8)})
            square_sum(2)
            pe.wait_ge(S["h_ready"], 32)

            def ret_body(name, first):
                def body(i):
                    O = outputs(name, i)
                    for j in range(12):
                        whole(name, i, j, hs)
                        if 5 <= j <= 8:
                            n = j - 5
                            pe.wait_ge(evacuated, O(4 + n, 1 + NB))
                            if n >= 2:
                                pe.wait_ge(S["ret_vrow"], i * 4 + (4 * first + n - 1))
                            for k in range(2):
                                ins = transpose_to(mx[:, 1 + n % 2, 128 * k:128 * k + 128],
                                                   vt_r[:, T * (n % 2) + 128 * k:T * (n % 2) + 128 * k + 128])
                            ins.then_inc(S["ret_vt"], 1)
                        if j == 6:
                            pe.wait_ge(S["ret_qk"], i * 1 + (first + 1))
                            for k, a, n in ((0, 0, 256), (1, 256, 128)):
                                for d in range(2):
                                    ins = mm(mx[:, 0, a:a + n], k_r[:, T * d + 128 * k:T * d + 128 * k + 128],
                                             q_r[:, T * d + T - n:T * d + T], start=d == 0, stop=d == 1)
                            ins.then_inc(S["ret_scores"], 1)
                        if j == 9:
                            pe.wait_ge(S["ret_vcent"], i * 1 + (first + 1))
                            pe.wait_ge(S["decay_used"], i * 1 + (first + 1))
                            for n in range(4):
                                dst = mx[:, 3 + n // 2, T * (n % 2):T * (n % 2) + T]
                                mm(dst, vrow_r[:, 0, 128 * n:128 * n + 128], sd[:, 0:256], start=True, stop=False)
                                ins = mm(dst[:, 128:256], vrow_r[:, 1, 128 * n:128 * n + 128], sd[:, 256:384],
                                         start=False, stop=True)
                            ins.then_inc(S["ret_pv"], 1)
                        if j == 10:
                            pe.wait_ge(S["ret_squares"], i * 1 + (first + 1))
                            for n in range(4):
                                ins = mm(mx[:, 5, 0:T], ones, sq_r[:, n], start=n == 0, stop=n == 3)
                            ins.then_inc(S["stat_ready"], 1)
                run(pe, name, body)

            for ph, first in (("ret_a", 0), ("ret_b", 4)):
                ret_body(ph, first)
                pe.wait_ge(S["y_ret"], first + 3)
                residual("ret_out" + ph[3:], 1, ys, {12: (S["y_ret"], first + 4)})
            for b in range(FF_BLOCKS):
                if b == 0:
                    square_sum()
                    pe.wait_ge(S["h_ready"], 48)

                def up_body(i):
                    for j in range(4):
                        whole(f"up{b}", i, j, hs)
                run(pe, f"up{b}", up_body)
                pe.wait_ge(S["y_up"], 16 * b + 13)
                residual(f"down{b}", 1, ys, {k: (S["y_up"], 16 * b + k + 1) for k in (13, 14, 15)})
            square_sum()
            pe.wait_ge(S["h_ready"], 64)
            pe.wait_ge(evacuated, Count(first_out[LAST])(16, NB))
            pe.wait_ge(S["var_ready"], NORM["b_out"] + 1)
            for g in range(8):
                for u in range(4):
                    c = 4 * (g % 4) + u
                    ins = transpose_to(fin_bank(g)[:, 128 * u:128 * u + 128],
                                       xT[:, c, 128 * (g // 4):128 * (g // 4) + 128])
                ins.then_inc(S["fin_rows"], 1)


def _tiles(w, rows, cols):
    return [w[128 * r:128 * r + 128, c:c + 128] for c in cols for r in rows]


def _stream(name, inp):
    w_in0, w_out0, w_in1, w_out1 = inp["w_in0"], inp["w_out0"], inp["w_in1"], inp["w_out1"]
    n = PHASES[name][1]
    k16 = range(16)
    its = []
    ret_in, ret_out = inp["ret_w_in_2"][0], inp["ret_w_out_2"][0]
    up, down = inp["mlp_w_up_2"][0], inp["mlp_w_down_2"][0]
    for i in range(n):
        if name == "mem":
            cols = range(0, 512, 128)
            its.append(_tiles(inp[f"mem_k{1 - i}"], k16, cols) + _tiles(inp[f"mem_v{1 - i}"], k16, cols))
        elif name == "gate":
            its.append(_tiles(w_in0, k16, [s * 1024 + 128 * i for s in (3, 1, 2, 0)]))
        elif name == "gate_out":
            its.append(_tiles(w_out0, range(8), range(1024 * i, 1024 * i + 1024, 128)))
        elif name == "ssd":
            xbc = 4096 + 2048
            its.append(_tiles(w_in0, k16, [9248 + 128 * i, xbc + 2048 + 128 * i, xbc + 2560 + 128 * i]
                              + [xbc + 512 * i + 128 * t for t in range(4)]
                              + [4096 + 512 * i + 128 * t for t in range(4)] + [9760 + 128 * i]))
        elif name == "out0":
            its.append(_tiles(w_out0, list(range(24, 28)) + list(range(8, 24)), range(512 * i, 512 * i + 512, 128)))
        elif name == "latent":
            its.append(_tiles(w_in1, k16, [(768 if i == 0 else 0) + 128 * t for t in range(4)]))
        elif name == "latent_tail":
            kr = np.concatenate([w_in1[:, 1280:1344]] * 2, axis=1)
            its.append(_tiles(w_in1, k16, [512, 640]) + _tiles(kr, k16, [0]))
        elif name == "memq":
            its.append(_tiles(w_in1, k16, [3392 + 256 * i, 3520 + 256 * i, 3904 + 256 * i, 4032 + 256 * i]))
        elif name == "mla":
            uq, ukv = inp["mla_w_uq"], inp["mla_w_ukv"]
            qc, kc = 384 * i, 512 * i
            qr = np.concatenate([uq[:, qc + 128:qc + 192], uq[:, qc + 320:qc + 384]], axis=1)
            its.append(_tiles(uq, range(6), [qc, qc + 192]) + _tiles(qr, range(6), [0])
                       + _tiles(ukv, range(4), [kc, kc + 256, kc + 128, kc + 384])
                       + _tiles(w_in1, k16, [1344 + 256 * i, 1472 + 256 * i]))
        elif name == "out1":
            its.append(_tiles(w_out1, list(range(16, 20)) + list(range(16)), range(512 * i, 512 * i + 512, 128)))
        elif name in ("ret_a", "ret_b"):
            h = i + (4 if name == "ret_b" else 0)
            its.append(_tiles(ret_in, k16, [256 * h, 256 * h + 128, 2048 + 256 * h, 2176 + 256 * h]
                              + [4096 + 512 * h + 128 * t for t in range(4)]
                              + [8192 + 512 * h + 128 * t for t in range(4)]))
        elif name in ("ret_out_a", "ret_out_b"):
            r = 16 if name == "ret_out_b" else 0
            its.append(_tiles(ret_out, range(r, r + 16), range(512 * i, 512 * i + 512, 128)))
        elif name.startswith("up"):
            b = int(name[2:])
            its.append(_tiles(up, k16, [2048 * b + 512 * i + 128 * t for t in range(4)]))
        else:
            b = int(name[4:])
            its.append(_tiles(down, range(16 * b, 16 * b + 16), range(512 * i, 512 * i + 512, 128)))
    out = np.empty((n, P, sum(PHASES[name][0]) * 128), np.float32)
    for i, parts in enumerate(its):
        for t, w in enumerate(parts):
            out[i, :, 128 * t:128 * t + 128] = w
    return out


def _columns(v):
    return np.asarray(v).reshape(-1, P).T


def _vectors(inp):
    out = np.zeros((P, NVEC), np.float32)

    def put(name, cols):
        a, b = VEC[name]
        out[:, a:b] = cols
    for name, src in (("mem_norm", "mem_norm_w"), ("norm0", "norm0_w"), ("norm1", "norm1_w"), ("final", "final_norm_w"),
                      ("norm1_2", "norm1_2"), ("norm2_2", "norm2_2"), ("final_2", "final_norm_2"),
                      ("final_norm1_2", "final_norm_w"),
                      ("q_norm", "mla_q_norm_w"), ("kv_norm", "mla_kv_norm_w"), ("gn_gain", "ret_gn_gain_2"),
                      ("ssd_norm", "ssd_norm_w")):
        put(name, _columns(inp[src].reshape(-1)))
    gate = inp["sc_conv_w"]
    put("gate_conv", np.stack([_columns(gate[k]) for k in range(3)], axis=2).reshape(P, 24))
    taps = np.stack([_columns(inp["ssd_conv_w"][k]) for k in range(4)] + [_columns(inp["ssd_conv_b"])], axis=2)
    groups = [[16 + g, 20 + g] + [4 * g + t for t in range(4)] for g in range(GROUPS)]
    put("ssd_conv", np.concatenate([taps[:, t].reshape(P, 5) for g in groups for t in g], axis=1))
    put("ssd_d", _columns(np.repeat(inp["ssd_d"], 64)))
    put("dt_bias", np.broadcast_to(inp["ssd_dt_bias"], (P, 32)))
    put("a_log", np.broadcast_to(inp["ssd_a_log"], (P, 32)))
    inv = (10000.0 ** (-np.arange(32, dtype=np.float32) / np.float32(32))).astype(np.float32)
    put("inv_freq", np.tile(inv, 4)[:, None])
    put("sin_sign", np.where(np.arange(P) % 64 < 32, 1.0, -1.0)[:, None])
    return out


def _constants():
    k, q = np.arange(P)[:, None], np.arange(P)[None, :]
    con = np.zeros((P, NCONST), np.float32)
    for name, m in (("ident", k == q), ("ones", k == k), ("upto", k <= q), ("after", k > q)):
        con[:, CONST[name][0]:CONST[name][1]] = m
    causal = np.where(q <= k, 0.0, -1e30).astype(np.float32)
    mask = np.concatenate([causal, np.zeros((P, 128), np.float32), causal], axis=1)
    half_ = np.arange(0, 256, 2, dtype=np.float32)
    inv = (np.float32(10000.0) ** (-half_ / np.float32(256))).astype(np.float32)
    ang = (inv[:, None] * np.arange(T, dtype=np.float32)[None]).astype(np.float32).astype(np.float64)
    tab = np.concatenate([np.cos(ang), np.sin(ang)], axis=1).astype(np.float32)
    tk, tq = np.arange(T)[:, None], np.arange(T)[None]
    dist = np.where(tk // 64 == tq // 64, np.abs(tq - tk), tq - tk)
    seen = tk // 64 <= tq // 64
    decay = np.zeros((RET_HEADS, P, 384), np.float32)
    for h in range(RET_HEADS):
        full = np.where(seen, (1.0 - 2.0 ** (-5.0 - h)) ** dist, 0.0) / 16.0
        decay[h] = np.concatenate([full[:128], full[128:, 128:]], axis=1)
    return con, mask, tab, decay


def kernel(**inputs):
    import concourse.bacc as _bacc
    from concourse.bass_utils import run_bass_kernel_spmd as _run

    inp = {k: np.asarray(v) for k, v in inputs.items()}
    con, mask, tab, decay = _constants()
    w_dt = np.stack([inp["w_in0"][128 * k:128 * k + 128, 9216:9248] for k in range(16)], axis=1)
    arrays = {f"w_{name}": _stream(name, inp) for name in ORDER}
    arrays |= {"w_dt": w_dt, "vecs": _vectors(inp), "consts": con, "mla_mask": mask, "ret_tab": tab,
               "ret_decay": decay, "pos": np.ascontiguousarray(np.broadcast_to(inp["positions"], (P, T))),
               "x": inp["x"], "mem": inp["mem"]}
    nc = _bacc.Bacc("TRN2", target_bir_lowering=False, num_devices=1)
    arrays = {f"in_{k}": np.ascontiguousarray(v) for k, v in arrays.items()}
    aps = {k[3:]: nc.dram_tensor(k, v.shape, mybir.dt.from_np(v.dtype), kind="ExternalInput").ap()
           for k, v in arrays.items()}
    out = nc.dram_tensor("out_y", (1, T, D), F32, kind="ExternalOutput").ap()
    streams = {name: aps.pop(f"w_{name}") for name in ORDER}
    build(nc, streams, out=out, **aps)
    r = _run(nc, [arrays], core_ids=[0])
    return r.results[0]["out_y"]
```
